# Optimizing a Trainium2 kernel written in Bass

```python
import math
import jax, jax.numpy as jnp
from jax import lax
import numpy as np

D_MODEL = 1024
BATCH = 1
SEQ = 1024
DEPTH = 1
DEC_BATCH = 1
DEC_SEQ = 64
PAST_LEN = 512

CHUNK = 64
D_MIX = D_MODEL
D_SSM = D_MIX // 2
D_CONV = D_MIX - D_SSM
SSM_GROUP = 16
N_SSM_GROUPS = D_SSM // SSM_GROUP
SSM_STATE = 64
CONV_WIDTH = 3
CONV_HEADS = 8
D_PROJ = D_SSM + 3 * D_CONV
N_EXPERTS = 64
TOP_K = 6
N_EXPERT_GROUPS = 8
TOPK_GROUPS = 4
D_EXPERT = 256
D_SHARED = D_EXPERT
ROUTED_SCALE = 2.5
MOE_BLOCK = 128
DEEPNORM_ALPHA = (2.0 * DEPTH) ** 0.25
DEEPNORM_BETA = (8.0 * DEPTH) ** -0.25
LN_EPS = 1e-5
RMS_EPS = 1e-6

kernel_name = 'hybrid_s5_shortconv_moe_stream'

def layer_norm(x, g, b):
    xf = x.astype(jnp.float32)
    mu = xf.mean(-1, keepdims=True)
    var = jnp.square(xf - mu).mean(-1, keepdims=True)
    return ((xf - mu) * lax.rsqrt(var + LN_EPS) * g.astype(jnp.float32) + b.astype(jnp.float32)).astype(x.dtype)

def rms_norm(x, g):
    xf = x.astype(jnp.float32)
    return (xf * lax.rsqrt(jnp.mean(xf * xf, -1, keepdims=True) + RMS_EPS) * g.astype(jnp.float32)).astype(x.dtype)

def _complex_affine_combine(e1, e2):
    a1r, a1i, b1r, b1i = e1
    a2r, a2i, b2r, b2i = e2
    return (a2r * a1r - a2i * a1i,
            a2r * a1i + a2i * a1r,
            a2r * b1r - a2i * b1i + b2r,
            a2r * b1i + a2i * b1r + b2i)

def s5_ssm(u, h0_re, h0_im, lam_re, lam_im, log_dt, b_re, b_im, c_re, c_im, d_skip):
    bsz, l, _ = u.shape
    uf = u.astype(jnp.float32).reshape(bsz, l, N_SSM_GROUPS, SSM_GROUP)
    lr = lam_re.astype(jnp.float32)
    li = lam_im.astype(jnp.float32)
    dt = jnp.exp(log_dt.astype(jnp.float32))[:, None]
    mag = jnp.exp(lr * dt)
    ar = mag * jnp.cos(li * dt)
    ai = mag * jnp.sin(li * dt)
    den = lr * lr + li * li
    qr = ((ar - 1.0) * lr + ai * li) / den
    qi = (ai * lr - (ar - 1.0) * li) / den
    br_ = b_re.astype(jnp.float32)
    bi_ = b_im.astype(jnp.float32)
    bbar_r = qr[..., None] * br_ - qi[..., None] * bi_
    bbar_i = qr[..., None] * bi_ + qi[..., None] * br_
    bu_r = jnp.einsum('blgc,gpc->blgp', uf, bbar_r)
    bu_i = jnp.einsum('blgc,gpc->blgp', uf, bbar_i)
    h0r = h0_re.astype(jnp.float32)
    h0i = h0_im.astype(jnp.float32)
    bu_r = bu_r.at[:, 0].add(ar * h0r - ai * h0i)
    bu_i = bu_i.at[:, 0].add(ar * h0i + ai * h0r)
    a_r = jnp.broadcast_to(ar, bu_r.shape)
    a_i = jnp.broadcast_to(ai, bu_i.shape)
    _, _, hr, hi = lax.associative_scan(_complex_affine_combine, (a_r, a_i, bu_r, bu_i), axis=1)
    y = (jnp.einsum('blgp,gcp->blgc', hr, c_re.astype(jnp.float32))
         - jnp.einsum('blgp,gcp->blgc', hi, c_im.astype(jnp.float32))
         + d_skip.astype(jnp.float32).reshape(N_SSM_GROUPS, SSM_GROUP) * uf)
    return y.reshape(bsz, l, D_SSM), hr[:, -1], hi[:, -1]

def gated_short_conv(gate_b, gate_c, v, buf, conv_w):
    cv = gate_c * v
    full = jnp.concatenate([buf.astype(cv.dtype), cv], axis=1)
    l = v.shape[1]
    y = full[:, 0:l] * conv_w[0]
    for k in range(1, CONV_WIDTH):
        y = y + full[:, k:k + l] * conv_w[k]
    return gate_b * y, full[:, full.shape[1] - (CONV_WIDTH - 1):]

def token_mixing(h, h0_re, h0_im, conv_buf, w_in, lam_re, lam_im, log_dt, ssm_b_re, ssm_b_im,
                 ssm_c_re, ssm_c_im, ssm_d, w_glu, b_glu, conv_w, beta_ssm, beta_conv, w_out):
    p = h @ w_in
    u, gb, gc, v = jnp.split(p, [D_SSM, D_SSM + D_CONV, D_SSM + 2 * D_CONV], axis=-1)
    y_ssm, hT_re, hT_im = s5_ssm(u, h0_re, h0_im, lam_re, lam_im, log_dt, ssm_b_re, ssm_b_im,
                                 ssm_c_re, ssm_c_im, ssm_d)
    g = jax.nn.gelu(y_ssm)
    y_ssm = (g * jax.nn.sigmoid(g @ w_glu.astype(jnp.float32) + b_glu.astype(jnp.float32))).astype(h.dtype)
    y_conv, new_buf = gated_short_conv(gb, gc, v, conv_buf, conv_w)
    mixed = jnp.concatenate([rms_norm(y_ssm, beta_ssm), rms_norm(y_conv, beta_conv)], axis=-1)
    return mixed @ w_out, hT_re, hT_im, new_buf

def route(h, w_router, router_bias):
    t = h.shape[0]
    scores = jax.nn.sigmoid((h @ w_router).astype(jnp.float32))
    sel = scores + router_bias.astype(jnp.float32)
    per_group = N_EXPERTS // N_EXPERT_GROUPS
    grp_score = lax.top_k(sel.reshape(t, N_EXPERT_GROUPS, per_group), 2)[0].sum(-1)
    _, top_g = lax.top_k(grp_score, TOPK_GROUPS)
    gmask = jnp.any(top_g[..., None] == jnp.arange(N_EXPERT_GROUPS), axis=-2)
    masked = jnp.where(jnp.repeat(gmask, per_group, axis=-1), sel, -jnp.inf)
    _, top_e = lax.top_k(masked, TOP_K)
    w = jnp.take_along_axis(scores, top_e, axis=-1)
    w = w / jnp.sum(w, -1, keepdims=True) * ROUTED_SCALE
    return top_e, w

def routed_experts(h, top_e, top_w, w_gate, w_up, w_down):
    t, d = h.shape
    tk = t * TOP_K
    n_blocks = tk // MOE_BLOCK + N_EXPERTS
    rows = n_blocks * MOE_BLOCK
    flat_e = top_e.reshape(-1)
    flat_tok = jnp.repeat(jnp.arange(t, dtype=jnp.int32), TOP_K)
    flat_w = top_w.reshape(-1)
    order = jnp.argsort(flat_e)
    e_sorted = flat_e[order]
    counts = jnp.bincount(flat_e, length=N_EXPERTS)
    padded = (counts + MOE_BLOCK - 1) // MOE_BLOCK * MOE_BLOCK
    pad_end = jnp.cumsum(padded)
    pad_start = pad_end - padded
    start = jnp.cumsum(counts) - counts
    dest = pad_start[e_sorted] + jnp.arange(tk) - start[e_sorted]
    row_tok = jnp.full((rows,), t, jnp.int32).at[dest].set(flat_tok[order])
    row_w = jnp.zeros((rows,), flat_w.dtype).at[dest].set(flat_w[order])
    block_e = jnp.minimum(jnp.searchsorted(pad_end, jnp.arange(n_blocks) * MOE_BLOCK, side='right'),
                          N_EXPERTS - 1)
    h_pad = jnp.concatenate([h, jnp.zeros((1, d), h.dtype)], axis=0)

    def expert_block(args):
        tok, e = args
        xb = h_pad[tok]
        hid = jax.nn.silu(xb @ w_gate[e]) * (xb @ w_up[e])
        return hid @ w_down[e]

    yb = lax.map(expert_block, (row_tok.reshape(n_blocks, MOE_BLOCK), block_e))
    yb = yb.reshape(rows, d) * row_w[:, None].astype(yb.dtype)
    return jax.ops.segment_sum(yb, row_tok, num_segments=t + 1)[:t]

def moe_ffn(h, w_router, router_bias, w_gate, w_up, w_down, ws_gate, ws_up, ws_down):
    top_e, top_w = route(h, w_router, router_bias)
    routed = routed_experts(h, top_e, top_w, w_gate, w_up, w_down)
    shared = (jax.nn.silu(h @ ws_gate) * (h @ ws_up)) @ ws_down
    return routed.astype(h.dtype) + shared

def setup_inputs(seed: int = 0) -> dict:
    key = jax.random.key(seed)
    ks = list(jax.random.split(key, 40))
    nrm = lambda k, s: jax.random.normal(k, s, jnp.float32)
    L, G, P, E = DEPTH, N_SSM_GROUPS, SSM_STATE, N_EXPERTS
    inp = {}
    inp['x_prompt'] = nrm(ks[0], (BATCH, SEQ, D_MODEL))
    inp['x_sample'] = nrm(ks[1], (DEC_BATCH, DEC_SEQ, D_MODEL))
    inp['state_ssm_re'] = 0.3 * nrm(ks[2], (L, DEC_BATCH, G, P))
    inp['state_ssm_im'] = 0.3 * nrm(ks[3], (L, DEC_BATCH, G, P))
    inp['cache_conv'] = nrm(ks[4], (L, DEC_BATCH, CONV_WIDTH - 1, D_CONV))
    inp['ln_in_g'] = 1.0 + 0.02 * nrm(ks[5], (D_MODEL,))
    inp['ln_in_b'] = 0.02 * nrm(ks[6], (D_MODEL,))
    inp['w_in'] = nrm(ks[7], (L, D_MODEL, D_PROJ)) * D_MODEL ** -0.5
    inp['lam_re'] = -0.5 + 0.01 * nrm(ks[8], (L, G, P))
    inp['lam_im'] = jnp.pi * jnp.arange(P, dtype=jnp.float32) + 1e-3 * nrm(ks[9], (L, G, P))
    inp['log_dt'] = jax.random.uniform(ks[10], (L, G), jnp.float32, math.log(1e-3), math.log(1e-1))
    inp['ssm_b_re'] = nrm(ks[11], (L, G, P, SSM_GROUP)) * (2 * SSM_GROUP) ** -0.5
    inp['ssm_b_im'] = nrm(ks[12], (L, G, P, SSM_GROUP)) * (2 * SSM_GROUP) ** -0.5
    inp['ssm_c_re'] = nrm(ks[13], (L, G, SSM_GROUP, P)) * P ** -0.5
    inp['ssm_c_im'] = nrm(ks[14], (L, G, SSM_GROUP, P)) * P ** -0.5
    inp['ssm_d'] = nrm(ks[15], (L, D_SSM))
    inp['w_glu'] = nrm(ks[16], (L, D_SSM, D_SSM)) * D_SSM ** -0.5
    inp['b_glu'] = 0.02 * nrm(ks[17], (L, D_SSM))
    inp['conv_w'] = nrm(ks[18], (L, CONV_WIDTH, D_CONV)) * CONV_WIDTH ** -0.5
    inp['beta_ssm'] = 1.0 + 0.02 * nrm(ks[19], (L, D_SSM))
    inp['beta_conv'] = 1.0 + 0.02 * nrm(ks[20], (L, D_CONV))
    inp['w_out'] = nrm(ks[21], (L, D_MIX, D_MODEL)) * D_MIX ** -0.5 * DEEPNORM_BETA
    inp['ln1_g'] = 1.0 + 0.02 * nrm(ks[22], (L, D_MODEL))
    inp['ln1_b'] = 0.02 * nrm(ks[23], (L, D_MODEL))
    inp['w_router'] = nrm(ks[24], (L, D_MODEL, E)) * D_MODEL ** -0.5
    inp['router_bias'] = 0.01 * nrm(ks[25], (L, E))
    inp['w_gate'] = nrm(ks[26], (L, E, D_MODEL, D_EXPERT)) * D_MODEL ** -0.5
    inp['w_up'] = nrm(ks[27], (L, E, D_MODEL, D_EXPERT)) * D_MODEL ** -0.5
    inp['w_down'] = nrm(ks[28], (L, E, D_EXPERT, D_MODEL)) * D_EXPERT ** -0.5 * DEEPNORM_BETA
    inp['ws_gate'] = nrm(ks[29], (L, D_MODEL, D_SHARED)) * D_MODEL ** -0.5
    inp['ws_up'] = nrm(ks[30], (L, D_MODEL, D_SHARED)) * D_MODEL ** -0.5
    inp['ws_down'] = nrm(ks[31], (L, D_SHARED, D_MODEL)) * D_SHARED ** -0.5 * DEEPNORM_BETA
    inp['ln2_g'] = 1.0 + 0.02 * nrm(ks[32], (L, D_MODEL))
    inp['ln2_b'] = 0.02 * nrm(ks[33], (L, D_MODEL))
    return inp

def reference(x_prompt, x_sample, state_ssm_re, state_ssm_im, cache_conv, ln_in_g, ln_in_b,
              w_in, lam_re, lam_im, log_dt, ssm_b_re, ssm_b_im, ssm_c_re, ssm_c_im, ssm_d,
              w_glu, b_glu, conv_w, beta_ssm, beta_conv, w_out, ln1_g, ln1_b,
              w_router, router_bias, w_gate, w_up, w_down, ws_gate, ws_up, ws_down,
              ln2_g, ln2_b):
    hp = layer_norm(x_prompt, ln_in_g, ln_in_b)
    hs = layer_norm(x_sample, ln_in_g, ln_in_b)
    bp = hp.shape[0]
    n_prompt = hp.shape[0] * hp.shape[1]
    p_re, p_im, p_conv, s_re, s_im, s_conv = [], [], [], [], [], []
    for i in range(DEPTH):
        mix_w = (w_in[i], lam_re[i], lam_im[i], log_dt[i], ssm_b_re[i], ssm_b_im[i],
                 ssm_c_re[i], ssm_c_im[i], ssm_d[i], w_glu[i], b_glu[i], conv_w[i],
                 beta_ssm[i], beta_conv[i], w_out[i])
        zero_h = jnp.zeros((bp, N_SSM_GROUPS, SSM_STATE), jnp.float32)
        zero_buf = jnp.zeros((bp, CONV_WIDTH - 1, D_CONV), hp.dtype)
        mp, pr, pi, pc = token_mixing(hp, zero_h, zero_h, zero_buf, *mix_w)
        ms, sr, si, sc = token_mixing(hs, state_ssm_re[i], state_ssm_im[i], cache_conv[i], *mix_w)
        hp = layer_norm(DEEPNORM_ALPHA * hp + mp, ln1_g[i], ln1_b[i])
        hs = layer_norm(DEEPNORM_ALPHA * hs + ms, ln1_g[i], ln1_b[i])
        tokens = jnp.concatenate([hp.reshape(-1, D_MODEL), hs.reshape(-1, D_MODEL)], axis=0)
        f = moe_ffn(tokens, w_router[i], router_bias[i], w_gate[i], w_up[i], w_down[i],
                    ws_gate[i], ws_up[i], ws_down[i])
        hp = layer_norm(DEEPNORM_ALPHA * hp + f[:n_prompt].reshape(hp.shape), ln2_g[i], ln2_b[i])
        hs = layer_norm(DEEPNORM_ALPHA * hs + f[n_prompt:].reshape(hs.shape), ln2_g[i], ln2_b[i])
        p_re.append(pr); p_im.append(pi); p_conv.append(pc)
        s_re.append(sr); s_im.append(si); s_conv.append(sc)
    return (hp, hs, jnp.stack(p_re), jnp.stack(p_im), jnp.stack(p_conv),
            jnp.stack(s_re), jnp.stack(s_im), jnp.stack(s_conv))


_drawn_inputs = setup_inputs


def setup_inputs(seed=0):
    import zlib

    import numpy as np

    out = dict(_drawn_inputs(seed))
    spreads = {}
    factors = {'lam_re': 46.144, 'b_glu': 3.296, 'ln2_g': 20.464, 'ln2_b': 21.249}
    for name, (base, spread) in spreads.items():
        noise = np.random.default_rng([zlib.crc32(name.encode()), seed]).standard_normal(out[name].shape)
        drawn = base * np.exp(spread * noise) if base else spread * noise
        out[name] = __import__('jax').numpy.asarray(drawn.astype(out[name].dtype))
    for name, factor in factors.items():
        out[name] = (out[name] * factor).astype(out[name].dtype)
    return out
```

```python
from contextlib import ExitStack

import numpy as np
import concourse.bass as bass
from concourse import mybir

ALU = mybir.AluOpType
ACT = mybir.ActivationFunctionType
F32 = mybir.dt.float32
I32 = mybir.dt.int32
BF16 = mybir.dt.bfloat16

P = 128
D = 1024
KD = D // P
N_PROMPT = 1024
N_SAMPLE = 64
N_TOK = N_PROMPT + N_SAMPLE
N_TILES = (N_TOK + P - 1) // P
LAST_ROWS = N_TOK - (N_TILES - 1) * P
ROWS = N_TILES * P
D_HALF = 512
KH = D_HALF // P
GROUPS = 32
GC = 16
STATE = 64
GT = P // GC
T = 8
NK = N_TOK // T
NKP = N_PROMPT // T
N_EXP = 64
N_EGRP = 8
TOP_GROUPS = 4
TOP_K = 6
D_EXP = 256
ROUTED_SCALE = 2.5
SLOT_SETS = N_TILES + 1
CW = 384
TOK_CHUNKS = [(0, CW), (CW, CW), (2 * CW, N_TOK - 2 * CW)]
ALPHA = 2.0 ** 0.25
LN_EPS = 1e-5
RMS_EPS = 1e-6
TWO_PI_HI = 6.28125
TWO_PI_MID = 0.0019350051879882812
TWO_PI_LO = 3.019915981956753e-07
ROUND = 12582912.0
PI_BELOW = 3.1415925
TRIPLES = [(0, 3), (3, 3), (6, 2)]


class Names:
    pass


def chain(eng, own):
    count = {}

    def link(ins, sem=own):
        count[sem] = count.get(sem, 0) + 1
        ins.then_inc(sem, 1)
        eng.wait_ge(sem, count[sem])
    return link


def bc(ap, axis, n):
    shape = list(ap.shape)
    shape.insert(axis, n)
    return ap.unsqueeze(axis).to_broadcast(shape)


class Pools:

    def __init__(self, nc, ctx, stage):
        self.nc, self.ctx, self.stage, self.sems = nc, ctx, stage, []
        ctx.callback(self.clear)

    def sb(self, name, shape, dt=F32):
        return self.ctx.enter_context(self.nc.sbuf_tensor(f"{self.stage}_{name}", shape, dt))

    def ps(self, name, shape, dt=F32):
        return self.ctx.enter_context(self.nc.psum_tensor(f"{self.stage}_{name}", shape, dt))

    def sem(self, name):
        self.sems.append(self.nc.alloc_semaphore(f"{self.stage}_{name}"))
        return self.sems[-1]

    def clear(self):
        if self.sems:
            self.nc.clear_and_free_semaphores(self.sems)
            self.nc.all_engine_barrier()


def trunk_stage(nc, io, keep, co):
    with ExitStack() as ctx:
        m = Pools(nc, ctx, "trunk")
        x = m.sb("x", [P, N_TILES, D])
        lng, lnb = m.sb("lng", [P, D]), m.sb("lnb", [P, D])
        stats = m.sb("stats", [P, N_TILES, 2, 6])
        mv = m.sb("mv", [P, N_TILES, 2])
        rstd = m.sb("rstd", [P, N_TILES])
        nmr = m.sb("nmr", [P, N_TILES])
        scaled = m.sb("scaled", [P, 2, D])
        eps = m.sb("eps", [P, 1])
        ones_sq = m.sb("ones_sq", [P, P])
        rows = m.sb("rows", [GROUPS, 5, P])
        ldt = m.sb("ldt", [GROUPS, 1])
        crow = m.sb("crow", [P, KH, P])
        crow_sw = m.sb("crow_sw", [P, KH, P])
        par = m.sb("par", [P, 5, GROUPS])
        t = m.sb("t", [P, 12, GROUPS])
        ang = m.sb("ang", [P, 2, GROUPS])
        tb = m.sb("tb", [P, 2, GROUPS, GC])
        bs = m.sb("bs", [P, GROUPS, GC])
        bsw = m.sb("bsw", [P, GROUPS, GC])
        sq = m.sb("sq", [P, 3, GROUPS])
        pst = m.ps("pst", [P, 4, 4, P])
        pso = m.ps("pso", [P, 2, 512])
        s_x = [m.sem(f"x{i}") for i in range(N_TILES)]
        s_ln, s_par, s_b, s_c = m.sem("ln"), m.sem("par"), m.sem("b"), m.sem("c")
        s_const, s_pool = m.sem("const"), m.sem("pool")
        s_stat, s_std, s_rstd = m.sem("stat"), m.sem("std"), m.sem("rstd")
        s_norm, s_gain, s_h, s_tr, s_ev = m.sem("norm"), m.sem("gain"), m.sem("h"), m.sem("tr"), m.sem("ev")
        s_scaled, s_hp = m.sem("scaled"), [m.sem("hp0"), m.sem("hp1")]
        s_rows, s_part, s_parc, s_crd = m.sem("rows"), m.sem("part"), m.sem("parc"), m.sem("crd")
        s_dt, s_arg, s_mag, s_ang, s_sin, s_bsw = (m.sem(n) for n in ("dt", "arg", "mag", "ang", "sin", "bsw"))
        s_v, s_g = m.sem("v"), m.sem("g")
        block = ctx.enter_context(nc.Block())

        def dup(dst, src, order):
            return [(dst[:, 64 * h:64 * h + 64], src[w]) for h, w in enumerate(order)]

        @block.sync
        def _(sp):
            h0 = (io.state_ssm_re[0, 0], io.state_ssm_im[0, 0])
            lr = (io.lam_re[0],) * 2
            li = (io.lam_im[0],) * 2
            for k, (src, order) in enumerate((
                    (lr, (0, 1)), (li, (0, 1)), (h0, (0, 1)), (h0, (1, 0)))):
                slot = (0, 1, 3, 4)[k]
                for dst, s in dup(rows[:, slot, :], src, order):
                    sp.dma_start(dst, s).then_inc(s_par, 16)
            with nc.allow_non_contiguous_dma(reason="a column of step sizes"):
                sp.dma_start(ldt[:, :], io.log_dt.rearrange("a g -> g a")).then_inc(s_par, 16)
            for i in range(N_TILES - 1):
                sp.dma_start(x[:, i, :], io.x_prompt[0, i * P:(i + 1) * P, :]).then_inc(s_x[i], 16)
            sp.dma_start(x[0:LAST_ROWS, N_TILES - 1, :], io.x_sample[0]).then_inc(s_x[N_TILES - 1], 16)
            for i in range(N_TILES):
                sp.wait_ge(s_scaled, i + 1)
                sp.dma_start(io.resid[i * P:(i + 1) * P, :], scaled[:, i % 2, :]).then_inc(s_hp[i % 2], 16)
            for k in range(2):
                sp.wait_ge(s_hp[k], 16 * len(range(k, N_TILES, 2)))

        @block.scalar
        def _(act):
            act.dma_start(bs[0:64, :, :], io.ssm_b_re[0].rearrange("g p c -> p g c")).then_inc(s_b, 16)
            act.dma_start(bs[64:128, :, :], io.ssm_b_im[0].rearrange("g p c -> p g c")).then_inc(s_b, 16)
            act.dma_start(lng[:, :], io.ln_in_g.partition_broadcast(P)).then_inc(s_ln, 16)
            act.dma_start(lnb[:, :], io.ln_in_b.partition_broadcast(P)).then_inc(s_ln, 16)
            c_re = io.ssm_c_re[0].rearrange("(m g) c p -> (g c) m p", m=KH)
            c_im = io.ssm_c_im[0].rearrange("(m g) c p -> (g c) m p", m=KH)
            act.dma_start(crow[:, :, 0:64], c_re).then_inc(s_c, 16)
            act.dma_start(crow[:, :, 64:128], c_im).then_inc(s_c, 16)
            act.dma_start(crow_sw[:, :, 0:64], c_im).then_inc(s_c, 16)
            act.dma_start(crow_sw[:, :, 64:128], c_re).then_inc(s_c, 16)
            act.wait_ge(s_parc, 1)
            act.activation(t[:, 0, :], par[:, 2, :], ACT.Exp).then_inc(s_dt, 1)
            act.wait_ge(s_arg, 1)
            act.activation(t[:, 2, :], t[:, 1, :], ACT.Exp).then_inc(s_mag, 1)
            act.wait_ge(s_ang, 1)
            act.activation(t[:, 4:6, :], ang[:, :, :], ACT.Sin).then_inc(s_sin, 1)
            act.wait_ge(s_stat, 1)
            act.wait_ge(s_const, 1)
            act.activation(rstd[:, :], mv[:, :, 1], ACT.Sqrt, bias=eps[:, 0:1]).then_inc(s_std, 1)
            act.wait_ge(s_rstd, 1)
            for i in range(N_TILES):
                act.activation(x[:, i, :], x[:, i, :], ACT.Identity, bias=nmr[:, i:i + 1],
                               scale=rstd[:, i:i + 1]).then_inc(s_norm, 1)
            for i in range(N_TILES):
                act.wait_ge(s_h, i + 1)
                if i >= 2:
                    act.wait_ge(s_hp[i % 2], 16 * (i // 2))
                act.mul(scaled[:, i % 2, :], x[:, i, :], ALPHA).then_inc(s_scaled, 1)
                for half in range(2):
                    n = 2 * i + half
                    act.wait_ge(s_tr, n + 1)
                    w = P if i < N_TILES - 1 else LAST_ROWS
                    act.activation(keep.hT[:, 4 * half:4 * half + 4, i * P:i * P + w],
                                   pst[:, n % 4, :, 0:w], ACT.Copy).then_inc(s_ev, 1)

        @block.gpsimd
        def _(pool):
            link = chain(pool, s_pool)
            link(pool.memset(x[64:128, N_TILES - 1, :], 0.0))
            link(pool.memset(ones_sq[:, :], 1.0))
            link(pool.affine_select(out=keep.ident[:, :], in_=ones_sq[:, :], compare_op=ALU.is_equal, fill=0.0,
                                    base=0, pattern=[[-1, P]], channel_multiplier=1))
            link(pool.memset(eps[:, :], LN_EPS))
            link(pool.memset(co.sign[64:128, :], -1.0))
            pool.memset(co.sign[0:64, :], 1.0).then_inc(s_const, 1)
            pool.wait_ge(s_const, 1)
            for i in range(N_TILES):
                pool.wait_ge(s_gain, i + 1)
                if i == 0:
                    pool.wait_ge(s_ln, 32)
                pool.tensor_tensor(x[:, i, :], x[:, i, :], lnb[:, :], ALU.add).then_inc(s_h, 1)

        @block.tensor
        def _(pe):
            pe.wait_ge(s_const, 1)
            pe.wait_ge(s_rows, 1)
            for k in range(5):
                tr = pe.transpose(pso[:, 0, k * GROUPS:(k + 1) * GROUPS], rows[:, k, :],
                                  keep.ident[0:GROUPS, 0:GROUPS])
            tr.then_inc(s_part, 1)
            pe.wait_ge(s_c, 64)
            for v, src in enumerate((crow, crow_sw)):
                if v:
                    pe.wait_ge(s_crd, 1)
                for k in range(KH):
                    tr = pe.transpose(pso[:, 1, k * P:(k + 1) * P], src[:, k, :], keep.ident[:, :])
                tr.then_inc(s_part, 1)
            for i in range(N_TILES):
                pe.wait_ge(s_h, i + 1)
                for half in range(2):
                    n = 2 * i + half
                    if n >= 4:
                        pe.wait_ge(s_ev, n - 3)
                    for k in range(4):
                        c = (4 * half + k) * P
                        tr = pe.transpose(pst[:, n % 4, k, :], x[:, i, c:c + P], keep.ident[:, :])
                    tr.then_inc(s_tr, 1)

        @block.vector
        def _(v):
            link = chain(v, s_v)
            tt, ts, stt = v.tensor_tensor, v.tensor_scalar, v.scalar_tensor_tensor

            def cmul(outr, outi, ar, ai, br, bi, tmp):
                tt(tmp[0], ar, br, ALU.mult)
                tt(tmp[1], ai, bi, ALU.mult)
                tt(tmp[2], ar, bi, ALU.mult)
                link(tt(tmp[3], ai, br, ALU.mult))
                tt(outr, tmp[0], tmp[1], ALU.subtract)
                link(tt(outi, tmp[2], tmp[3], ALU.add))

            v.wait_ge(s_par, 16 * 9)
            link(v.tensor_copy(rows[:, 2, :], ldt[:, 0:1].to_broadcast([GROUPS, P])))
            v.sem_inc(s_rows, 1)
            v.wait_ge(s_part, 1)
            v.tensor_copy(par[:, :, :], pso[:, 0, 0:5 * GROUPS].rearrange("p (a g) -> p a g", a=5)).then_inc(s_parc, 1)
            v.wait_ge(s_parc, 1)
            lr, li, h0, h0sw = (par[:, k, :] for k in (0, 1, 3, 4))
            v.wait_ge(s_dt, 1)
            tt(t[:, 1, :], lr, t[:, 0, :], ALU.mult).then_inc(s_arg, 1)
            link(tt(t[:, 3, :], li, t[:, 0, :], ALU.mult))
            th = t[:, 3, :]
            for k in range(2):
                n = t[:, 6 + k, :]
                link(ts(n, th, float(1 / (2 * np.pi)), 0.25 * k, ALU.mult, ALU.add))
                link(ts(n, n, ROUND, None, ALU.add))
                link(ts(n, n, ROUND, None, ALU.subtract))
                link(stt(out=ang[:, k, :], in0=n, scalar=-TWO_PI_HI, in1=th, op0=ALU.mult, op1=ALU.add))
                link(stt(out=ang[:, k, :], in0=n, scalar=-TWO_PI_MID, in1=ang[:, k, :], op0=ALU.mult, op1=ALU.add))
                link(stt(out=ang[:, k, :], in0=n, scalar=-TWO_PI_LO, in1=ang[:, k, :], op0=ALU.mult, op1=ALU.add))
                if k:
                    link(ts(ang[:, k, :], ang[:, k, :], float(np.pi / 2), None, ALU.add))
                link(ts(ang[:, k, :], ang[:, k, :], PI_BELOW, -PI_BELOW, ALU.min, ALU.max))
            v.sem_inc(s_ang, 1)
            v.wait_ge(s_sin, 1)
            v.wait_ge(s_mag, 1)
            sin, cos, mag = t[:, 4, :], t[:, 5, :], t[:, 2, :]
            tmp = [t[:, k, :] for k in (8, 9, 10, 11)]

            def unit(c, s):
                tt(tmp[0], c, c, ALU.mult)
                link(tt(tmp[1], s, s, ALU.mult))
                link(tt(tmp[2], tmp[0], tmp[1], ALU.add))
                link(ts(tmp[2], tmp[2], -0.5, 1.5, ALU.mult, ALU.add))
                tt(c, c, tmp[2], ALU.mult)
                link(tt(s, s, tmp[2], ALU.mult))

            unit(cos, sin)
            pr, pi = co.pr, co.pi
            v.memset(pr[:, :, 0], 1.0)
            v.memset(pi[:, :, 0], 0.0)
            tt(pr[:, :, 1], mag, cos, ALU.mult)
            link(tt(pi[:, :, 1], mag, sin, ALU.mult))
            cmul(pr[:, :, 2], pi[:, :, 2], pr[:, :, 1], pi[:, :, 1], pr[:, :, 1], pi[:, :, 1], tmp)
            for lo in (1, 2):
                cmul(pr[:, :, 2 + lo], pi[:, :, 2 + lo], pr[:, :, lo], pi[:, :, lo], pr[:, :, 2], pi[:, :, 2], tmp)
            for lo in (1, 2, 3, 4):
                cmul(pr[:, :, 4 + lo], pi[:, :, 4 + lo], pr[:, :, lo], pi[:, :, lo], pr[:, :, 4], pi[:, :, 4], tmp)
            den, ar1 = t[:, 6, :], t[:, 7, :]
            ai = pi[:, :, 1]
            tt(tmp[0], lr, lr, ALU.mult)
            link(tt(tmp[1], li, li, ALU.mult))
            link(tt(den, tmp[0], tmp[1], ALU.add))
            v.reciprocal(den, den)
            link(ts(ar1, pr[:, :, 1], -1.0, None, ALU.add))
            tt(tmp[0], ar1, lr, ALU.mult)
            tt(tmp[1], ai, li, ALU.mult)
            tt(tmp[2], ai, lr, ALU.mult)
            link(tt(tmp[3], ar1, li, ALU.mult))
            tt(tmp[0], tmp[0], tmp[1], ALU.add)
            link(tt(tmp[2], tmp[3], tmp[2], ALU.subtract))
            qr, nqi = t[:, 0, :], t[:, 1, :]
            tt(qr, tmp[0], den, ALU.mult)
            link(tt(nqi, tmp[2], den, ALU.mult))
            v.wait_ge(s_const, 1)
            sg = co.sign[:, 0:1]
            link(ts(nqi, nqi, sg, None, ALU.mult))
            tt(co.nsi[:, :, :], pi[:, :, :], sg.unsqueeze(2).to_broadcast([P, GROUPS, 9]), ALU.mult)
            tt(co.prs[:, :, :], pr[:, :, :], sg.unsqueeze(2).to_broadcast([P, GROUPS, 9]), ALU.mult)
            link(ts(co.npi[:, :, :], pi[:, :, :], -1.0, None, ALU.mult))
            v.wait_ge(s_b, 32)
            v.tensor_copy(bsw[0:64, :, :], bs[64:128, :, :])
            link(v.tensor_copy(bsw[64:128, :, :], bs[0:64, :, :]))
            qrb, nqb = bc(qr, 2, GC), bc(nqi, 2, GC)
            tt(tb[:, 0], bs[:, :, :], qrb, ALU.mult)
            link(tt(tb[:, 1], bsw[:, :, :], nqb, ALU.mult))
            link(tt(co.bb[:, :, :], tb[:, 0], tb[:, 1], ALU.add))
            tt(tb[:, 0], bsw[:, :, :], qrb, ALU.mult)
            link(tt(tb[:, 1], bs[:, :, :], nqb, ALU.mult))
            link(tt(co.bbsw[:, :, :], tb[:, 0], tb[:, 1], ALU.subtract))
            tt(tmp[0], h0, pr[:, :, 8], ALU.mult)
            link(tt(tmp[1], h0sw, co.nsi[:, :, 8], ALU.mult))
            v.tensor_copy(co.h0[:, :], h0)
            link(tt(co.ah0[:, :], tmp[0], tmp[1], ALU.subtract))
            er, ei, mg = sq[:, 0, :], sq[:, 1, :], sq[:, 2, :]
            v.tensor_copy(er, cos)
            v.tensor_copy(mg, mag)
            link(v.tensor_copy(ei, sin))
            for k in range(3):
                tt(mg, mg, mg, ALU.mult)
                cmul(er, ei, er, ei, er, ei, tmp)
                unit(er, ei)
            v.tensor_copy(co.decay[:, :], mg)
            for lvl in range(7):
                v.tensor_copy(co.er[:, :, lvl], er)
                link(ts(co.eis[:, :, lvl], ei, sg, None, ALU.mult))
                if lvl < 6:
                    cmul(er, ei, er, ei, er, ei, tmp)
                    unit(er, ei)
            for k, dst in enumerate((co.cs, co.csw)):
                v.wait_ge(s_part, 2 + k)
                v.tensor_copy(dst[:, :], pso[:, 1, :]).then_inc(s_crd, 1)
            v.wait_ge(s_const, 1)
            for i in range(N_TILES):
                v.wait_ge(s_x[i], 16)
                for h in range(2):
                    st = v.bn_stats(stats[:, i, h, :], x[:, i, h * 512:(h + 1) * 512])
            link(st)
            for i in range(N_TILES):
                ag = v.bn_aggr(mv[:, i, :], stats[:, i, :, :])
            ag.then_inc(s_stat, 1)
            v.wait_ge(s_std, 1)
            link(v.reciprocal(rstd[:, :], rstd[:, :]))
            stt(out=nmr[:, :], in0=mv[:, :, 0], scalar=-1.0, in1=rstd[:, :], op0=ALU.mult,
                op1=ALU.mult).then_inc(s_rstd, 1)
            v.wait_ge(s_ln, 32)
            for i in range(N_TILES):
                v.wait_ge(s_norm, i + 1)
                tt(x[:, i, :], x[:, i, :], lng[:, :], ALU.mult).then_inc(s_gain, 1)


def mixing_stage(nc, io, keep, co):
    with ExitStack() as ctx:
        m = Pools(nc, ctx, "mix")
        RING = 3
        hT = keep.hT
        gT, ycT = keep.gT[:, :, 0:N_TOK], keep.ycT[:, :, 0:N_TOK]
        win = m.sb("win", [P, RING, KD, P])
        v_sb = m.sb("v", [P, N_TOK])
        gb = m.sb("gb", [P, N_TOK])
        cv = m.sb("cv", [P, N_TOK + 4])
        SAMPLE = N_PROMPT + 2
        cacheT = m.sb("cacheT", [P, KH, 2])
        taps = m.sb("taps", [P, KH, 3])
        u = m.sb("u", [P, GT, NK])
        bt = m.sb("bt", [P, GT, P])
        btsw = m.sb("btsw", [P, GT, P])
        bp = m.sb("bp", [P, GT, P])
        c1 = m.sb("c1", [P, GT, (T + 1) * GC])
        c2 = m.sb("c2", [P, GT, T * GC])
        toep = m.sb("toep", [P, GT, P])
        kf = m.sb("kf", [GC, GT, 2 * T, GC])
        dd = m.sb("dd", [GC, GROUPS, GC])
        t1, t2 = m.sb("t1", [P, GT * (T + 1) * GC]), m.sb("t2", [P, GT * (T + 1) * GC])
        cos, sin, dec = (m.sb(n, [P, GT, NK]) for n in ("cos", "sin", "dec"))
        q1, q2 = m.sb("q1", [P, GT * NKP // 2]), m.sb("q2", [P, GT * NKP // 2])
        w, g = m.sb("w", [P, GT, NK]), m.sb("g", [P, GT, NK])
        hc, hs = m.sb("hc", [P, GT, NK]), m.sb("hs", [P, GT, NK])
        y = m.sb("y", [P, GT, NK])
        fin = m.sb("fin", [P, 2, 2, GROUPS])
        swap = m.sb("swap", [P, P])
        fo = m.sb("fo", [GROUPS, 2, P])
        proj = m.ps("proj", [P, 3, 512])
        sb = m.ps("ssm", [P, 4, 512])
        misc = m.ps("misc", [P, 512])

        s_w = [m.sem(f"w{i}") for i in range(RING)]
        s_small, s_const = m.sem("small"), m.sem("const")
        s_proj, s_pact, s_pdve = m.sem("proj"), m.sem("pact"), m.sem("pdve")
        s_uout = [m.sem(f"uout{c}") for c in range(KH)]
        s_uin, s_yout, s_yin = m.sem("uin"), m.sem("yout"), m.sem("yin")
        s_bp, s_bpt, s_bt, s_c, s_k, s_kev, s_kdma, s_toep = (
            m.sem(n) for n in ("bp", "bpt", "bt", "c", "k", "kev", "kdma", "toep"))
        s_tab, s_bu, s_app, s_hch, s_y, s_yev = (m.sem(n) for n in ("tab", "bu", "app", "hch", "y", "yev"))
        s_rot, s_gel = m.sem("rot"), m.sem("gel")
        s_cv, s_gbr, s_conv = m.sem("cv"), m.sem("gbr"), m.sem("conv")
        s_cvout, s_fin, s_finp, s_finc, s_out = m.sem("cvout"), m.sem("fin"), m.sem("finp"), m.sem("finc"), m.sem("out")
        s_v, s_g, s_cvr = m.sem("vch"), m.sem("gch"), m.sem("cvr")
        block = ctx.enter_context(nc.Block())

        order = [("u", 0), ("u", 1), ("S", 0), ("u", 2), ("Y", 0), ("S", 1), ("u", 3), ("v", 0), ("Y", 1), ("S", 2),
                 ("gc", 0), ("gb", 0), ("v", 1), ("Y", 2), ("S", 3), ("gc", 1), ("gb", 1), ("v", 2), ("Y", 3),
                 ("gc", 2), ("gb", 2), ("v", 3), ("gc", 3), ("gb", 3)]
        column = {"u": 0, "gb": KH, "gc": 2 * KH, "v": 3 * KH}
        tiles = [o for o in order if o[0] in column]
        emptied, act_n, dve_n = [], 0, 0
        for kind, _ in tiles:
            for _ in TOK_CHUNKS:
                if kind == "gc":
                    dve_n += 1
                    emptied.append((s_pdve, dve_n))
                else:
                    act_n += 1
                    emptied.append((s_pact, act_n))
        first = {o: 3 * i for i, o in enumerate(tiles)}
        pact_after = {o: emptied[first[o] + 2][1] for o in tiles}

        @block.sync
        def _(sp):
            def weight(i):
                kind, c = tiles[i]
                if i >= RING:
                    sp.wait_ge(s_proj, 3 * (i - RING) + 3)
                col = (column[kind] + c) * P
                sp.dma_start(win[:, i % RING, :, :],
                             io.w_in[0].rearrange("(k p) n -> p k n", p=P)[:, :, col:col + P]).then_inc(s_w[i % RING], 16)

            sent = [0]

            def weights(n):
                while sent[0] < min(n, len(tiles)):
                    weight(sent[0])
                    sent[0] += 1
            weights(3)
            with nc.allow_non_contiguous_dma(reason="per-channel rows"):
                sp.dma_start(cacheT[:, :, 0], io.cache_conv[0, 0, 0].rearrange("(c p) -> p c", p=P)).then_inc(s_small, 16)
                sp.dma_start(cacheT[:, :, 1], io.cache_conv[0, 0, 1].rearrange("(c p) -> p c", p=P)).then_inc(s_small, 16)
                for k in range(3):
                    sp.dma_start(taps[:, :, k], io.conv_w[0, k].rearrange("(c p) -> p c", p=P)).then_inc(s_small, 16)
            sp.dma_start(dd[:, :, :], io.ssm_d[0].rearrange("(g c) -> g c", c=GC).partition_broadcast(GC)).then_inc(s_small, 16)
            done = 0
            for kind, c in order:
                if kind in column:
                    done += 1
                if kind == "u":
                    sp.wait_ge(s_pact, pact_after[("u", c)])
                    sp.dma_start(io.ud[c * P:(c + 1) * P, :], gT[:, c, :]).then_inc(s_uout[c], 16)
                if kind == "S":
                    sp.wait_ge(s_uout[c], 16)
                    if c:
                        sp.wait_ge(s_y, 3 * c)
                    ud = io.ud[c * P:(c + 1) * P, :].rearrange("(g c) (s k) -> s c g k", g=GT, s=T)
                    for s in range(T):
                        sp.dma_start(u[GC * s:GC * (s + 1), :, :], ud[s]).then_inc(s_uin, 16)
                    sp.wait_ge(s_kdma, c + 1)
                    for s in range(T):
                        sp.dma_start(toep[GC * s:GC * (s + 1), :, :].rearrange("p g (t c) -> p g t c", c=GC),
                                     kf[:, :, T - s:2 * T - s, :]).then_inc(s_toep, 16)
                if kind == "Y":
                    sp.wait_ge(s_yev, 3 * (c + 1))
                    yd = io.yd[c * P:(c + 1) * P, :].rearrange("(g c) (t k) -> t c g k", g=GT, t=T)
                    for s in range(T):
                        sp.dma_start(yd[s], y[GC * s:GC * (s + 1), :, :]).then_inc(s_yout, 16)
                    sp.wait_ge(s_yout, 16 * T * (c + 1))
                    sp.dma_start(gT[:, c, :], io.yd[c * P:(c + 1) * P, :]).then_inc(s_yin, 16)
                weights(done + 3)
            n_out = 0
            sp.wait_ge(s_finc, 2)
            for k, (re, im) in enumerate(((io.out_ssm_re_p, io.out_ssm_im_p), (io.out_ssm_re_s, io.out_ssm_im_s))):
                sp.dma_start(re[0, 0], fo[:, k, 0:STATE]).then_inc(s_out, 16)
                sp.dma_start(im[0, 0], fo[:, k, STATE:P]).then_inc(s_out, 16)
                n_out += 2
            sp.wait_ge(s_out, 16 * n_out)
            sp.wait_ge(s_cvout, 16 * 4 * KH)
            sp.wait_ge(s_yin, 16 * KH)

        @block.scalar
        def _(act):
            n = 0
            for kind, c in order:
                if kind in ("u", "v", "gb"):
                    for (lo, ln) in TOK_CHUNKS:
                        i = first[(kind, c)] + TOK_CHUNKS.index((lo, ln))
                        act.wait_ge(s_proj, i + 1)
                        src = proj[:, i % 3, 0:ln]
                        if kind == "u":
                            dst = gT[:, c, :].rearrange("p (s k) -> p k s", s=T)[:, lo // T:(lo + ln) // T, :]
                            src = src.rearrange("p (k s) -> p k s", s=T)
                        elif kind == "v":
                            dst = v_sb[:, lo:lo + ln]
                            if c and lo == 0:
                                act.wait_ge(s_cv, c)
                        else:
                            dst = gb[:, lo:lo + ln]
                            if c and lo == 0:
                                act.wait_ge(s_conv, c)
                        act.activation(dst, src, ACT.Copy).then_inc(s_pact, 1)
                if kind == "S":
                    if c:
                        act.wait_ge(s_bu, 3 * c)
                    for h in range(2):
                        act.wait_ge(s_bpt, 2 * c + h + 1)
                        src = sb[:, h, :].rearrange("p (g q) -> p g q", g=4)
                        act.activation(bt[:, 4 * h:4 * h + 4, :], src, ACT.Copy).then_inc(s_bt, 1)
                        act.activation(btsw[:, 4 * h:4 * h + 4, 0:64], src[:, :, 64:128], ACT.Copy).then_inc(s_bt, 1)
                        act.activation(btsw[:, 4 * h:4 * h + 4, 64:128], src[:, :, 0:64], ACT.Copy).then_inc(s_bt, 1)
                if kind == "Y":
                    if c:
                        act.wait_ge(s_yout, 16 * T * c)
                    for j, (g0, gn) in enumerate(TRIPLES):
                        act.wait_ge(s_y, 3 * c + j + 1)
                        act.activation(y[:, g0:g0 + gn, :], sb[:, j, 0:gn * NK].rearrange("p (g k) -> p g k", g=gn),
                                       ACT.Copy).then_inc(s_yev, 1)

        @block.gpsimd
        def _(pool):
            link = chain(pool, s_g)
            link(pool.memset(kf[:, :, :, :], 0.0))
            link(pool.memset(cv[:, 0:2], 0.0))
            link(pool.memset(hc[:, :, 0:1], 0.0))
            link(pool.memset(hs[:, :, 0:1], 0.0))
            link(pool.memset(hs[:, :, NKP:NKP + 1], 0.0))
            link(pool.memset(swap[:, :], 0.0))
            link(pool.affine_select(out=swap[:, :], in_=swap[:, :], compare_op=ALU.not_equal, fill=-1.0,
                                    base=-64, pattern=[[-1, P]], channel_multiplier=1))
            link(pool.affine_select(out=swap[:, :], in_=swap[:, :], compare_op=ALU.not_equal, fill=1.0,
                                    base=64, pattern=[[-1, P]], channel_multiplier=1))
            pool.wait_ge(s_small, 16 * 6)
            pool.tensor_tensor(dd[:, :, :], dd[:, :, :], bc(keep.ident[0:GC, 0:GC], 1, GROUPS),
                               ALU.mult).then_inc(s_const, 1)
            pool.wait_ge(s_const, 1)
            for c in range(KH):
                gs = slice(GT * c, GT * (c + 1))
                if c:
                    pool.wait_ge(s_app, c)
                link(pool.memset(cos[:, :, 0:1], 1.0))
                link(pool.memset(sin[:, :, 0:1], 0.0))
                for lvl in range(7):
                    n = 1 << lvl
                    er, ei = bc(co.er[:, gs, lvl], 2, n), bc(co.eis[:, gs, lvl], 2, n)
                    a, b = (t[:, 0:GT * n].rearrange("p (g k) -> p g k", g=GT) for t in (q1, q2))
                    link(pool.tensor_tensor(a, cos[:, :, 0:n], er, ALU.mult))
                    link(pool.tensor_tensor(b, sin[:, :, 0:n], ei, ALU.mult))
                    link(pool.tensor_tensor(cos[:, :, n:2 * n], a, b, ALU.subtract))
                    link(pool.tensor_tensor(a, sin[:, :, 0:n], er, ALU.mult))
                    link(pool.tensor_tensor(b, cos[:, :, 0:n], ei, ALU.mult))
                    link(pool.tensor_tensor(sin[:, :, n:2 * n], a, b, ALU.add))
                link(pool.tensor_copy(cos[:, :, NKP:NK], cos[:, :, 0:NK - NKP]))
                link(pool.tensor_copy(sin[:, :, NKP:NK], sin[:, :, 0:NK - NKP]))
                link(pool.tensor_copy(dec[:, :, :], bc(co.decay[:, gs], 2, NK)))
                link(pool.memset(dec[:, :, 0:1], 0.0))
                pool.memset(dec[:, :, NKP:NKP + 1], 0.0).then_inc(s_tab, 1)
                pool.wait_ge(s_tab, c + 1)
            with nc.allow_non_contiguous_dma(reason="a few columns"):
                for c in range(KH):
                    pool.wait_ge(s_cv, c + 1)
                    for dst, col in ((io.out_conv_p, N_PROMPT), (io.out_conv_s, N_TOK + 2)):
                        for k in range(2):
                            pool.dma_start(dst[0, 0, k, c * P:(c + 1) * P].rearrange("(p a) -> p a", a=1),
                                           cv[:, col + k:col + k + 1]).then_inc(s_cvout, 16)

        @block.tensor
        def _(pe):
            pn = 0
            for kind, c in order:
                if kind in column:
                    i = tiles.index((kind, c))
                    pe.wait_ge(s_w[i % RING], 16 * (i // RING + 1))
                    for lo, ln in TOK_CHUNKS:
                        if pn >= 3:
                            pe.wait_ge(*emptied[pn - 3])
                        for k in range(KD):
                            mm = pe.matmul(proj[:, pn % 3, 0:ln], win[:, i % RING, k, :], hT[:, k, lo:lo + ln],
                                           start=(k == 0), stop=(k == KD - 1))
                        mm.then_inc(s_proj, 1)
                        pn += 1
                if kind == "S":
                    pe.wait_ge(s_bp, c + 1)
                    if c:
                        pe.wait_ge(s_yev, 3 * c)
                    for h in range(2):
                        for q in range(4):
                            tr = pe.transpose(sb[:, h, q * P:(q + 1) * P], bp[:, 4 * h + q, :], keep.ident[:, :])
                        tr.then_inc(s_bpt, 1)
                    pe.wait_ge(s_c, c + 1)
                    for h in range(2):
                        for q in range(4):
                            gi = 4 * h + q
                            mm = pe.matmul(sb[0:GC, 2 + h, q * P:(q + 1) * P], co.bb[:, GT * c + gi, :],
                                           c1[:, gi, 0:T * GC], start=True, stop=True)
                    mm.then_inc(s_k, 1)
                    pe.wait_ge(s_bt, 6 * (c + 1))
                    pe.wait_ge(s_kev, c + 1)
                    pe.wait_ge(s_uin, 16 * T * (c + 1))
                    for j, (g0, gn) in enumerate(TRIPLES):
                        a, b = (0, 1) if j % 2 == 0 else (2, 3)
                        if j == 2:
                            pe.wait_ge(s_hch, 3 * c + 1)
                        for q in range(gn):
                            pe.matmul(sb[:, a, q * NK:(q + 1) * NK], bt[:, g0 + q, :], u[:, g0 + q, :],
                                      start=True, stop=True)
                        for q in range(gn):
                            mm = pe.matmul(sb[:, b, q * NK:(q + 1) * NK], btsw[:, g0 + q, :], u[:, g0 + q, :],
                                           start=True, stop=True)
                        mm.then_inc(s_bu, 1)
                if kind == "Y":
                    pe.wait_ge(s_toep, 16 * T * (c + 1))
                    pe.wait_ge(s_rot, c + 1)
                    for j, (g0, gn) in enumerate(TRIPLES):
                        for q in range(gn):
                            o, gi = sb[:, j, q * NK:(q + 1) * NK], g0 + q
                            pe.matmul(o, toep[:, gi, :], u[:, gi, :], start=True, stop=False)
                            pe.matmul(o, c1[:, gi, GC:(T + 1) * GC], hc[:, gi, :], start=False, stop=False)
                            mm = pe.matmul(o, c2[:, gi, :], hs[:, gi, :], start=False, stop=True)
                        mm.then_inc(s_y, 1)
            pe.wait_ge(s_fin, KH)
            for k in range(2):
                pe.matmul(misc[0:GROUPS, k * P:(k + 1) * P], fin[:, k, 0, :], keep.ident[:, :], start=True, stop=False)
                mm = pe.matmul(misc[0:GROUPS, k * P:(k + 1) * P], fin[:, k, 1, :], swap[:, :], start=False, stop=True)
            mm.then_inc(s_finp, 1)

        @block.vector
        def _(v):
            link = chain(v, s_v)
            tt, ts, stt = v.tensor_tensor, v.tensor_scalar, v.scalar_tensor_tensor
            v.wait_ge(s_small, 16 * 6)

            def coefficients(c):
                gs = slice(GT * c, GT * (c + 1))
                a = t1[:, 0:GT * T * GC].rearrange("p (g s c) -> p g s c", g=GT, s=T)
                b = t2[:, 0:GT * T * GC].rearrange("p (g s c) -> p g s c", g=GT, s=T)

                def shaped(x, n):
                    return x[:, 0:GT * n * GC].rearrange("p (g s c) -> p g s c", g=GT, s=n)

                if c:
                    v.wait_ge(s_bpt, 2 * c)
                tt(a, bc(co.bb[:, gs, :], 2, T), bc(co.pr[:, gs, 0:T][:, :, ::-1], 3, GC), ALU.mult)
                link(tt(b, bc(co.bbsw[:, gs, :], 2, T), bc(co.nsi[:, gs, 0:T][:, :, ::-1], 3, GC), ALU.mult))
                link(tt(bp[:, :, :].rearrange("p g (s c) -> p g s c", c=GC), a, b, ALU.subtract), s_bp)
                if c:
                    v.wait_ge(s_y, 3 * c)
                cs = co.cs[:, P * c:P * (c + 1)].rearrange("p (g c) -> p g c", c=GC)
                csw = co.csw[:, P * c:P * (c + 1)].rearrange("p (g c) -> p g c", c=GC)
                a9, b9 = shaped(t1, T + 1), shaped(t2, T + 1)
                link(tt(a9, bc(cs, 2, T + 1), bc(co.prs[:, gs, :], 3, GC), ALU.mult))
                link(tt(b9, bc(csw, 2, T + 1), bc(co.npi[:, gs, :], 3, GC), ALU.mult))
                link(tt(c1[:, :, :].rearrange("p g (s c) -> p g s c", c=GC), a9, b9, ALU.add))
                tt(a, bc(cs, 2, T), bc(co.npi[:, gs, 1:], 3, GC), ALU.mult)
                link(tt(b, bc(csw, 2, T), bc(co.prs[:, gs, 1:], 3, GC), ALU.mult))
                link(tt(c2[:, :, :].rearrange("p g (s c) -> p g s c", c=GC), a, b, ALU.subtract), s_c)
                v.wait_ge(s_k, c + 1)
                v.wait_ge(s_const, 1)
                if c:
                    v.wait_ge(s_toep, 16 * T * c)
                for h in range(2):
                    cp = v.tensor_copy(kf[:, 4 * h:4 * h + 4, T:2 * T, :],
                                       sb[0:GC, 2 + h, :].rearrange("p (g s c) -> p g s c", g=4, s=T))
                cp.then_inc(s_kev, 1)
                v.wait_ge(s_kev, c + 1)
                tt(kf[:, :, T, :], kf[:, :, T, :], dd[:, gs, :], ALU.add).then_inc(s_kdma, 1)

            def scan(c):
                gs = slice(GT * c, GT * (c + 1))
                v.wait_ge(s_tab, c + 1)
                for j, (g0, gn) in enumerate(TRIPLES):
                    a, b = (0, 1) if j % 2 == 0 else (2, 3)
                    v.wait_ge(s_bu, 3 * c + j + 1)
                    x1 = t1[:, g0 * NK:(g0 + gn) * NK].rearrange("p (g k) -> p g k", g=gn)
                    x2 = t2[:, g0 * NK:(g0 + gn) * NK].rearrange("p (g k) -> p g k", g=gn)
                    pa = sb[:, a, 0:gn * NK].rearrange("p (g k) -> p g k", g=gn)
                    pb = sb[:, b, 0:gn * NK].rearrange("p (g k) -> p g k", g=gn)
                    tt(x1, pa, cos[:, g0:g0 + gn, :], ALU.mult)
                    link(tt(x2, pb, sin[:, g0:g0 + gn, :], ALU.mult), s_hch)
                flat = [x[:, 0:GT * NK].rearrange("p (g k) -> p g k", g=GT) for x in (t1, t2)]
                link(tt(w[:, :, :], flat[0], flat[1], ALU.add))
                link(tt(w[:, :, NKP], w[:, :, NKP], co.ah0[:, gs], ALU.add))
                link(v.tensor_tensor_scan(g[:, :, :].rearrange("p g k -> p (g k)"),
                                          dec[:, :, :].rearrange("p g k -> p (g k)"),
                                          w[:, :, :].rearrange("p g k -> p (g k)"), 0.0, ALU.mult, ALU.add))
                if c == 0:
                    v.wait_ge(s_const, 1)
                for dst, tab in ((hc, cos), (hs, sin)):
                    tt(dst[:, :, 1:NKP], g[:, :, 0:NKP - 1], tab[:, :, 0:NKP - 1], ALU.mult)
                    tt(dst[:, :, NKP + 1:NK], g[:, :, NKP:NK - 1], tab[:, :, NKP:NK - 1], ALU.mult)
                for k, last in enumerate((NKP - 1, NK - 1)):
                    tt(fin[:, k, 0, gs], g[:, :, last], cos[:, :, last], ALU.mult)
                    f = tt(fin[:, k, 1, gs], g[:, :, last], sin[:, :, last], ALU.mult)
                link(f, s_app)
                link(v.tensor_copy(hc[:, :, NKP], co.h0[:, gs]), s_rot)
                for k in range(2):
                    f = ts(fin[:, k, 1, gs], fin[:, k, 1, gs], co.sign[:, 0:1], None, ALU.mult)
                link(f, s_fin)

            def gate(c):
                for j, (lo, ln) in enumerate(TOK_CHUNKS):
                    i = first[("gc", c)] + j
                    v.wait_ge(s_proj, i + 1)
                    if j == 0:
                        v.wait_ge(s_pact, pact_after[("v", c)])
                        if c:
                            v.wait_ge(s_cvout, 16 * 4 * c)
                    for a, b, shift in ((lo, min(lo + ln, N_PROMPT), 2), (max(lo, N_PROMPT), lo + ln, 4)):
                        if a < b:
                            mu = tt(cv[:, a + shift:b + shift], proj[:, i % 3, a - lo:b - lo], v_sb[:, a:b], ALU.mult)
                    link(mu, s_pdve)
                link(v.tensor_copy(cv[:, SAMPLE:SAMPLE + 2], cacheT[:, c, :]), s_cv)

            def conv(c):
                v.wait_ge(s_const, 1)
                x = t1[:, 0:N_TOK + 2]
                n = N_TOK + 2
                link(ts(x, cv[:, 0:n], taps[:, c, 0:1], None, ALU.mult))
                link(stt(out=x, in0=cv[:, 1:n + 1], scalar=taps[:, c, 1:2], in1=x, op0=ALU.mult, op1=ALU.add))
                link(stt(out=x, in0=cv[:, 2:n + 2], scalar=taps[:, c, 2:3], in1=x, op0=ALU.mult, op1=ALU.add))
                v.wait_ge(s_pact, pact_after[("gb", c)])
                tt(ycT[:, c, 0:N_PROMPT], t1[:, 0:N_PROMPT], gb[:, 0:N_PROMPT], ALU.mult)
                link(tt(ycT[:, c, N_PROMPT:N_TOK], t1[:, SAMPLE:SAMPLE + N_SAMPLE], gb[:, N_PROMPT:N_TOK],
                        ALU.mult), s_conv)

            for kind, c in order:
                if kind == "S":
                    coefficients(c)
                    scan(c)
                if kind == "gc":
                    gate(c)
                if kind == "gb":
                    conv(c)
            v.wait_ge(s_finp, 1)
            v.tensor_copy(fo[:, :, :].rearrange("p a b -> p (a b)"), misc[0:GROUPS, 0:2 * P]).then_inc(s_finc, 2)


def output_stage(nc, io, keep):
    with ExitStack() as ctx:
        m = Pools(nc, ctx, "out")
        gT, ycT = keep.gT, keep.ycT
        gn = m.sb("gn", [P, KH, ROWS])
        w_glu = m.sb("w_glu", [P, KH, D_HALF])
        w_out = m.sb("w_out", [P, KD, D])
        ws_in = m.sb("ws_in", [P, KD, 2 * D_EXP])
        ws_dn = m.sb("ws_dn", [P, 2, D])
        w_rt = m.sb("w_rt", [P, KD, N_EXP])
        lng, lnb = m.sb("lng", [P, D]), m.sb("lnb", [P, D])
        bglu = m.sb("bglu", [P, KH])
        beta = m.sb("beta", [P, KD])
        sig = m.sb("sig", [P, 2, CW])
        ssq = m.sb("ssq", [P, 2, ROWS])
        sqt = m.sb("sqt", [P, ROWS])
        ones = m.sb("ones", [P, 1])
        eps = m.sb("eps", [P, 2])
        rr = m.sb("rr", [P, N_TILES, 2])
        res = m.sb("res", [P, 2, D])
        z = m.sb("z", [P, D])
        x = m.sb("x", [P, 2, D])
        xT = m.sb("xT", [P, KD, P])
        stats = m.sb("stats", [P, 2, 6])
        mv = m.sb("mv", [P, 2])
        rs = m.sb("rs", [P, 2])
        sg = m.sb("sg", [P, D_EXP])
        hid = m.sb("hid", [P, D_EXP])
        hidT = m.sb("hidT", [P, 2, P])
        ao = m.sb("ao", [P, D])
        po = m.ps("po", [P, 2, 2, 512])
        pt = m.ps("pt", [P, 2, 512])
        pg = m.ps("pg", [P, 512])
        pm = m.ps("pm", [P, 512])

        s_wg, s_wo, s_ws, s_wr, s_ln, s_small = (m.sem(n) for n in ("wg", "wo", "ws", "wr", "ln", "small"))
        s_pad, s_const, s_g, s_v, s_a = m.sem("pad"), m.sem("const"), m.sem("gch"), m.sem("vch"), m.sem("ach")
        s_gelu, s_glu, s_sig, s_mix = m.sem("gelu"), m.sem("glu"), m.sem("sig"), m.sem("mix")
        s_wob, s_ssq, s_ss, s_rt, s_rr = m.sem("wob"), m.sem("ssq"), m.sem("ss"), m.sem("rt"), m.sem("rr")
        s_res = [m.sem("res0"), m.sem("res1")]
        s_po, s_z, s_zd, s_std, s_rstd, s_nm, s_gain, s_x = (
            m.sem(n) for n in ("po", "z", "zd", "std", "rstd", "nm", "gain", "x"))
        s_tr, s_xT, s_rl, s_lg, s_pg, s_silu, s_hid, s_ht, s_hT, s_pd, s_ao = (
            m.sem(n) for n in ("tr", "xT", "rl", "lg", "pg", "silu", "hid", "ht", "hT", "pd", "ao"))
        s_tok, s_acc = [m.sem("tok0"), m.sem("tok1")], m.sem("acc")
        block = ctx.enter_context(nc.Block())
        glu = [(ch, mo) for ch in range(len(TOK_CHUNKS)) for mo in range(KH)]

        @block.sync
        def _(sp):
            sp.dma_start(w_glu[:, :, :], io.w_glu[0].rearrange("(k p) n -> p k n", p=P)).then_inc(s_wg, 16)
            with nc.allow_non_contiguous_dma(reason="per-channel rows"):
                sp.dma_start(bglu[:, :], io.b_glu[0].rearrange("(c p) -> p c", p=P)).then_inc(s_small, 16)
                sp.dma_start(beta[:, 0:KH], io.beta_ssm[0].rearrange("(c p) -> p c", p=P)).then_inc(s_small, 16)
                sp.dma_start(beta[:, KH:KD], io.beta_conv[0].rearrange("(c p) -> p c", p=P)).then_inc(s_small, 16)
            sp.dma_start(w_out[:, :, :], io.w_out[0].rearrange("(k p) n -> p k n", p=P)).then_inc(s_wo, 16)
            sp.dma_start(lng[:, :], io.ln1_g[0].partition_broadcast(P)).then_inc(s_ln, 16)
            sp.dma_start(lnb[:, :], io.ln1_b[0].partition_broadcast(P)).then_inc(s_ln, 16)
            sp.dma_start(w_rt[:, :, :], io.w_router[0].rearrange("(k p) n -> p k n", p=P)).then_inc(s_wr, 16)
            sp.dma_start(ws_in[:, :, 0:D_EXP], io.ws_gate[0].rearrange("(k p) n -> p k n", p=P)).then_inc(s_ws, 16)
            sp.dma_start(ws_in[:, :, D_EXP:], io.ws_up[0].rearrange("(k p) n -> p k n", p=P)).then_inc(s_ws, 16)
            sp.dma_start(ws_dn[:, :, :], io.ws_down[0].rearrange("(k p) n -> p k n", p=P)).then_inc(s_ws, 16)
            for i in range(N_TILES):
                if i >= 2:
                    sp.wait_ge(s_z, 2 * (i - 1))
                sp.dma_start(res[:, i % 2, :], io.resid[i * P:(i + 1) * P, :]).then_inc(s_res[i % 2], 16)

        @block.scalar
        def _(act):
            link = chain(act, s_a)
            act.wait_ge(s_const, 1)
            for c in range(KH):
                act.activation(gn[:, c, 0:N_TOK].rearrange("p (k s) -> p s k", s=T),
                               gT[:, c, 0:N_TOK].rearrange("p (s k) -> p s k", s=T),
                               ACT.Gelu_apprx_tanh).then_inc(s_gelu, 1)
            act.wait_ge(s_small, 48)
            for n, (ch, mo) in enumerate(glu):
                lo, ln = TOK_CHUNKS[ch]
                act.wait_ge(s_glu, n + 1)
                if n >= 2:
                    act.wait_ge(s_mix, n - 1)
                act.activation(sig[:, n % 2, 0:ln], po[:, (n // 2) % 2, n % 2, 0:ln], ACT.Sigmoid,
                               bias=bglu[:, mo:mo + 1]).then_inc(s_sig, 1)
            act.wait_ge(s_ss, 1)
            act.activation(rr[:, :, :].rearrange("p a b -> p (a b)"), pm[:, 0:2 * N_TILES], ACT.Sqrt,
                           bias=eps[:, 0:1], scale=1.0 / D_HALF).then_inc(s_rt, 1)

            def std(i):
                act.wait_ge(s_zd, i + 1)
                act.activation(rs[:, 0:1], mv[:, 1:2], ACT.Sqrt, bias=eps[:, 1:2]).then_inc(s_std, 1)
                act.wait_ge(s_rstd, i + 1)
                if i >= 2:
                    act.wait_ge(s_tok[i % 2], 16 * (i // 2))
                    act.wait_ge(s_ao, 2 * (i - 1))
                act.activation(x[:, i % 2, :], z[:, :], ACT.Identity, bias=rs[:, 1:2],
                               scale=rs[:, 0:1]).then_inc(s_nm, 1)

            def rest(i):
                for h in range(2):
                    act.wait_ge(s_tr, 2 * i + h + 1)
                    if i and h == 0:
                        act.wait_ge(s_pg, i)
                    act.activation(xT[:, 4 * h:4 * h + 4, :], pt[:, h, :].rearrange("p (k t) -> p k t", k=4),
                                   ACT.Copy).then_inc(s_xT, 1)
                act.wait_ge(s_rl, i + 1)
                act.activation(keep.scores[:, i, :], pm[:, 0:N_EXP], ACT.Copy).then_inc(s_lg, 1)
                act.wait_ge(s_pg, i + 1)
                if i:
                    act.wait_ge(s_hid, i)
                act.activation(sg[:, :], pg[:, 0:D_EXP], ACT.Silu).then_inc(s_silu, 1)
                act.wait_ge(s_ht, i + 1)
                if i:
                    act.wait_ge(s_pd, 2 * i)
                act.activation(hidT[:, :, :].rearrange("p a b -> p (a b)"), pm[:, 128:384], ACT.Copy).then_inc(s_hT, 1)

            for i in range(N_TILES):
                std(i)
                if i:
                    rest(i - 1)
            rest(N_TILES - 1)

        @block.gpsimd
        def _(pool):
            link = chain(pool, s_g)
            link(pool.memset(gn[:, :, N_TOK:], 0.0))
            link(pool.memset(gT[:, :, N_TOK:], 0.0))
            link(pool.memset(ycT[:, :, N_TOK:], 0.0))
            link(pool.memset(ones[:, :], 1.0))
            link(pool.memset(eps[:, 0:1], RMS_EPS))
            pool.memset(eps[:, 1:2], LN_EPS).then_inc(s_const, 1)
            pool.wait_ge(s_small, 48)
            pool.wait_ge(s_wo, 16)
            for k in range(KD):
                pool.tensor_scalar(w_out[:, k, :], w_out[:, k, :], beta[:, k:k + 1], None, ALU.mult).then_inc(s_wob, 1)
            for part, src in ((1, ycT), (0, gT)):
                for c in range(KH):
                    if part == 0:
                        pool.wait_ge(s_mix, len(glu) - KH + c + 1)
                    if c == 0:
                        link(pool.tensor_tensor(ssq[:, part, :], src[:, c, :], src[:, c, :], ALU.mult))
                    else:
                        link(pool.tensor_tensor(sqt[:, :], src[:, c, :], src[:, c, :], ALU.mult))
                        link(pool.tensor_tensor(ssq[:, part, :], ssq[:, part, :], sqt[:, :], ALU.add))
            pool.sem_inc(s_ssq, 1)
            pool.wait_ge(s_ln, 32)
            for i in range(N_TILES):
                pool.wait_ge(s_gain, i + 1)
                pool.tensor_tensor(x[:, i % 2, :], x[:, i % 2, :], lnb[:, :], ALU.add).then_inc(s_x, 1)
                pool.wait_ge(s_x, i + 1)
                pool.dma_start(io.tok[i * P:(i + 1) * P, :], x[:, i % 2, :]).then_inc(s_tok[i % 2], 16)
                if i:
                    pool.wait_ge(s_ao, 2 * i)
                    pool.dma_start(io.acc[(i - 1) * P:i * P, :], ao[:, :]).then_inc(s_acc, 16)
            pool.wait_ge(s_ao, 2 * N_TILES)
            pool.dma_start(io.acc[(N_TILES - 1) * P:N_TILES * P, :], ao[:, :]).then_inc(s_acc, 16)
            pool.dma_start(io.tok[ROWS:ROWS + P, :], ao[:, :]).then_inc(s_acc, 16)
            pool.dma_start(io.acc[ROWS:ROWS + P, :], ao[:, :]).then_inc(s_acc, 16)
            pool.wait_ge(s_acc, 16 * (N_TILES + 2))
            for k in range(2):
                pool.wait_ge(s_tok[k], 16 * len(range(k, N_TILES, 2)))

        @block.tensor
        def _(pe):
            pe.wait_ge(s_wg, 16)
            pe.wait_ge(s_gelu, KH)
            for n, (ch, mo) in enumerate(glu):
                lo, ln = TOK_CHUNKS[ch]
                if n >= 4:
                    pe.wait_ge(s_sig, n - 3)
                for k in range(KH):
                    mm = pe.matmul(po[:, (n // 2) % 2, n % 2, 0:ln], w_glu[:, k, mo * P:(mo + 1) * P],
                                   gn[:, k, lo:lo + ln], start=(k == 0), stop=(k == KH - 1))
                mm.then_inc(s_glu, 1)
            pe.wait_ge(s_ssq, 1)
            for i in range(N_TILES):
                for h in range(2):
                    mm = pe.matmul(pm[:, 2 * i + h:2 * i + h + 1], ssq[:, h, i * P:(i + 1) * P], ones[:, :],
                                   start=True, stop=True)
            mm.then_inc(s_ss, 1)
            pe.wait_ge(s_sig, len(glu))
            pe.wait_ge(s_mix, len(glu))
            pe.wait_ge(s_wob, KD)

            def project(i):
                for h in range(2):
                    n = 2 * i + h
                    if n >= 2:
                        pe.wait_ge(s_z, n - 1)
                    for part, src in enumerate((gT, ycT)):
                        for k in range(KH):
                            mm = pe.matmul(po[:, n % 2, part, :], src[:, k, i * P:(i + 1) * P],
                                           w_out[:, KH * part + k, 512 * h:512 * (h + 1)],
                                           start=(k == 0), stop=(k == KH - 1))
                    mm.then_inc(s_po, 1)

            def shared(i):
                pe.wait_ge(s_x, i + 1)
                for h in range(2):
                    if i:
                        pe.wait_ge(s_ao, 2 * (i - 1) + h + 1)
                    for k in range(4):
                        tr = pe.transpose(pt[:, h, k * P:(k + 1) * P], x[:, i % 2, (4 * h + k) * P:(4 * h + k + 1) * P],
                                          keep.ident[:, :])
                    tr.then_inc(s_tr, 1)
                pe.wait_ge(s_xT, 2 * (i + 1))
                if i == 0:
                    pe.wait_ge(s_wr, 16)
                    pe.wait_ge(s_ws, 48)
                    pe.wait_ge(s_rt, 1)
                else:
                    pe.wait_ge(s_lg, i)
                    pe.wait_ge(s_hT, i)
                    pe.wait_ge(s_hid, i)
                for k in range(KD):
                    mm = pe.matmul(pm[:, 0:N_EXP], xT[:, k, :], w_rt[:, k, :], start=(k == 0), stop=(k == KD - 1))
                mm.then_inc(s_rl, 1)
                for k in range(KD):
                    mm = pe.matmul(pg[:, :], xT[:, k, :], ws_in[:, k, :], start=(k == 0), stop=(k == KD - 1))
                mm.then_inc(s_pg, 1)

            def shared_out(i):
                pe.wait_ge(s_hid, i + 1)
                pe.wait_ge(s_lg, i + 1)
                for k in range(2):
                    tr = pe.transpose(pm[:, 128 + k * P:128 + (k + 1) * P], hid[:, k * P:(k + 1) * P], keep.ident[:, :])
                tr.then_inc(s_ht, 1)
                pe.wait_ge(s_hT, i + 1)
                for h in range(2):
                    for k in range(2):
                        mm = pe.matmul(pt[:, h, :], hidT[:, k, :], ws_dn[:, k, 512 * h:512 * (h + 1)],
                                       start=(k == 0), stop=(k == 1))
                    mm.then_inc(s_pd, 1)

            for i in range(N_TILES):
                project(i)
                if i:
                    shared(i - 1)
                    shared_out(i - 1)
            shared(N_TILES - 1)
            shared_out(N_TILES - 1)

        @block.vector
        def _(v):
            link = chain(v, s_v)
            tt, ts, stt = v.tensor_tensor, v.tensor_scalar, v.scalar_tensor_tensor
            v.wait_ge(s_const, 1)
            v.wait_ge(s_gelu, KH)
            for n, (ch, mo) in enumerate(glu):
                lo, ln = TOK_CHUNKS[ch]
                v.wait_ge(s_sig, n + 1)
                tt(gT[:, mo, lo:lo + ln], gn[:, mo, lo:lo + ln], sig[:, n % 2, 0:ln], ALU.mult).then_inc(s_mix, 1)
            v.wait_ge(s_rt, 1)
            link(v.reciprocal(rr[:, :, :], rr[:, :, :]))

            def norm(i):
                v.wait_ge(s_res[i % 2], 16 * (i // 2 + 1))
                if i:
                    v.wait_ge(s_nm, i)
                for h in range(2):
                    n = 2 * i + h
                    cols = slice(512 * h, 512 * (h + 1))
                    v.wait_ge(s_po, n + 1)
                    link(stt(out=z[:, cols], in0=po[:, n % 2, 0, :], scalar=rr[:, i, 0:1], in1=res[:, i % 2, cols],
                             op0=ALU.mult, op1=ALU.add))
                    link(stt(out=z[:, cols], in0=po[:, n % 2, 1, :], scalar=rr[:, i, 1:2], in1=z[:, cols],
                             op0=ALU.mult, op1=ALU.add), s_z)
                    link(v.bn_stats(stats[:, h, :], z[:, cols]))
                link(v.bn_aggr(mv[:, :], stats[:, :, :]), s_zd)
                v.wait_ge(s_std, i + 1)
                link(v.reciprocal(rs[:, 0:1], rs[:, 0:1]))
                link(stt(out=rs[:, 1:2], in0=mv[:, 0:1], scalar=-1.0, in1=rs[:, 0:1], op0=ALU.mult, op1=ALU.mult),
                     s_rstd)
                v.wait_ge(s_nm, i + 1)
                if i == 0:
                    v.wait_ge(s_ln, 32)
                link(tt(x[:, i % 2, :], x[:, i % 2, :], lng[:, :], ALU.mult), s_gain)

            def rest(i):
                v.wait_ge(s_silu, i + 1)
                if i:
                    v.wait_ge(s_ht, i)
                link(tt(hid[:, :], sg[:, :], pg[:, D_EXP:], ALU.mult), s_hid)
                if i:
                    v.wait_ge(s_acc, 16 * i)
                v.wait_ge(s_x, i + 1)
                for h in range(2):
                    cols = slice(512 * h, 512 * (h + 1))
                    v.wait_ge(s_pd, 2 * i + h + 1)
                    link(stt(out=ao[:, cols], in0=x[:, i % 2, cols], scalar=ALPHA, in1=pt[:, h, :], op0=ALU.mult,
                             op1=ALU.add), s_ao)

            for i in range(N_TILES):
                norm(i)
                if i:
                    rest(i - 1)
            rest(N_TILES - 1)


def routing_stage(nc, io, keep, rt):
    with ExitStack() as ctx:
        m = Pools(nc, ctx, "route")
        NT, NE, NG = N_TILES, N_EXP, N_EGRP
        bias = m.sb("bias", [P, NE])
        sc = m.sb("sc", [P, NT, NE])
        sel = m.sb("sel", [P, NT, NE])
        g8 = m.sb("g8", [P, NT, NG, 8])
        gs = m.sb("gs", [P, NT, NG])
        gt, ge = m.sb("gt", [P, NT, NG, NG]), m.sb("ge", [P, NT, NG, NG])
        lower = m.sb("lower", [P, NG, NG])
        gm = m.sb("gm", [P, NT, NG])
        pen = m.sb("pen", [P, NT, NG])
        t8 = m.sb("t8", [P, NT, 8])
        i8 = m.sb("i8", [P, NT, 8], mybir.dt.uint32)
        f8 = m.sb("f8", [P, NT, 8])
        iota_e = m.sb("iota_e", [P, NE])
        hot = m.sb("hot", [P, NT, NE, TOP_K])
        mask = m.sb("mask", [P, NT, NE])
        mask_b = m.sb("mask_b", [P, NT, NE], BF16)
        wsum = m.sb("wsum", [P, NT])
        wt = m.sb("wt", [P, NT, NE])
        rest = m.sb("rest", [P, NT, NE])
        upper = m.sb("upper", [P, P], BF16)
        ones_b = m.sb("ones_b", [P, P], BF16)
        carry = m.sb("carry", [P, NT + 1, NE])
        pos = m.sb("pos", [P, NT, NE])
        extra, ends, cmp = m.sb("extra", [P, NE]), m.sb("ends", [P, NE]), m.sb("cmp", [P, NE])
        one_e = m.sb("one_e", [P, NE])
        row = m.sb("row", [P, 1])
        eo, jo, over, tmp1 = (m.sb(n, [P, 1]) for n in ("eo", "jo", "over", "tmp1"))
        evens = m.sb("evens", [1, 64])
        tabf = m.sb("tabf", [1, 2, P + 8])
        ps = m.ps("ps", [P, 4, 512])
        pt = m.ps("pt", [P, 512])
        s_bias, s_const, s_g, s_v = m.sem("bias"), m.sem("const"), m.sem("gch"), m.sem("vch")
        s_sig, s_mask, s_pos, s_eo, s_t, s_split, s_lg = (m.sem(n) for n in ("sig", "mask", "pos", "eo", "t", "split", "lg"))
        block = ctx.enter_context(nc.Block())
        HALVES = [(0, 5), (5, 4)]

        @block.sync
        def _(sp):
            sp.dma_start(bias[:, :], io.router_bias[0].partition_broadcast(P)).then_inc(s_bias, 16)

        @block.scalar
        def _(act):
            act.activation(sc[:, :, :], keep.scores[:, :, :], ACT.Sigmoid).then_inc(s_sig, 1)

        @block.gpsimd
        def _(pool):
            link = chain(pool, s_g)
            link(pool.memset(lower[:, :, :], 1.0))
            link(pool.affine_select(out=lower[:, :, :], in_=lower[:, :, :], compare_op=ALU.is_gt, fill=0.0, base=0,
                                    pattern=[[1, NG], [-1, NG]], channel_multiplier=0))
            link(pool.iota(rt.slot_i[:, :], pattern=[[1, P * SLOT_SETS]], base=0, channel_multiplier=0))
            link(pool.tensor_copy(rt.slot[:, :], rt.slot_i[:, :]))
            link(pool.tensor_copy(iota_e[:, :], rt.slot[:, 0:NE]))
            link(pool.iota(rt.slot_i[:, 0:1], pattern=[[1, 1]], base=0, channel_multiplier=1))
            link(pool.tensor_copy(row[:, :], rt.slot_i[:, 0:1]))
            link(pool.tensor_scalar(rt.dummy[:, :], row[:, :], float(ROWS), None, ALU.add))
            link(pool.memset(one_e[:, :], 1.0))
            link(pool.tensor_scalar(evens[:, :], rt.slot[0:1, 0:64], 2.0, 1.5, ALU.mult, ALU.add))
            for tile in range(NT):
                link(pool.memset(rt.vals[:, 0, tile, 1:2], float(tile)))
            link(pool.tensor_copy(rt.vals[:, 0, :, 0:1], row[:, 0:1].unsqueeze(1).to_broadcast([P, NT, 1])))
            link(pool.memset(rt.vals[:, 0, :, 2:3], 1.0))
            link(pool.tensor_copy(rt.vals[:, 1, :, 0:3], rt.vals[:, 0, :, 0:3]))
            link(pool.memset(ones_b[:, :], 1.0))
            link(pool.affine_select(out=upper[:, :], in_=ones_b[:, :], compare_op=ALU.is_gt, fill=0.0, base=0,
                                    pattern=[[1, P]], channel_multiplier=-1))
            pool.memset(rt.tab[:, :, :], 0).then_inc(s_const, 1)

        @block.tensor
        def _(pe):
            pe.wait_ge(s_mask, 1)
            for k, (lo, n) in enumerate(HALVES):
                pe.matmul(ps[:, k, 0:n * NE], upper[:, :], mask_b[:, lo:lo + n, :].rearrange("p a b -> p (a b)"),
                          start=True, stop=True)
                mm = pe.matmul(ps[:, 2 + k, 0:n * NE], ones_b[:, :],
                               mask_b[:, lo:lo + n, :].rearrange("p a b -> p (a b)"), start=True, stop=True)
            mm.then_inc(s_pos, 1)
            pe.wait_ge(s_eo, 1)
            pe.transpose(pt[0:1, 0:P], eo[:, 0:1], keep.ident[:, :])
            pe.transpose(pt[0:1, P:2 * P], jo[:, 0:1], keep.ident[:, :]).then_inc(s_t, 1)

        @block.vector
        def _(v):
            link = chain(v, s_v)
            tt, ts, stt = v.tensor_tensor, v.tensor_scalar, v.scalar_tensor_tensor
            v.wait_ge(s_bias, 16)
            v.wait_ge(s_sig, 1)
            v.wait_ge(s_const, 1)
            link(tt(sel[:, :, :], sc[:, :, :], bc(bias[:, :], 1, NT), ALU.add))
            per = NE // NG
            for i in range(NT):
                for g in range(NG):
                    mx = v.max(g8[:, i, g, :], sel[:, i, per * g:per * (g + 1)])
            link(mx)
            link(tt(gs[:, :, :], g8[:, :, :, 0], g8[:, :, :, 1], ALU.add))
            other, own = bc(gs[:, :, :], 2, NG), bc(gs[:, :, :], 3, NG)
            tt(gt[:, :, :, :], other, own, ALU.is_gt)
            link(tt(ge[:, :, :, :], other, own, ALU.is_equal))
            for i in range(NT):
                lo = tt(ge[:, i, :, :], ge[:, i, :, :], lower[:, :, :], ALU.mult)
            link(lo)
            link(tt(gt[:, :, :, :], gt[:, :, :, :], ge[:, :, :, :], ALU.add))
            link(v.reduce_sum(gm[:, :, :], gt[:, :, :, :], axis=mybir.AxisListType.X))
            link(ts(gm[:, :, :], gm[:, :, :], TOP_GROUPS - 0.5, None, ALU.is_lt))
            link(ts(pen[:, :, :], gm[:, :, :], 1e30, -1e30, ALU.mult, ALU.add))
            sel4 = sel[:, :, :].rearrange("p t (g e) -> p (t g) e", g=NG)
            gmf, penf = (bc(a[:, :, :].rearrange("p t g -> p (t g)"), 2, per) for a in (gm, pen))
            link(tt(sel4, sel4, gmf, ALU.mult))
            link(tt(sel4, sel4, penf, ALU.add))
            for i in range(NT):
                mx = v.max(t8[:, i, :], sel[:, i, :])
            link(mx)
            for i in range(NT):
                mx = v.max_index(i8[:, i, :], t8[:, i, :], sel[:, i, :])
            link(mx)
            link(v.tensor_copy(f8[:, :, :], i8[:, :, :]))
            for i in range(NT):
                eq = tt(hot[:, i, :, :], bc(f8[:, i, 0:TOP_K], 1, NE), bc(iota_e[:, :], 2, TOP_K), ALU.is_equal)
            link(eq)
            link(v.reduce_sum(mask[:, :, :], hot[:, :, :, :], axis=mybir.AxisListType.X))
            link(v.memset(mask[LAST_ROWS:P, NT - 1, :], 0.0))
            link(v.tensor_copy(mask_b[:, :, :], mask[:, :, :]), s_mask)
            link(tt(wt[:, :, :], sc[:, :, :], mask[:, :, :], ALU.mult))
            link(v.reduce_sum(wsum[:, :], wt[:, :, :], axis=mybir.AxisListType.X))
            link(ts(wsum[:, :], wsum[:, :], 1e-30, None, ALU.max))
            link(v.reciprocal(wsum[:, :], wsum[:, :]))
            link(tt(wt[:, :, :], wt[:, :, :], bc(wsum[:, :], 2, NE), ALU.mult))
            link(ts(wt[:, :, :], wt[:, :, :], ROUTED_SCALE, None, ALU.mult))
            src = wt
            for k in range(3):
                link(v.tensor_copy(rt.parts[:, :, :, k], src[:, :, :]))
                if k < 2:
                    link(tt(rest[:, :, :], src[:, :, :], rt.parts[:, :, :, k], ALU.subtract))
                    src = rest
            v.wait_ge(s_pos, 1)
            link(v.memset(carry[:, 0, :], 0.0))
            for i in range(NT):
                k, o = (0, i) if i < 5 else (1, i - 5)
                link(tt(carry[:, i + 1, :], carry[:, i, :], ps[:, 2 + k, o * NE:(o + 1) * NE], ALU.add))
            for k, (lo, n) in enumerate(HALVES):
                p = tt(pos[:, lo:lo + n, :], ps[:, k, 0:n * NE].rearrange("p (a b) -> p a b", a=n),
                       carry[:, lo:lo + n, :], ALU.add)
            link(p)
            link(ts(pos[:, :, :], pos[:, :, :], 1.0, None, ALU.add))
            link(tt(pos[:, :, :], pos[:, :, :], mask[:, :, :], ALU.mult))
            link(ts(rt.posm[:, :, :], pos[:, :, :], -1.0, None, ALU.add))
            cnt = carry[:, NT, :]
            link(ts(extra[:, :], cnt, float(P) + 0.5, None, ALU.is_gt))
            for j in range(2, NT):
                link(ts(cmp[:, :], cnt, float(P * j) + 0.5, None, ALU.is_gt))
                link(tt(extra[:, :], extra[:, :], cmp[:, :], ALU.add))
            link(v.tensor_tensor_scan(ends[:, :], one_e[:, :], extra[:, :], 0.0, ALU.mult, ALU.add))
            total = ends[:, NE - 1:NE]
            link(ts(cmp[:, :], ends[:, :], row[:, 0:1], None, ALU.is_le))
            link(v.reduce_sum(eo[:, :], cmp[:, :], axis=mybir.AxisListType.X))
            link(tt(cmp[:, :], cmp[:, :], extra[:, :], ALU.mult))
            link(v.reduce_sum(tmp1[:, :], cmp[:, :], axis=mybir.AxisListType.X))
            link(ts(jo[:, :], row[:, :], tmp1[:, 0:1], 1.0, ALU.subtract, ALU.add))
            link(tt(over[:, :], row[:, :], total, ALU.is_ge))
            link(ts(eo[:, :], eo[:, :], float(NE - 1), None, ALU.min))
            link(ts(over[:, :], over[:, :], 1000.0, None, ALU.mult))
            link(tt(jo[:, :], jo[:, :], over[:, :], ALU.add))
            link(ts(jo[:, :], jo[:, :], float(SLOT_SETS - 1), None, ALU.min))
            link(ts(jo[:, :], jo[:, :], float(P), None, ALU.mult), s_eo)
            link(v.tensor_copy(tabf[0:1, 0, 0:NE], iota_e[0:1, :]))
            link(v.memset(tabf[0:1, 1, 0:NE], 0.0))
            v.wait_ge(s_t, 1)
            OV = P + 8 - NE
            for k in range(2):
                link(v.tensor_copy(tabf[0:1, k, NE:P + 8], pt[0:1, k * P:k * P + OV]))
            link(v.tensor_copy(rt.tab[0:1, 0:2, :], tabf[:, :, :]))
            link(tt(evens[:, :], evens[:, :], ends[0:1, NE - 1:NE].to_broadcast([1, 64]), ALU.is_lt))
            link(v.reduce_sum(tmp1[0:1, :], evens[:, :], axis=mybir.AxisListType.X))
            link(ts(tmp1[0:1, :], tmp1[0:1, :], 2.0, float(NE), ALU.mult, ALU.add))
            link(v.tensor_copy(rt.tab[0:1, 2, 0:1], tmp1[0:1, :]))


def expert_stage(nc, io, keep, rt):
    with ExitStack() as ctx:
        m = Pools(nc, ctx, "moe")
        wgu = m.sb("wgu", [P, 2, KD, 2 * D_EXP])
        wd = m.sb("wd", [P, 2, 2, D])
        pick = m.sb("pick", [P, 2, N_TILES, P], BF16)
        info = m.sb("info", [P, 8])
        tmp = m.sb("tmp", [P, 2])
        idx_g = m.sb("idx_g", [P, 2], I32)
        idx_s = m.sb("idx_s", [P, 2], I32)
        gate = m.sb("gate", [P, 2])
        xg = m.sb("xg", [P, 2, D])
        xT = m.sb("xT", [P, 2, KD, P])
        sg = m.sb("sg", [P, 2, D_EXP])
        hid = m.sb("hid", [P, 2, D_EXP])
        hidT = m.sb("hidT", [P, 2, 2, P])
        y = m.sb("y", [P, 2, D])
        p_gu = m.ps("p_gu", [P, 2, 512])
        p_dn = m.ps("p_dn", [P, 2, 512])
        p_tr = m.ps("p_tr", [P, 2, 512])
        p_ht = m.ps("p_ht", [P, 512])
        p_im = m.ps("p_im", [P, 512])
        up_done, down_done, x_turned, info_done, hid_turned = (m.sem(n) for n in ("gu", "dn", "tr", "im", "ht"))
        silu_done, xT_act, y_act = m.sem("silu"), m.sem("xa"), m.sem("da")
        pick_done, hid_done, xT_dve, hidT_done, idx_done, y_dve, s_v = (
            m.sem(n) for n in ("sel", "hid", "xd", "hd", "ix", "dd", "vch"))
        gathered = [m.sem("ga0"), m.sem("ga1")]
        added = [m.sem("sc0"), m.sem("sc1")]
        w_up_in = [m.sem("wgu0"), m.sem("wgu1")]
        w_down_in = [m.sem("wd0"), m.sem("wd1")]
        go = m.sem("go")
        block = ctx.enter_context(nc.Block())
        w_g = io.w_gate[0].rearrange("e (k p) n -> e p k n", p=P)
        w_u = io.w_up[0].rearrange("e (k p) n -> e p k n", p=P)
        w_d = io.w_down[0].rearrange("e (k p) n -> e p k n", p=P)
        HEAD = 3

        def wait(eng, sem, value):
            if not isinstance(value, int) or value > 0:
                eng.wait_ge(sem, value)

        def dma_count(n, par):
            return n * 8 + (16 - 8 * par)

        def over_blocks(eng, body):
            last = eng.value_load(rt.tab[0:1, 2, 0:1], min_val=N_EXP, max_val=N_EXP + 64)
            for n in range(HEAD):
                body(n, n % 2)
            with eng.Fori(2, last, 2) as b:
                for u in (1, 2):
                    body(b + u, u % 2)
            return last

        def entry(eng, k, n, top):
            at = n if isinstance(n, int) else bass.ds(n, 1)
            ap = rt.tab[0:1, k, n:n + 1] if isinstance(n, int) else rt.tab[0:1, k, at]
            return eng.value_load(ap, min_val=0, max_val=top)

        @block.sync
        def _(sp):
            def load(n, par):
                e = entry(sp, 0, n, N_EXP - 1)
                wait(sp, up_done, n - 1)
                for half, src in enumerate((w_g, w_u)):
                    sp.dma_start(wgu[:, par, :, D_EXP * half:D_EXP * (half + 1)],
                                 src[bass.ds(e, 1)].rearrange("a p k n -> (a p) k n")).then_inc(w_up_in[par], 16)
                wait(sp, down_done, n - 1)
                sp.dma_start(wd[:, par, :, :],
                             w_d[bass.ds(e, 1)].rearrange("a p k n -> (a p) k n")).then_inc(w_down_in[par], 16)
            over_blocks(sp, load)

        @block.scalar
        def _(act):
            def silu(n, par):
                wait(act, up_done, n + 1)
                wait(act, hid_done, n - 1)
                act.activation(sg[:, par, :], p_gu[:, par, 0:D_EXP], ACT.Silu).then_inc(silu_done, 1)

            def y_out(n, par):
                wait(act, down_done, n + 1)
                wait(act, added[par], dma_count(n - 2, par) if not isinstance(n, int) else 16 * (n // 2))
                act.activation(y[:, par, 0:512], p_dn[:, 0, :], ACT.Copy).then_inc(y_act, 1)

            def x_out(n, par):
                wait(act, x_turned, n + 1)
                wait(act, up_done, n - 1)
                act.activation(xT[:, par, 0:4, :], p_tr[:, 0, :].rearrange("p (k t) -> p k t", k=4),
                               ACT.Copy).then_inc(xT_act, 1)

            def body(n, par):
                if isinstance(n, int) and n == 0:
                    x_out(0, 0)
                    silu(0, 0)
                    x_out(1, 1)
                    return
                silu(n, par)
                y_out(n - 1, 1 - par)
                x_out(n + 1, 1 - par)
            over_blocks(act, body)
            last = act.value_load(rt.tab[0:1, 2, 0:1], min_val=N_EXP, max_val=N_EXP + 64)
            y_out(last + 0, 0)

        @block.gpsimd
        def _(pool):
            def gather(n, par):
                wait(pool, idx_done, n + 1)
                wait(pool, x_turned, n - 1)
                pool.sem_inc(go, 1)
                pool.indirect_dma_start(out=xg[:, par, :], out_offset=None, in_=io.tok,
                                        in_offset=bass.IndirectOffsetOnAxis(ap=idx_g[:, par:par + 1], axis=0)
                                        ).then_inc(gathered[par], 16)

            def scatter(n, par):
                wait(pool, y_act, n + 1)
                wait(pool, y_dve, n + 1)
                wait(pool, added[1 - par], dma_count(n - 1, 1 - par) if not isinstance(n, int) or n else 0)
                pool.sem_inc(go, 1)
                pool.indirect_dma_start(out=io.acc, in_=y[:, par, :], in_offset=None,
                                        out_offset=bass.IndirectOffsetOnAxis(ap=idx_s[:, par:par + 1], axis=0),
                                        compute_op=ALU.add).then_inc(added[par], 16)

            def body(n, par):
                if isinstance(n, int) and n == 0:
                    for k in range(3):
                        gather(k, k % 2)
                    return
                scatter(n - 1, 1 - par)
                gather(n + 2, par)
            last = over_blocks(pool, body)
            scatter(last + 0, 0)
            wait(pool, added[0], dma_count(last, 0))
            wait(pool, gathered[0], dma_count(last + 2, 0))
            wait(pool, gathered[1], dma_count(last + 1, 1))

        @block.tensor
        def _(pe):
            def up(n, par):
                wait(pe, w_up_in[par], n * 16 + (32 - 16 * par))
                wait(pe, xT_act, n + 1)
                wait(pe, xT_dve, n + 1)
                wait(pe, hid_done, n - 1)
                for k in range(KD):
                    mm = pe.matmul(p_gu[:, par, :], xT[:, par, k, :], wgu[:, par, k, :], start=(k == 0), stop=(k == KD - 1))
                mm.then_inc(up_done, 1)

            def down(n, par):
                wait(pe, w_down_in[par], dma_count(n, par))
                wait(pe, hidT_done, n + 1)
                wait(pe, y_act, n)
                wait(pe, y_dve, n)
                for h in range(2):
                    for k in range(2):
                        mm = pe.matmul(p_dn[:, h, :], hidT[:, par, k, :], wd[:, par, k, 512 * h:512 * (h + 1)],
                                       start=(k == 0), stop=(k == 1))
                mm.then_inc(down_done, 1)

            def turn_x(n, par):
                wait(pe, gathered[par], dma_count(n, par))
                wait(pe, xT_act, n)
                wait(pe, xT_dve, n)
                for k in range(KD):
                    tr = pe.transpose(p_tr[:, k // 4, (k % 4) * P:(k % 4 + 1) * P], xg[:, par, k * P:(k + 1) * P],
                                      keep.ident[:, :])
                tr.then_inc(x_turned, 1)

            def look_up(n, par):
                wait(pe, pick_done, n + 1)
                wait(pe, idx_done, n)
                for k in range(N_TILES):
                    mm = pe.matmul(p_im[:, 0:6], pick[:, par, k, :], rt.vals[:, par, k, :], start=(k == 0),
                                   stop=(k == N_TILES - 1))
                mm.then_inc(info_done, 1)

            def turn_hid(n, par):
                wait(pe, hid_done, n + 1)
                wait(pe, hidT_done, n)
                for k in range(2):
                    tr = pe.transpose(p_ht[:, k * P:(k + 1) * P], hid[:, par, k * P:(k + 1) * P], keep.ident[:, :])
                tr.then_inc(hid_turned, 1)

            def body(n, par):
                if isinstance(n, int) and n == 0:
                    look_up(0, 0)
                    look_up(1, 1)
                    turn_x(0, 0)
                    up(0, 0)
                else:
                    up(n, par)
                    down(n - 1, 1 - par)
                turn_x(n + 1, 1 - par)
                look_up(n + 2, par)
                turn_hid(n, par)
            last = over_blocks(pe, body)
            down(last + 0, 0)

        @block.vector
        def _(v):
            tt, ts, stt = v.tensor_tensor, v.tensor_scalar, v.scalar_tensor_tensor

            def choose(n, par):
                e = entry(v, 0, n, N_EXP - 1)
                j = entry(v, 1, n, P * (SLOT_SETS - 1))
                wait(v, info_done, n - 1)
                tt(pick[:, par, :, :], bc(rt.slot[:, bass.ds(j, P)], 1, N_TILES),
                   rt.posm[:, :, bass.ds(e, 1)].to_broadcast([P, N_TILES, P]), ALU.is_equal)
                v.tensor_copy(rt.vals[:, par, :, 3:6].unsqueeze(2), rt.parts[:, :, bass.ds(e, 1), :]).then_inc(pick_done, 1)

            def index(n, par, link):
                wait(v, info_done, n + 1)
                wait(v, hid_done, n - 1)
                wait(v, gathered[par], dma_count(n - 2, par) if not isinstance(n, int) else 16 * (n // 2))
                link(v.tensor_copy(info[:, 0:6], p_im[:, 0:6]))
                ts(tmp[:, 0:1], info[:, 2:3], -1.0, 1.0, ALU.mult, ALU.add)
                stt(out=tmp[:, 1:2], in0=info[:, 1:2], scalar=float(P), in1=info[:, 0:1], op0=ALU.mult, op1=ALU.add)
                link(tt(gate[:, par:par + 1], info[:, 3:4], info[:, 4:5], ALU.add))
                tt(gate[:, par:par + 1], gate[:, par:par + 1], info[:, 5:6], ALU.add)
                link(stt(out=tmp[:, 0:1], in0=tmp[:, 0:1], scalar=rt.dummy[:, 0:1], in1=tmp[:, 1:2], op0=ALU.mult,
                         op1=ALU.add))
                v.tensor_copy(idx_g[:, par:par + 1], tmp[:, 0:1]).then_inc(idx_done, 1)
                wait(v, idx_done, n + 1)

            def hidden(n, par):
                wait(v, silu_done, n + 1)
                wait(v, hid_turned, n - 1)
                wait(v, added[par], dma_count(n - 2, par) if not isinstance(n, int) else 16 * (n // 2))
                v.tensor_copy(idx_s[:, par:par + 1], idx_g[:, par:par + 1])
                stt(out=hid[:, par, :], in0=sg[:, par, :], scalar=gate[:, par:par + 1], in1=p_gu[:, par, D_EXP:],
                    op0=ALU.mult, op1=ALU.mult).then_inc(hid_done, 1)

            def x_out(n, par):
                wait(v, x_turned, n + 1)
                wait(v, up_done, n - 1)
                v.tensor_copy(xT[:, par, 4:8, :], p_tr[:, 1, :].rearrange("p (k t) -> p k t", k=4)).then_inc(xT_dve, 1)

            def y_out(n, par):
                wait(v, down_done, n + 1)
                wait(v, added[par], dma_count(n - 2, par) if not isinstance(n, int) else 16 * (n // 2))
                v.tensor_copy(y[:, par, 512:], p_dn[:, 1, :]).then_inc(y_dve, 1)

            def hid_out(n, par):
                wait(v, hid_turned, n + 1)
                wait(v, down_done, n - 1)
                v.tensor_copy(hidT[:, par, :, :], p_ht[:, 0:2 * P].rearrange("p (k t) -> p k t", k=2)).then_inc(hidT_done, 1)

            LINKS = 3

            def linker(n):
                k = [0]

                def link(ins):
                    k[0] += 1
                    ins.then_inc(s_v, 1)
                    v.wait_ge(s_v, n * LINKS + k[0])
                return link

            def body(n, par):
                if isinstance(n, int) and n == 0:
                    choose(0, 0)
                    choose(1, 1)
                    index(0, 0, linker(0))
                    index(1, 1, linker(1))
                    x_out(0, 0)
                choose(n + 2, par)
                hidden(n, par)
                if not isinstance(n, int) or n:
                    y_out(n - 1, 1 - par)
                x_out(n + 1, 1 - par)
                index(n + 2, par, linker(n + 2))
                hid_out(n, par)
            last = over_blocks(v, body)
            y_out(last + 0, 0)


def final_stage(nc, io, keep):
    with ExitStack() as ctx:
        m = Pools(nc, ctx, "final")
        x = m.sb("x", [P, N_TILES, D])
        lng, lnb = m.sb("lng", [P, D]), m.sb("lnb", [P, D])
        stats = m.sb("stats", [P, N_TILES, 2, 6])
        mv = m.sb("mv", [P, N_TILES, 2])
        rs = m.sb("rs", [P, N_TILES, 2])
        eps = m.sb("eps", [P, 1])
        s_x = [m.sem(f"x{i}") for i in range(N_TILES)]
        s_ln, s_eps, s_stat, s_std, s_rs, s_nm, s_gain, s_y, s_out, s_v = (
            m.sem(n) for n in ("ln", "eps", "stat", "std", "rs", "nm", "gain", "y", "out", "vch"))
        block = ctx.enter_context(nc.Block())

        @block.sync
        def _(sp):
            for i in range(N_TILES):
                sp.dma_start(x[:, i, :], io.acc[i * P:(i + 1) * P, :]).then_inc(s_x[i], 16)
            for i in range(N_TILES):
                sp.wait_ge(s_y, i + 1)
                if i < N_TILES - 1:
                    sp.dma_start(io.out_y_p[0, i * P:(i + 1) * P, :], x[:, i, :]).then_inc(s_out, 16)
                else:
                    sp.dma_start(io.out_y_s[0], x[0:LAST_ROWS, i, :]).then_inc(s_out, 16)
            sp.wait_ge(s_out, 16 * N_TILES)

        @block.gpsimd
        def _(pool):
            pool.memset(eps[:, :], LN_EPS).then_inc(s_eps, 1)
            pool.wait_ge(s_ln, 32)
            for i in range(N_TILES):
                pool.wait_ge(s_gain, i + 1)
                pool.tensor_tensor(x[:, i, :], x[:, i, :], lnb[:, :], ALU.add).then_inc(s_y, 1)

        @block.scalar
        def _(act):
            act.dma_start(lng[:, :], io.ln2_g[0].partition_broadcast(P)).then_inc(s_ln, 16)
            act.dma_start(lnb[:, :], io.ln2_b[0].partition_broadcast(P)).then_inc(s_ln, 16)
            act.wait_ge(s_eps, 1)
            for i in range(N_TILES):
                act.wait_ge(s_stat, i + 1)
                act.activation(rs[:, i, 0:1], mv[:, i, 1:2], ACT.Sqrt, bias=eps[:, 0:1]).then_inc(s_std, 1)
                act.wait_ge(s_rs, i + 1)
                act.activation(x[:, i, :], x[:, i, :], ACT.Identity, bias=rs[:, i, 1:2],
                               scale=rs[:, i, 0:1]).then_inc(s_nm, 1)

        @block.vector
        def _(v):
            link = chain(v, s_v)

            def scale(i):
                v.wait_ge(s_std, i + 1)
                link(v.reciprocal(rs[:, i, 0:1], rs[:, i, 0:1]))
                v.scalar_tensor_tensor(out=rs[:, i, 1:2], in0=mv[:, i, 0:1], scalar=-1.0, in1=rs[:, i, 0:1],
                                       op0=ALU.mult, op1=ALU.mult).then_inc(s_rs, 1)

            def gain(i):
                v.wait_ge(s_nm, i + 1)
                if i == 0:
                    v.wait_ge(s_ln, 32)
                v.tensor_tensor(x[:, i, :], x[:, i, :], lng[:, :], ALU.mult).then_inc(s_gain, 1)

            for i in range(N_TILES):
                v.wait_ge(s_x[i], 16)
                v.bn_stats(stats[:, i, 0, :], x[:, i, 0:512])
                link(v.bn_stats(stats[:, i, 1, :], x[:, i, 512:]))
                v.bn_aggr(mv[:, i, :], stats[:, i, :, :]).then_inc(s_stat, 1)
                if i:
                    gain(i - 1)
                scale(i)
            gain(N_TILES - 1)


def build(nc, args):
    io = Names()
    io.x_prompt, io.x_sample, io.state_ssm_re = args["x_prompt"], args["x_sample"], args["state_ssm_re"]
    io.state_ssm_im, io.cache_conv, io.ln_in_g = args["state_ssm_im"], args["cache_conv"], args["ln_in_g"]
    io.ln_in_b, io.w_in, io.lam_re = args["ln_in_b"], args["w_in"], args["lam_re"]
    io.lam_im, io.log_dt, io.ssm_b_re = args["lam_im"], args["log_dt"], args["ssm_b_re"]
    io.ssm_b_im, io.ssm_c_re, io.ssm_c_im = args["ssm_b_im"], args["ssm_c_re"], args["ssm_c_im"]
    io.ssm_d, io.w_glu, io.b_glu = args["ssm_d"], args["w_glu"], args["b_glu"]
    io.conv_w, io.beta_ssm, io.beta_conv = args["conv_w"], args["beta_ssm"], args["beta_conv"]
    io.w_out, io.ln1_g, io.ln1_b = args["w_out"], args["ln1_g"], args["ln1_b"]
    io.w_router, io.router_bias, io.w_gate = args["w_router"], args["router_bias"], args["w_gate"]
    io.w_up, io.w_down, io.ws_gate = args["w_up"], args["w_down"], args["ws_gate"]
    io.ws_up, io.ws_down, io.ln2_g = args["ws_up"], args["ws_down"], args["ln2_g"]
    io.ln2_b, io.out_y_p, io.out_y_s = args["ln2_b"], args["out_y_p"], args["out_y_s"]
    io.out_ssm_re_p, io.out_ssm_im_p, io.out_conv_p = args["out_ssm_re_p"], args["out_ssm_im_p"], args["out_conv_p"]
    io.out_ssm_re_s, io.out_ssm_im_s, io.out_conv_s = args["out_ssm_re_s"], args["out_ssm_im_s"], args["out_conv_s"]

    def dram(name, shape):
        return nc.dram_tensor(name, shape, F32, kind="Internal").ap()

    io.resid = dram("resid", (ROWS, D))
    io.ud = dram("ud", (D_HALF, N_TOK))
    io.yd = dram("yd", (D_HALF, N_TOK))
    io.tok = dram("tok", (ROWS + P, D))
    io.acc = dram("acc", (ROWS + P, D))
    with ExitStack() as ctx:
        m = Pools(nc, ctx, "keep")
        keep = Names()
        keep.ident = m.sb("ident", [P, P])
        keep.scores = m.sb("scores", [P, N_TILES, N_EXP])
        with ExitStack() as half:
            h = Pools(nc, half, "keep")
            keep.gT = h.sb("gT", [P, KH, ROWS])
            keep.ycT = h.sb("ycT", [P, KH, ROWS])
            with ExitStack() as first:
                f = Pools(nc, first, "co")
                keep.hT = f.sb("hT", [P, KD, N_TOK])
                co = Names()
                co.sign = f.sb("sign", [P, 1])
                co.pr = f.sb("pr", [P, GROUPS, T + 1])
                co.pi = f.sb("pi", [P, GROUPS, T + 1])
                co.prs = f.sb("prs", [P, GROUPS, T + 1])
                co.npi = f.sb("npi", [P, GROUPS, T + 1])
                co.nsi = f.sb("nsi", [P, GROUPS, T + 1])
                co.bb = f.sb("bb", [P, GROUPS, GC])
                co.bbsw = f.sb("bbsw", [P, GROUPS, GC])
                co.cs = f.sb("cs", [P, KH * P])
                co.csw = f.sb("csw", [P, KH * P])
                co.h0 = f.sb("h0", [P, GROUPS])
                co.ah0 = f.sb("ah0", [P, GROUPS])
                co.er = f.sb("er", [P, GROUPS, 7])
                co.eis = f.sb("eis", [P, GROUPS, 7])
                co.decay = f.sb("decay", [P, GROUPS])
                trunk_stage(nc, io, keep, co)
                mixing_stage(nc, io, keep, co)
            output_stage(nc, io, keep)
        with ExitStack() as moe:
            r = Pools(nc, moe, "rt")
            rt = Names()
            rt.slot_i = r.sb("slot_i", [P, P * SLOT_SETS], I32)
            rt.slot = r.sb("slot", [P, P * SLOT_SETS])
            rt.dummy = r.sb("dummy", [P, 1])
            rt.vals = r.sb("vals", [P, 2, N_TILES, 6], BF16)
            rt.parts = r.sb("parts", [P, N_TILES, N_EXP, 3], BF16)
            rt.posm = r.sb("posm", [P, N_TILES, N_EXP])
            rt.tab = r.sb("tab", [1, 3, P + 8], I32)
            routing_stage(nc, io, keep, rt)
            expert_stage(nc, io, keep, rt)
        final_stage(nc, io, keep)
    return


_INS = ['x_prompt', 'x_sample', 'state_ssm_re', 'state_ssm_im', 'cache_conv', 'ln_in_g', 'ln_in_b', 'w_in', 'lam_re',
        'lam_im', 'log_dt', 'ssm_b_re', 'ssm_b_im', 'ssm_c_re', 'ssm_c_im', 'ssm_d', 'w_glu', 'b_glu', 'conv_w',
        'beta_ssm', 'beta_conv', 'w_out', 'ln1_g', 'ln1_b', 'w_router', 'router_bias', 'w_gate', 'w_up', 'w_down',
        'ws_gate', 'ws_up', 'ws_down', 'ln2_g', 'ln2_b']
_OUTS = [("out_y_p", (1, 1024, 1024)), ("out_y_s", (1, 64, 1024)),
         ("out_ssm_re_p", (1, 1, 32, 64)), ("out_ssm_im_p", (1, 1, 32, 64)), ("out_conv_p", (1, 1, 2, 512)),
         ("out_ssm_re_s", (1, 1, 32, 64)), ("out_ssm_im_s", (1, 1, 32, 64)), ("out_conv_s", (1, 1, 2, 512))]


def kernel(**inputs):
    import numpy as _np
    import concourse.bacc as _bacc
    from concourse import mybir as _mybir
    from concourse.bass_utils import run_bass_kernel_spmd as _run

    nc = _bacc.Bacc("TRN2", target_bir_lowering=False, num_devices=1)
    arrays, args = {}, {}
    for name in _INS:
        a = _np.ascontiguousarray(inputs[name])
        arrays[f"in_{name}_dram"] = a
        args[name] = nc.dram_tensor(f"in_{name}_dram", a.shape, _mybir.dt.from_np(a.dtype), kind="ExternalInput").ap()
    for name, shape in _OUTS:
        args[name] = nc.dram_tensor(f"{name}_dram", shape, _mybir.dt.from_np(_np.dtype("float32")),
                                    kind="ExternalOutput").ap()
    build(nc, args)
    r = _run(nc, [arrays], core_ids=[0])
    return tuple(r.results[0][f"{name}_dram"] for name, _ in _OUTS)
```

```python
from contextlib import ExitStack

import numpy as np
import concourse.bass as bass
from concourse import mybir

ALU = mybir.AluOpType
ACT = mybir.ActivationFunctionType
F32 = mybir.dt.float32
F32R = mybir.dt.float32r
I32 = mybir.dt.int32
BF16 = mybir.dt.bfloat16

P = 128
D = 1024
KD = D // P
N_PROMPT = 1024
N_SAMPLE = 64
N_TOK = N_PROMPT + N_SAMPLE
N_TILES = (N_TOK + P - 1) // P
LAST_ROWS = N_TOK - (N_TILES - 1) * P
ROWS = N_TILES * P
D_HALF = 512
KH = D_HALF // P
GROUPS = 32
GC = 16
STATE = 64
GT = P // GC
T = 8
NK = N_TOK // T
NKP = N_PROMPT // T
N_EXP = 64
N_EGRP = 8
TOP_GROUPS = 4
TOP_K = 6
D_EXP = 256
ROUTED_SCALE = 2.5
SLOT_SETS = N_TILES + 1
CW = 384
TOK_CHUNKS = [(0, CW), (CW, CW), (2 * CW, N_TOK - 2 * CW)]
ALPHA = 2.0 ** 0.25
LN_EPS = 1e-5
RMS_EPS = 1e-6
TWO_PI_HI = 6.28125
TWO_PI_MID = 0.0019350051879882812
TWO_PI_LO = 3.019915981956753e-07
ROUND = 12582912.0
PI_BELOW = 3.1415925
TRIPLES = [(0, 3), (3, 3), (6, 2)]


class Names:
    pass


def chain(eng, own):
    count = {}

    def link(ins, sem=own):
        count[sem] = count.get(sem, 0) + 1
        ins.then_inc(sem, 1)
        eng.wait_ge(sem, count[sem])
    return link


def bc(ap, axis, n):
    shape = list(ap.shape)
    shape.insert(axis, n)
    return ap.unsqueeze(axis).to_broadcast(shape)


class Pools:

    def __init__(self, nc, ctx, stage):
        self.nc, self.ctx, self.stage, self.sems = nc, ctx, stage, []
        ctx.callback(self.clear)

    def sb(self, name, shape, dt=F32):
        return self.ctx.enter_context(self.nc.sbuf_tensor(f"{self.stage}_{name}", shape, dt))

    def ps(self, name, shape, dt=F32):
        return self.ctx.enter_context(self.nc.psum_tensor(f"{self.stage}_{name}", shape, dt))

    def sem(self, name):
        self.sems.append(self.nc.alloc_semaphore(f"{self.stage}_{name}"))
        return self.sems[-1]

    def clear(self):
        if self.sems:
            self.nc.clear_and_free_semaphores(self.sems)
            self.nc.all_engine_barrier()


def trunk_stage(nc, io, keep, co):
    with ExitStack() as ctx:
        m = Pools(nc, ctx, "trunk")
        x = m.sb("x", [P, N_TILES, D])
        lng, lnb = m.sb("lng", [P, D]), m.sb("lnb", [P, D])
        stats = m.sb("stats", [P, N_TILES, 2, 6])
        mv = m.sb("mv", [P, N_TILES, 2])
        rstd = m.sb("rstd", [P, N_TILES])
        nmr = m.sb("nmr", [P, N_TILES])
        scaled = m.sb("scaled", [P, 2, D])
        eps = m.sb("eps", [P, 1])
        ones_sq = m.sb("ones_sq", [P, P])
        rows = m.sb("rows", [GROUPS, 5, P])
        ldt = m.sb("ldt", [GROUPS, 1])
        crow = m.sb("crow", [P, KH, P])
        crow_sw = m.sb("crow_sw", [P, KH, P])
        par = m.sb("par", [P, 5, GROUPS])
        t = m.sb("t", [P, 12, GROUPS])
        ang = m.sb("ang", [P, 2, GROUPS])
        tb = m.sb("tb", [P, 2, GROUPS, GC])
        bs = m.sb("bs", [P, GROUPS, GC])
        bsw = m.sb("bsw", [P, GROUPS, GC])
        sq = m.sb("sq", [P, 3, GROUPS])
        pst = m.ps("pst", [P, 4, 4, P])
        pso = m.ps("pso", [P, 2, 512])
        s_x = [m.sem(f"x{i}") for i in range(N_TILES)]
        s_ln, s_par, s_b, s_c = m.sem("ln"), m.sem("par"), m.sem("b"), m.sem("c")
        s_const, s_pool = m.sem("const"), m.sem("pool")
        s_stat, s_std, s_rstd = m.sem("stat"), m.sem("std"), m.sem("rstd")
        s_norm, s_gain, s_h, s_tr, s_ev = m.sem("norm"), m.sem("gain"), m.sem("h"), m.sem("tr"), m.sem("ev")
        s_scaled, s_hp = m.sem("scaled"), [m.sem("hp0"), m.sem("hp1")]
        s_rows, s_part, s_parc, s_crd = m.sem("rows"), m.sem("part"), m.sem("parc"), m.sem("crd")
        s_dt, s_arg, s_mag, s_ang, s_sin, s_bsw = (m.sem(n) for n in ("dt", "arg", "mag", "ang", "sin", "bsw"))
        s_v, s_g = m.sem("v"), m.sem("g")
        block = ctx.enter_context(nc.Block())

        def dup(dst, src, order):
            return [(dst[:, 64 * h:64 * h + 64], src[w]) for h, w in enumerate(order)]

        @block.sync
        def _(sp):
            h0 = (io.state_ssm_re[0, 0], io.state_ssm_im[0, 0])
            lr = (io.lam_re[0],) * 2
            li = (io.lam_im[0],) * 2
            for k, (src, order) in enumerate((
                    (lr, (0, 1)), (li, (0, 1)), (h0, (0, 1)), (h0, (1, 0)))):
                slot = (0, 1, 3, 4)[k]
                for dst, s in dup(rows[:, slot, :], src, order):
                    sp.dma_start(dst, s).then_inc(s_par, 16)
            with nc.allow_non_contiguous_dma(reason="a column of step sizes"):
                sp.dma_start(ldt[:, :], io.log_dt.rearrange("a g -> g a")).then_inc(s_par, 16)
            for i in range(N_TILES - 1):
                sp.dma_start(x[:, i, :], io.x_prompt[0, i * P:(i + 1) * P, :]).then_inc(s_x[i], 16)
            sp.dma_start(x[0:LAST_ROWS, N_TILES - 1, :], io.x_sample[0]).then_inc(s_x[N_TILES - 1], 16)
            for i in range(N_TILES):
                sp.wait_ge(s_scaled, i + 1)
                sp.dma_start(io.resid[i * P:(i + 1) * P, :], scaled[:, i % 2, :]).then_inc(s_hp[i % 2], 16)
            for k in range(2):
                sp.wait_ge(s_hp[k], 16 * len(range(k, N_TILES, 2)))

        @block.scalar
        def _(act):
            act.dma_start(bs[0:64, :, :], io.ssm_b_re[0].rearrange("g p c -> p g c")).then_inc(s_b, 16)
            act.dma_start(bs[64:128, :, :], io.ssm_b_im[0].rearrange("g p c -> p g c")).then_inc(s_b, 16)
            act.dma_start(lng[:, :], io.ln_in_g.partition_broadcast(P)).then_inc(s_ln, 16)
            act.dma_start(lnb[:, :], io.ln_in_b.partition_broadcast(P)).then_inc(s_ln, 16)
            c_re = io.ssm_c_re[0].rearrange("(m g) c p -> (g c) m p", m=KH)
            c_im = io.ssm_c_im[0].rearrange("(m g) c p -> (g c) m p", m=KH)
            act.dma_start(crow[:, :, 0:64], c_re).then_inc(s_c, 16)
            act.dma_start(crow[:, :, 64:128], c_im).then_inc(s_c, 16)
            act.dma_start(crow_sw[:, :, 0:64], c_im).then_inc(s_c, 16)
            act.dma_start(crow_sw[:, :, 64:128], c_re).then_inc(s_c, 16)
            act.wait_ge(s_parc, 1)
            act.activation(t[:, 0, :], par[:, 2, :], ACT.Exp).then_inc(s_dt, 1)
            act.wait_ge(s_arg, 1)
            act.activation(t[:, 2, :], t[:, 1, :], ACT.Exp).then_inc(s_mag, 1)
            act.wait_ge(s_ang, 1)
            act.activation(t[:, 4:6, :], ang[:, :, :], ACT.Sin).then_inc(s_sin, 1)
            act.wait_ge(s_stat, 1)
            act.wait_ge(s_const, 1)
            act.activation(rstd[:, :], mv[:, :, 1], ACT.Sqrt, bias=eps[:, 0:1]).then_inc(s_std, 1)
            act.wait_ge(s_rstd, 1)
            for i in range(N_TILES):
                act.activation(x[:, i, :], x[:, i, :], ACT.Identity, bias=nmr[:, i:i + 1],
                               scale=rstd[:, i:i + 1]).then_inc(s_norm, 1)
            for i in range(N_TILES):
                act.wait_ge(s_h, i + 1)
                if i >= 2:
                    act.wait_ge(s_hp[i % 2], 16 * (i // 2))
                act.mul(scaled[:, i % 2, :], x[:, i, :], ALPHA).then_inc(s_scaled, 1)
                for half in range(2):
                    n = 2 * i + half
                    act.wait_ge(s_tr, n + 1)
                    w = P if i < N_TILES - 1 else LAST_ROWS
                    act.activation(keep.hT[:, 4 * half:4 * half + 4, i * P:i * P + w],
                                   pst[:, n % 4, :, 0:w], ACT.Copy).then_inc(s_ev, 1)

        @block.gpsimd
        def _(pool):
            link = chain(pool, s_pool)
            link(pool.memset(x[64:128, N_TILES - 1, :], 0.0))
            link(pool.memset(ones_sq[:, :], 1.0))
            link(pool.affine_select(out=keep.ident[:, :], in_=ones_sq[:, :], compare_op=ALU.is_equal, fill=0.0,
                                    base=0, pattern=[[-1, P]], channel_multiplier=1))
            link(pool.memset(eps[:, :], LN_EPS))
            link(pool.memset(co.sign[64:128, :], -1.0))
            pool.memset(co.sign[0:64, :], 1.0).then_inc(s_const, 1)
            pool.wait_ge(s_const, 1)
            for i in range(N_TILES):
                pool.wait_ge(s_gain, i + 1)
                if i == 0:
                    pool.wait_ge(s_ln, 32)
                pool.tensor_tensor(x[:, i, :], x[:, i, :], lnb[:, :], ALU.add).then_inc(s_h, 1)

        @block.tensor
        def _(pe):
            pe.wait_ge(s_const, 1)
            pe.wait_ge(s_rows, 1)
            for k in range(5):
                tr = pe.transpose(pso[:, 0, k * GROUPS:(k + 1) * GROUPS], rows[:, k, :],
                                  keep.ident[0:GROUPS, 0:GROUPS])
            tr.then_inc(s_part, 1)
            pe.wait_ge(s_c, 64)
            for v, src in enumerate((crow, crow_sw)):
                if v:
                    pe.wait_ge(s_crd, 1)
                for k in range(KH):
                    tr = pe.transpose(pso[:, 1, k * P:(k + 1) * P], src[:, k, :], keep.ident[:, :])
                tr.then_inc(s_part, 1)
            for i in range(N_TILES):
                pe.wait_ge(s_h, i + 1)
                for half in range(2):
                    n = 2 * i + half
                    if n >= 4:
                        pe.wait_ge(s_ev, n - 3)
                    for k in range(4):
                        c = (4 * half + k) * P
                        tr = pe.transpose(pst[:, n % 4, k, :], x[:, i, c:c + P], keep.ident[:, :])
                    tr.then_inc(s_tr, 1)

        @block.vector
        def _(v):
            link = chain(v, s_v)
            tt, ts, stt = v.tensor_tensor, v.tensor_scalar, v.scalar_tensor_tensor

            def cmul(outr, outi, ar, ai, br, bi, tmp):
                tt(tmp[0], ar, br, ALU.mult)
                tt(tmp[1], ai, bi, ALU.mult)
                tt(tmp[2], ar, bi, ALU.mult)
                link(tt(tmp[3], ai, br, ALU.mult))
                tt(outr, tmp[0], tmp[1], ALU.subtract)
                link(tt(outi, tmp[2], tmp[3], ALU.add))

            v.wait_ge(s_par, 16 * 9)
            link(v.tensor_copy(rows[:, 2, :], ldt[:, 0:1].to_broadcast([GROUPS, P])))
            v.sem_inc(s_rows, 1)
            v.wait_ge(s_part, 1)
            v.tensor_copy(par[:, :, :], pso[:, 0, 0:5 * GROUPS].rearrange("p (a g) -> p a g", a=5)).then_inc(s_parc, 1)
            v.wait_ge(s_parc, 1)
            lr, li, h0, h0sw = (par[:, k, :] for k in (0, 1, 3, 4))
            v.wait_ge(s_dt, 1)
            tt(t[:, 1, :], lr, t[:, 0, :], ALU.mult).then_inc(s_arg, 1)
            link(tt(t[:, 3, :], li, t[:, 0, :], ALU.mult))
            th = t[:, 3, :]
            for k in range(2):
                n = t[:, 6 + k, :]
                link(ts(n, th, float(1 / (2 * np.pi)), 0.25 * k, ALU.mult, ALU.add))
                link(ts(n, n, ROUND, None, ALU.add))
                link(ts(n, n, ROUND, None, ALU.subtract))
                link(stt(out=ang[:, k, :], in0=n, scalar=-TWO_PI_HI, in1=th, op0=ALU.mult, op1=ALU.add))
                link(stt(out=ang[:, k, :], in0=n, scalar=-TWO_PI_MID, in1=ang[:, k, :], op0=ALU.mult, op1=ALU.add))
                link(stt(out=ang[:, k, :], in0=n, scalar=-TWO_PI_LO, in1=ang[:, k, :], op0=ALU.mult, op1=ALU.add))
                if k:
                    link(ts(ang[:, k, :], ang[:, k, :], float(np.pi / 2), None, ALU.add))
                link(ts(ang[:, k, :], ang[:, k, :], PI_BELOW, -PI_BELOW, ALU.min, ALU.max))
            v.sem_inc(s_ang, 1)
            v.wait_ge(s_sin, 1)
            v.wait_ge(s_mag, 1)
            sin, cos, mag = t[:, 4, :], t[:, 5, :], t[:, 2, :]
            tmp = [t[:, k, :] for k in (8, 9, 10, 11)]

            def unit(c, s):
                tt(tmp[0], c, c, ALU.mult)
                link(tt(tmp[1], s, s, ALU.mult))
                link(tt(tmp[2], tmp[0], tmp[1], ALU.add))
                link(ts(tmp[2], tmp[2], -0.5, 1.5, ALU.mult, ALU.add))
                tt(c, c, tmp[2], ALU.mult)
                link(tt(s, s, tmp[2], ALU.mult))

            unit(cos, sin)
            pr, pi = co.pr, co.pi
            v.memset(pr[:, :, 0], 1.0)
            v.memset(pi[:, :, 0], 0.0)
            tt(pr[:, :, 1], mag, cos, ALU.mult)
            link(tt(pi[:, :, 1], mag, sin, ALU.mult))
            cmul(pr[:, :, 2], pi[:, :, 2], pr[:, :, 1], pi[:, :, 1], pr[:, :, 1], pi[:, :, 1], tmp)
            for lo in (1, 2):
                cmul(pr[:, :, 2 + lo], pi[:, :, 2 + lo], pr[:, :, lo], pi[:, :, lo], pr[:, :, 2], pi[:, :, 2], tmp)
            for lo in (1, 2, 3, 4):
                cmul(pr[:, :, 4 + lo], pi[:, :, 4 + lo], pr[:, :, lo], pi[:, :, lo], pr[:, :, 4], pi[:, :, 4], tmp)
            den, ar1 = t[:, 6, :], t[:, 7, :]
            ai = pi[:, :, 1]
            tt(tmp[0], lr, lr, ALU.mult)
            link(tt(tmp[1], li, li, ALU.mult))
            link(tt(den, tmp[0], tmp[1], ALU.add))
            v.reciprocal(den, den)
            link(ts(ar1, pr[:, :, 1], -1.0, None, ALU.add))
            tt(tmp[0], ar1, lr, ALU.mult)
            tt(tmp[1], ai, li, ALU.mult)
            tt(tmp[2], ai, lr, ALU.mult)
            link(tt(tmp[3], ar1, li, ALU.mult))
            tt(tmp[0], tmp[0], tmp[1], ALU.add)
            link(tt(tmp[2], tmp[3], tmp[2], ALU.subtract))
            qr, nqi = t[:, 0, :], t[:, 1, :]
            tt(qr, tmp[0], den, ALU.mult)
            link(tt(nqi, tmp[2], den, ALU.mult))
            v.wait_ge(s_const, 1)
            sg = co.sign[:, 0:1]
            link(ts(nqi, nqi, sg, None, ALU.mult))
            tt(co.nsi[:, :, :], pi[:, :, :], sg.unsqueeze(2).to_broadcast([P, GROUPS, 9]), ALU.mult)
            tt(co.prs[:, :, :], pr[:, :, :], sg.unsqueeze(2).to_broadcast([P, GROUPS, 9]), ALU.mult)
            link(ts(co.npi[:, :, :], pi[:, :, :], -1.0, None, ALU.mult))
            v.wait_ge(s_b, 32)
            v.tensor_copy(bsw[0:64, :, :], bs[64:128, :, :])
            link(v.tensor_copy(bsw[64:128, :, :], bs[0:64, :, :]))
            qrb, nqb = bc(qr, 2, GC), bc(nqi, 2, GC)
            tt(tb[:, 0], bs[:, :, :], qrb, ALU.mult)
            link(tt(tb[:, 1], bsw[:, :, :], nqb, ALU.mult))
            link(tt(co.bb[:, :, :], tb[:, 0], tb[:, 1], ALU.add))
            tt(tb[:, 0], bsw[:, :, :], qrb, ALU.mult)
            link(tt(tb[:, 1], bs[:, :, :], nqb, ALU.mult))
            link(tt(co.bbsw[:, :, :], tb[:, 0], tb[:, 1], ALU.subtract))
            tt(tmp[0], h0, pr[:, :, 8], ALU.mult)
            link(tt(tmp[1], h0sw, co.nsi[:, :, 8], ALU.mult))
            v.tensor_copy(co.h0[:, :], h0)
            link(tt(co.ah0[:, :], tmp[0], tmp[1], ALU.subtract))
            er, ei, mg = sq[:, 0, :], sq[:, 1, :], sq[:, 2, :]
            v.tensor_copy(er, cos)
            v.tensor_copy(mg, mag)
            link(v.tensor_copy(ei, sin))
            for k in range(3):
                tt(mg, mg, mg, ALU.mult)
                cmul(er, ei, er, ei, er, ei, tmp)
                unit(er, ei)
            v.tensor_copy(co.decay[:, :], mg)
            for lvl in range(7):
                v.tensor_copy(co.er[:, :, lvl], er)
                link(ts(co.eis[:, :, lvl], ei, sg, None, ALU.mult))
                if lvl < 6:
                    cmul(er, ei, er, ei, er, ei, tmp)
                    unit(er, ei)
            for k, dst in enumerate((co.cs, co.csw)):
                v.wait_ge(s_part, 2 + k)
                v.tensor_copy(dst[:, :], pso[:, 1, :]).then_inc(s_crd, 1)
            v.wait_ge(s_const, 1)
            for i in range(N_TILES):
                v.wait_ge(s_x[i], 16)
                for h in range(2):
                    st = v.bn_stats(stats[:, i, h, :], x[:, i, h * 512:(h + 1) * 512])
            link(st)
            for i in range(N_TILES):
                ag = v.bn_aggr(mv[:, i, :], stats[:, i, :, :])
            ag.then_inc(s_stat, 1)
            v.wait_ge(s_std, 1)
            link(v.reciprocal(rstd[:, :], rstd[:, :]))
            stt(out=nmr[:, :], in0=mv[:, :, 0], scalar=-1.0, in1=rstd[:, :], op0=ALU.mult,
                op1=ALU.mult).then_inc(s_rstd, 1)
            v.wait_ge(s_ln, 32)
            for i in range(N_TILES):
                v.wait_ge(s_norm, i + 1)
                tt(x[:, i, :], x[:, i, :], lng[:, :], ALU.mult).then_inc(s_gain, 1)


def mixing_stage(nc, io, keep, co):
    with ExitStack() as ctx:
        m = Pools(nc, ctx, "mix")
        RING = 3
        hT = keep.hT
        gT, ycT = keep.gT[:, :, 0:N_TOK], keep.ycT[:, :, 0:N_TOK]
        win = m.sb("win", [P, RING, KD, P])
        v_sb = m.sb("v", [P, N_TOK])
        gb = m.sb("gb", [P, N_TOK])
        cv = m.sb("cv", [P, N_TOK + 4])
        SAMPLE = N_PROMPT + 2
        cacheT = m.sb("cacheT", [P, KH, 2])
        taps = m.sb("taps", [P, KH, 3])
        u = m.sb("u", [P, GT, NK])
        bt = m.sb("bt", [P, GT, P])
        btsw = m.sb("btsw", [P, GT, P])
        bp = m.sb("bp", [P, GT, P])
        c1 = m.sb("c1", [P, GT, (T + 1) * GC])
        c2 = m.sb("c2", [P, GT, T * GC])
        toep = m.sb("toep", [P, GT, P])
        kf = m.sb("kf", [GC, GT, 2 * T, GC])
        dd = m.sb("dd", [GC, GROUPS, GC])
        t1, t2 = m.sb("t1", [P, GT * (T + 1) * GC]), m.sb("t2", [P, GT * (T + 1) * GC])
        cos, sin, dec = (m.sb(n, [P, GT, NK]) for n in ("cos", "sin", "dec"))
        q1, q2 = m.sb("q1", [P, GT * NKP // 2]), m.sb("q2", [P, GT * NKP // 2])
        w, g = m.sb("w", [P, GT, NK]), m.sb("g", [P, GT, NK])
        hc, hs = m.sb("hc", [P, GT, NK]), m.sb("hs", [P, GT, NK])
        y = m.sb("y", [P, GT, NK])
        fin = m.sb("fin", [P, 2, 2, GROUPS])
        swap = m.sb("swap", [P, P])
        fo = m.sb("fo", [GROUPS, 2, P])
        proj = m.ps("proj", [P, 3, 512])
        sb = m.ps("ssm", [P, 4, 512])
        misc = m.ps("misc", [P, 512])

        s_w = [m.sem(f"w{i}") for i in range(RING)]
        s_small, s_const = m.sem("small"), m.sem("const")
        s_proj, s_pact, s_pdve = m.sem("proj"), m.sem("pact"), m.sem("pdve")
        s_uout = [m.sem(f"uout{c}") for c in range(KH)]
        s_uin, s_yout, s_yin = m.sem("uin"), m.sem("yout"), m.sem("yin")
        s_bp, s_bpt, s_bt, s_c, s_k, s_kev, s_kdma, s_toep = (
            m.sem(n) for n in ("bp", "bpt", "bt", "c", "k", "kev", "kdma", "toep"))
        s_tab, s_bu, s_app, s_hch, s_y, s_yev = (m.sem(n) for n in ("tab", "bu", "app", "hch", "y", "yev"))
        s_rot, s_gel = m.sem("rot"), m.sem("gel")
        s_cv, s_gbr, s_conv = m.sem("cv"), m.sem("gbr"), m.sem("conv")
        s_cvout, s_fin, s_finp, s_finc, s_out = m.sem("cvout"), m.sem("fin"), m.sem("finp"), m.sem("finc"), m.sem("out")
        s_v, s_g, s_cvr = m.sem("vch"), m.sem("gch"), m.sem("cvr")
        block = ctx.enter_context(nc.Block())

        order = [("u", 0), ("u", 1), ("S", 0), ("u", 2), ("Y", 0), ("S", 1), ("u", 3), ("v", 0), ("Y", 1), ("S", 2),
                 ("gc", 0), ("gb", 0), ("v", 1), ("Y", 2), ("S", 3), ("gc", 1), ("gb", 1), ("v", 2), ("Y", 3),
                 ("gc", 2), ("gb", 2), ("v", 3), ("gc", 3), ("gb", 3)]
        column = {"u": 0, "gb": KH, "gc": 2 * KH, "v": 3 * KH}
        tiles = [o for o in order if o[0] in column]
        emptied, act_n, dve_n = [], 0, 0
        for kind, _ in tiles:
            for _ in TOK_CHUNKS:
                if kind == "gc":
                    dve_n += 1
                    emptied.append((s_pdve, dve_n))
                else:
                    act_n += 1
                    emptied.append((s_pact, act_n))
        first = {o: 3 * i for i, o in enumerate(tiles)}
        pact_after = {o: emptied[first[o] + 2][1] for o in tiles}

        @block.sync
        def _(sp):
            def weight(i):
                kind, c = tiles[i]
                if i >= RING:
                    sp.wait_ge(s_proj, 3 * (i - RING) + 3)
                col = (column[kind] + c) * P
                sp.dma_start(win[:, i % RING, :, :],
                             io.w_in[0].rearrange("(k p) n -> p k n", p=P)[:, :, col:col + P]).then_inc(s_w[i % RING], 16)

            sent = [0]

            def weights(n):
                while sent[0] < min(n, len(tiles)):
                    weight(sent[0])
                    sent[0] += 1
            weights(3)
            with nc.allow_non_contiguous_dma(reason="per-channel rows"):
                sp.dma_start(cacheT[:, :, 0], io.cache_conv[0, 0, 0].rearrange("(c p) -> p c", p=P)).then_inc(s_small, 16)
                sp.dma_start(cacheT[:, :, 1], io.cache_conv[0, 0, 1].rearrange("(c p) -> p c", p=P)).then_inc(s_small, 16)
                for k in range(3):
                    sp.dma_start(taps[:, :, k], io.conv_w[0, k].rearrange("(c p) -> p c", p=P)).then_inc(s_small, 16)
            sp.dma_start(dd[:, :, :], io.ssm_d[0].rearrange("(g c) -> g c", c=GC).partition_broadcast(GC)).then_inc(s_small, 16)
            done = 0
            for kind, c in order:
                if kind in column:
                    done += 1
                if kind == "u":
                    sp.wait_ge(s_pact, pact_after[("u", c)])
                    sp.dma_start(io.ud[c * P:(c + 1) * P, :], gT[:, c, :]).then_inc(s_uout[c], 16)
                if kind == "S":
                    sp.wait_ge(s_uout[c], 16)
                    if c:
                        sp.wait_ge(s_y, 3 * c)
                    ud = io.ud[c * P:(c + 1) * P, :].rearrange("(g c) (s k) -> s c g k", g=GT, s=T)
                    for s in range(T):
                        sp.dma_start(u[GC * s:GC * (s + 1), :, :], ud[s]).then_inc(s_uin, 16)
                    sp.wait_ge(s_kdma, c + 1)
                    for s in range(T):
                        sp.dma_start(toep[GC * s:GC * (s + 1), :, :].rearrange("p g (t c) -> p g t c", c=GC),
                                     kf[:, :, T - s:2 * T - s, :]).then_inc(s_toep, 16)
                if kind == "Y":
                    sp.wait_ge(s_yev, 3 * (c + 1))
                    yd = io.yd[c * P:(c + 1) * P, :].rearrange("(g c) (t k) -> t c g k", g=GT, t=T)
                    for s in range(T):
                        sp.dma_start(yd[s], y[GC * s:GC * (s + 1), :, :]).then_inc(s_yout, 16)
                    sp.wait_ge(s_yout, 16 * T * (c + 1))
                    sp.dma_start(gT[:, c, :], io.yd[c * P:(c + 1) * P, :]).then_inc(s_yin, 16)
                weights(done + 3)
            n_out = 0
            sp.wait_ge(s_finc, 2)
            for k, (re, im) in enumerate(((io.out_ssm_re_p, io.out_ssm_im_p), (io.out_ssm_re_s, io.out_ssm_im_s))):
                sp.dma_start(re[0, 0], fo[:, k, 0:STATE]).then_inc(s_out, 16)
                sp.dma_start(im[0, 0], fo[:, k, STATE:P]).then_inc(s_out, 16)
                n_out += 2
            sp.wait_ge(s_out, 16 * n_out)
            sp.wait_ge(s_cvout, 16 * 4 * KH)
            sp.wait_ge(s_yin, 16 * KH)

        @block.scalar
        def _(act):
            n = 0
            for kind, c in order:
                if kind in ("u", "v", "gb"):
                    for (lo, ln) in TOK_CHUNKS:
                        i = first[(kind, c)] + TOK_CHUNKS.index((lo, ln))
                        act.wait_ge(s_proj, i + 1)
                        src = proj[:, i % 3, 0:ln]
                        if kind == "u":
                            dst = gT[:, c, :].rearrange("p (s k) -> p k s", s=T)[:, lo // T:(lo + ln) // T, :]
                            src = src.rearrange("p (k s) -> p k s", s=T)
                        elif kind == "v":
                            dst = v_sb[:, lo:lo + ln]
                            if c and lo == 0:
                                act.wait_ge(s_cv, c)
                        else:
                            dst = gb[:, lo:lo + ln]
                            if c and lo == 0:
                                act.wait_ge(s_conv, c)
                        act.activation(dst, src, ACT.Copy).then_inc(s_pact, 1)
                if kind == "S":
                    if c:
                        act.wait_ge(s_bu, 3 * c)
                    for h in range(2):
                        act.wait_ge(s_bpt, 2 * c + h + 1)
                        src = sb[:, h, :].rearrange("p (g q) -> p g q", g=4)
                        act.activation(bt[:, 4 * h:4 * h + 4, :], src, ACT.Copy).then_inc(s_bt, 1)
                        act.activation(btsw[:, 4 * h:4 * h + 4, 0:64], src[:, :, 64:128], ACT.Copy).then_inc(s_bt, 1)
                        act.activation(btsw[:, 4 * h:4 * h + 4, 64:128], src[:, :, 0:64], ACT.Copy).then_inc(s_bt, 1)
                if kind == "Y":
                    if c:
                        act.wait_ge(s_yout, 16 * T * c)
                    for j, (g0, gn) in enumerate(TRIPLES):
                        act.wait_ge(s_y, 3 * c + j + 1)
                        act.activation(y[:, g0:g0 + gn, :], sb[:, j, 0:gn * NK].rearrange("p (g k) -> p g k", g=gn),
                                       ACT.Copy).then_inc(s_yev, 1)

        @block.gpsimd
        def _(pool):
            link = chain(pool, s_g)
            link(pool.memset(kf[:, :, :, :], 0.0))
            link(pool.memset(cv[:, 0:2], 0.0))
            link(pool.memset(hc[:, :, 0:1], 0.0))
            link(pool.memset(hs[:, :, 0:1], 0.0))
            link(pool.memset(hs[:, :, NKP:NKP + 1], 0.0))
            link(pool.memset(swap[:, :], 0.0))
            link(pool.affine_select(out=swap[:, :], in_=swap[:, :], compare_op=ALU.not_equal, fill=-1.0,
                                    base=-64, pattern=[[-1, P]], channel_multiplier=1))
            link(pool.affine_select(out=swap[:, :], in_=swap[:, :], compare_op=ALU.not_equal, fill=1.0,
                                    base=64, pattern=[[-1, P]], channel_multiplier=1))
            pool.wait_ge(s_small, 16 * 6)
            pool.tensor_tensor(dd[:, :, :], dd[:, :, :], bc(keep.ident[0:GC, 0:GC], 1, GROUPS),
                               ALU.mult).then_inc(s_const, 1)
            pool.wait_ge(s_const, 1)
            for c in range(KH):
                gs = slice(GT * c, GT * (c + 1))
                if c:
                    pool.wait_ge(s_app, c)
                link(pool.memset(cos[:, :, 0:1], 1.0))
                link(pool.memset(sin[:, :, 0:1], 0.0))
                for lvl in range(7):
                    n = 1 << lvl
                    er, ei = bc(co.er[:, gs, lvl], 2, n), bc(co.eis[:, gs, lvl], 2, n)
                    a, b = (t[:, 0:GT * n].rearrange("p (g k) -> p g k", g=GT) for t in (q1, q2))
                    link(pool.tensor_tensor(a, cos[:, :, 0:n], er, ALU.mult))
                    link(pool.tensor_tensor(b, sin[:, :, 0:n], ei, ALU.mult))
                    link(pool.tensor_tensor(cos[:, :, n:2 * n], a, b, ALU.subtract))
                    link(pool.tensor_tensor(a, sin[:, :, 0:n], er, ALU.mult))
                    link(pool.tensor_tensor(b, cos[:, :, 0:n], ei, ALU.mult))
                    link(pool.tensor_tensor(sin[:, :, n:2 * n], a, b, ALU.add))
                link(pool.tensor_copy(cos[:, :, NKP:NK], cos[:, :, 0:NK - NKP]))
                link(pool.tensor_copy(sin[:, :, NKP:NK], sin[:, :, 0:NK - NKP]))
                link(pool.tensor_copy(dec[:, :, :], bc(co.decay[:, gs], 2, NK)))
                link(pool.memset(dec[:, :, 0:1], 0.0))
                pool.memset(dec[:, :, NKP:NKP + 1], 0.0).then_inc(s_tab, 1)
                pool.wait_ge(s_tab, c + 1)
            with nc.allow_non_contiguous_dma(reason="a few columns"):
                for c in range(KH):
                    pool.wait_ge(s_cv, c + 1)
                    for dst, col in ((io.out_conv_p, N_PROMPT), (io.out_conv_s, N_TOK + 2)):
                        for k in range(2):
                            pool.dma_start(dst[0, 0, k, c * P:(c + 1) * P].rearrange("(p a) -> p a", a=1),
                                           cv[:, col + k:col + k + 1]).then_inc(s_cvout, 16)

        @block.tensor
        def _(pe):
            pn = 0
            for kind, c in order:
                if kind in column:
                    i = tiles.index((kind, c))
                    pe.wait_ge(s_w[i % RING], 16 * (i // RING + 1))
                    for lo, ln in TOK_CHUNKS:
                        if pn >= 3:
                            pe.wait_ge(*emptied[pn - 3])
                        for k in range(KD):
                            mm = pe.matmul(proj[:, pn % 3, 0:ln], win[:, i % RING, k, :], hT[:, k, lo:lo + ln],
                                           start=(k == 0), stop=(k == KD - 1))
                        mm.then_inc(s_proj, 1)
                        pn += 1
                if kind == "S":
                    pe.wait_ge(s_bp, c + 1)
                    if c:
                        pe.wait_ge(s_yev, 3 * c)
                    for h in range(2):
                        for q in range(4):
                            tr = pe.transpose(sb[:, h, q * P:(q + 1) * P], bp[:, 4 * h + q, :], keep.ident[:, :])
                        tr.then_inc(s_bpt, 1)
                    pe.wait_ge(s_c, c + 1)
                    for h in range(2):
                        for q in range(4):
                            gi = 4 * h + q
                            mm = pe.matmul(sb[0:GC, 2 + h, q * P:(q + 1) * P], co.bb[:, GT * c + gi, :],
                                           c1[:, gi, 0:T * GC], start=True, stop=True)
                    mm.then_inc(s_k, 1)
                    pe.wait_ge(s_bt, 6 * (c + 1))
                    pe.wait_ge(s_kev, c + 1)
                    pe.wait_ge(s_uin, 16 * T * (c + 1))
                    for j, (g0, gn) in enumerate(TRIPLES):
                        a, b = (0, 1) if j % 2 == 0 else (2, 3)
                        if j == 2:
                            pe.wait_ge(s_hch, 3 * c + 1)
                        for q in range(gn):
                            pe.matmul(sb[:, a, q * NK:(q + 1) * NK], bt[:, g0 + q, :], u[:, g0 + q, :],
                                      start=True, stop=True)
                        for q in range(gn):
                            mm = pe.matmul(sb[:, b, q * NK:(q + 1) * NK], btsw[:, g0 + q, :], u[:, g0 + q, :],
                                           start=True, stop=True)
                        mm.then_inc(s_bu, 1)
                if kind == "Y":
                    pe.wait_ge(s_toep, 16 * T * (c + 1))
                    pe.wait_ge(s_rot, c + 1)
                    for j, (g0, gn) in enumerate(TRIPLES):
                        for q in range(gn):
                            o, gi = sb[:, j, q * NK:(q + 1) * NK], g0 + q
                            pe.matmul(o, toep[:, gi, :], u[:, gi, :], start=True, stop=False)
                            pe.matmul(o, c1[:, gi, GC:(T + 1) * GC], hc[:, gi, :], start=False, stop=False)
                            mm = pe.matmul(o, c2[:, gi, :], hs[:, gi, :], start=False, stop=True)
                        mm.then_inc(s_y, 1)
            pe.wait_ge(s_fin, KH)
            for k in range(2):
                pe.matmul(misc[0:GROUPS, k * P:(k + 1) * P], fin[:, k, 0, :], keep.ident[:, :], start=True, stop=False)
                mm = pe.matmul(misc[0:GROUPS, k * P:(k + 1) * P], fin[:, k, 1, :], swap[:, :], start=False, stop=True)
            mm.then_inc(s_finp, 1)

        @block.vector
        def _(v):
            link = chain(v, s_v)
            tt, ts, stt = v.tensor_tensor, v.tensor_scalar, v.scalar_tensor_tensor
            v.wait_ge(s_small, 16 * 6)

            def coefficients(c):
                gs = slice(GT * c, GT * (c + 1))
                a = t1[:, 0:GT * T * GC].rearrange("p (g s c) -> p g s c", g=GT, s=T)
                b = t2[:, 0:GT * T * GC].rearrange("p (g s c) -> p g s c", g=GT, s=T)

                def shaped(x, n):
                    return x[:, 0:GT * n * GC].rearrange("p (g s c) -> p g s c", g=GT, s=n)

                if c:
                    v.wait_ge(s_bpt, 2 * c)
                tt(a, bc(co.bb[:, gs, :], 2, T), bc(co.pr[:, gs, 0:T][:, :, ::-1], 3, GC), ALU.mult)
                link(tt(b, bc(co.bbsw[:, gs, :], 2, T), bc(co.nsi[:, gs, 0:T][:, :, ::-1], 3, GC), ALU.mult))
                link(tt(bp[:, :, :].rearrange("p g (s c) -> p g s c", c=GC), a, b, ALU.subtract), s_bp)
                if c:
                    v.wait_ge(s_y, 3 * c)
                cs = co.cs[:, P * c:P * (c + 1)].rearrange("p (g c) -> p g c", c=GC)
                csw = co.csw[:, P * c:P * (c + 1)].rearrange("p (g c) -> p g c", c=GC)
                a9, b9 = shaped(t1, T + 1), shaped(t2, T + 1)
                link(tt(a9, bc(cs, 2, T + 1), bc(co.prs[:, gs, :], 3, GC), ALU.mult))
                link(tt(b9, bc(csw, 2, T + 1), bc(co.npi[:, gs, :], 3, GC), ALU.mult))
                link(tt(c1[:, :, :].rearrange("p g (s c) -> p g s c", c=GC), a9, b9, ALU.add))
                tt(a, bc(cs, 2, T), bc(co.npi[:, gs, 1:], 3, GC), ALU.mult)
                link(tt(b, bc(csw, 2, T), bc(co.prs[:, gs, 1:], 3, GC), ALU.mult))
                link(tt(c2[:, :, :].rearrange("p g (s c) -> p g s c", c=GC), a, b, ALU.subtract), s_c)
                v.wait_ge(s_k, c + 1)
                v.wait_ge(s_const, 1)
                if c:
                    v.wait_ge(s_toep, 16 * T * c)
                for h in range(2):
                    cp = v.tensor_copy(kf[:, 4 * h:4 * h + 4, T:2 * T, :],
                                       sb[0:GC, 2 + h, :].rearrange("p (g s c) -> p g s c", g=4, s=T))
                cp.then_inc(s_kev, 1)
                v.wait_ge(s_kev, c + 1)
                tt(kf[:, :, T, :], kf[:, :, T, :], dd[:, gs, :], ALU.add).then_inc(s_kdma, 1)

            def scan(c):
                gs = slice(GT * c, GT * (c + 1))
                v.wait_ge(s_tab, c + 1)
                for j, (g0, gn) in enumerate(TRIPLES):
                    a, b = (0, 1) if j % 2 == 0 else (2, 3)
                    v.wait_ge(s_bu, 3 * c + j + 1)
                    x1 = t1[:, g0 * NK:(g0 + gn) * NK].rearrange("p (g k) -> p g k", g=gn)
                    x2 = t2[:, g0 * NK:(g0 + gn) * NK].rearrange("p (g k) -> p g k", g=gn)
                    pa = sb[:, a, 0:gn * NK].rearrange("p (g k) -> p g k", g=gn)
                    pb = sb[:, b, 0:gn * NK].rearrange("p (g k) -> p g k", g=gn)
                    tt(x1, pa, cos[:, g0:g0 + gn, :], ALU.mult)
                    link(tt(x2, pb, sin[:, g0:g0 + gn, :], ALU.mult), s_hch)
                flat = [x[:, 0:GT * NK].rearrange("p (g k) -> p g k", g=GT) for x in (t1, t2)]
                link(tt(w[:, :, :], flat[0], flat[1], ALU.add))
                link(tt(w[:, :, NKP], w[:, :, NKP], co.ah0[:, gs], ALU.add))
                link(v.tensor_tensor_scan(g[:, :, :].rearrange("p g k -> p (g k)"),
                                          dec[:, :, :].rearrange("p g k -> p (g k)"),
                                          w[:, :, :].rearrange("p g k -> p (g k)"), 0.0, ALU.mult, ALU.add))
                if c == 0:
                    v.wait_ge(s_const, 1)
                for dst, tab in ((hc, cos), (hs, sin)):
                    tt(dst[:, :, 1:NKP], g[:, :, 0:NKP - 1], tab[:, :, 0:NKP - 1], ALU.mult)
                    tt(dst[:, :, NKP + 1:NK], g[:, :, NKP:NK - 1], tab[:, :, NKP:NK - 1], ALU.mult)
                for k, last in enumerate((NKP - 1, NK - 1)):
                    tt(fin[:, k, 0, gs], g[:, :, last], cos[:, :, last], ALU.mult)
                    f = tt(fin[:, k, 1, gs], g[:, :, last], sin[:, :, last], ALU.mult)
                link(f, s_app)
                link(v.tensor_copy(hc[:, :, NKP], co.h0[:, gs]), s_rot)
                for k in range(2):
                    f = ts(fin[:, k, 1, gs], fin[:, k, 1, gs], co.sign[:, 0:1], None, ALU.mult)
                link(f, s_fin)

            def gate(c):
                for j, (lo, ln) in enumerate(TOK_CHUNKS):
                    i = first[("gc", c)] + j
                    v.wait_ge(s_proj, i + 1)
                    if j == 0:
                        v.wait_ge(s_pact, pact_after[("v", c)])
                        if c:
                            v.wait_ge(s_cvout, 16 * 4 * c)
                    for a, b, shift in ((lo, min(lo + ln, N_PROMPT), 2), (max(lo, N_PROMPT), lo + ln, 4)):
                        if a < b:
                            mu = tt(cv[:, a + shift:b + shift], proj[:, i % 3, a - lo:b - lo], v_sb[:, a:b], ALU.mult)
                    link(mu, s_pdve)
                link(v.tensor_copy(cv[:, SAMPLE:SAMPLE + 2], cacheT[:, c, :]), s_cv)

            def conv(c):
                v.wait_ge(s_const, 1)
                x = t1[:, 0:N_TOK + 2]
                n = N_TOK + 2
                link(ts(x, cv[:, 0:n], taps[:, c, 0:1], None, ALU.mult))
                link(stt(out=x, in0=cv[:, 1:n + 1], scalar=taps[:, c, 1:2], in1=x, op0=ALU.mult, op1=ALU.add))
                link(stt(out=x, in0=cv[:, 2:n + 2], scalar=taps[:, c, 2:3], in1=x, op0=ALU.mult, op1=ALU.add))
                v.wait_ge(s_pact, pact_after[("gb", c)])
                tt(ycT[:, c, 0:N_PROMPT], t1[:, 0:N_PROMPT], gb[:, 0:N_PROMPT], ALU.mult)
                link(tt(ycT[:, c, N_PROMPT:N_TOK], t1[:, SAMPLE:SAMPLE + N_SAMPLE], gb[:, N_PROMPT:N_TOK],
                        ALU.mult), s_conv)

            for kind, c in order:
                if kind == "S":
                    coefficients(c)
                    scan(c)
                if kind == "gc":
                    gate(c)
                if kind == "gb":
                    conv(c)
            v.wait_ge(s_finp, 1)
            v.tensor_copy(fo[:, :, :].rearrange("p a b -> p (a b)"), misc[0:GROUPS, 0:2 * P]).then_inc(s_finc, 2)


def output_stage(nc, io, keep):
    with ExitStack() as ctx:
        m = Pools(nc, ctx, "out")
        w = Names()
        w.out_h, w.out_l = m.sb("wo_h", [P, KD, D], F32R), m.sb("wo_l", [P, KD, D], F32R)
        w.in_h, w.in_l = m.sb("wi_h", [P, KD, 2 * D_EXP], F32R), m.sb("wi_l", [P, KD, 2 * D_EXP], F32R)
        w.dn_h, w.dn_l = m.sb("wd_h", [P, 2, D], F32R), m.sb("wd_l", [P, 2, D], F32R)
        w.rt_h, w.rt_l = m.sb("wr_h", [P, KD, N_EXP], F32R), m.sb("wr_l", [P, KD, N_EXP], F32R)
        w.eps = m.sb("eps", [P, 2])
        w.rr = m.sb("rr", [P, N_TILES, 2])
        gate_stage(nc, io, keep, w)
        project_stage(nc, io, keep, w)


def gate_stage(nc, io, keep, w):
    with ExitStack() as ctx:
        m = Pools(nc, ctx, "glu")
        gT, ycT = keep.gT, keep.ycT
        gn = m.sb("gn", [P, KH, N_TOK])
        w_glu = m.sb("w_glu", [P, KH, D_HALF])
        bglu = m.sb("bglu", [P, KH])
        beta = m.sb("beta", [P, KD])
        sig = m.sb("sig", [P, 2, CW])
        sq = m.sb("sq", [P, 2, CW])
        sqt = keep.scores[:, :, :].rearrange("p t e -> p (t e)")
        raw = m.sb("raw", [P, 3, D])
        ssq = m.sb("ssq", [P, 2, ROWS])
        ones = m.sb("ones", [P, 1])
        pl = m.ps("pl", [P, 4, 512])
        pm = m.ps("pm", [P, 512])
        s_wg, s_small = m.sem("wg"), m.sem("small")
        s_raw = [m.sem(f"raw{k}") for k in range(3)]
        s_const, s_g, s_v = m.sem("const"), m.sem("gch"), m.sem("vch")
        s_gelu, s_glu, s_sig, s_mix, s_sq, s_added = (m.sem(n) for n in ("gelu", "glu", "sig", "mix", "sq", "added"))
        s_ysq, s_ss, s_rt, s_high = (m.sem(n) for n in ("ysq", "ss", "rt", "high"))
        s_low_dve, s_low_pool = m.sem("lowv"), m.sem("lowp")
        block = ctx.enter_context(nc.Block())
        glu = [(ch, mo) for ch in range(len(TOK_CHUNKS)) for mo in range(KH)]

        def added(n):
            return (KH - 1) * (n // KH) + n % KH

        PIECES = [("out", k) for k in range(KD)] + [("rt", 0)] + [("in", k) for k in range(KD // 2)] + [("dn", 0), ("dn", 1)]
        AFTER = [range(0), range(0, 1), range(1, 2), range(2, 4), range(4, 5), range(5, 7), range(7, 8), range(8, 10),
                 range(10, 11), range(11, 12), range(12, 14), range(14, 15)]

        def place(j):
            kind, k = PIECES[j]
            at = raw[:, j % 3, :]
            if kind == "out":
                return at, w.out_h[:, k, :], w.out_l[:, k, :]
            if kind == "dn":
                return at, w.dn_h[:, k, :], w.dn_l[:, k, :]
            if kind == "in":
                pair = slice(2 * k, 2 * k + 2)
                return at.rearrange("p (k n) -> p k n", k=2), w.in_h[:, pair, :], w.in_l[:, pair, :]
            return (at[:, 0:KD * N_EXP].rearrange("p (k n) -> p k n", k=KD), w.rt_h[:, :, :], w.rt_l[:, :, :])

        def loads(j):
            return sum(2 if PIECES[i][0] == "in" else 1 for i in range(j % 3, j + 1, 3))

        @block.sync
        def _(sp):
            sp.dma_start(w_glu[:, :, :], io.w_glu[0].rearrange("(k p) n -> p k n", p=P)).then_inc(s_wg, 16)
            with nc.allow_non_contiguous_dma(reason="per-channel rows"):
                sp.dma_start(bglu[:, :], io.b_glu[0].rearrange("(c p) -> p c", p=P)).then_inc(s_small, 16)
                sp.dma_start(beta[:, 0:KH], io.beta_ssm[0].rearrange("(c p) -> p c", p=P)).then_inc(s_small, 16)
                sp.dma_start(beta[:, KH:KD], io.beta_conv[0].rearrange("(c p) -> p c", p=P)).then_inc(s_small, 16)
            sources = {"out": io.w_out, "dn": io.ws_down}
            for j, (kind, k) in enumerate(PIECES):
                if j >= 3:
                    if PIECES[j - 3][0] == "out":
                        sp.wait_ge(s_low_dve, j - 2)
                    else:
                        sp.wait_ge(s_low_pool, j - 2 - KD)
                at = place(j)[0]
                if kind == "in":
                    for half, src in enumerate((io.ws_gate, io.ws_up)):
                        src = src[0].rearrange("(k p) n -> p k n", p=P)[:, 2 * k:2 * k + 2, :]
                        sp.dma_start(at[:, :, D_EXP * half:D_EXP * (half + 1)], src).then_inc(s_raw[j % 3], 16)
                elif kind == "rt":
                    sp.dma_start(at, io.w_router[0].rearrange("(k p) n -> p k n", p=P)).then_inc(s_raw[j % 3], 16)
                else:
                    sp.dma_start(at, sources[kind][0, k * P:(k + 1) * P, :]).then_inc(s_raw[j % 3], 16)

        @block.scalar
        def _(act):
            act.wait_ge(s_const, 1)
            for c in range(KH):
                act.activation(gn[:, c, :].rearrange("p (k s) -> p s k", s=T),
                               gT[:, c, 0:N_TOK].rearrange("p (s k) -> p s k", s=T),
                               ACT.Gelu_apprx_tanh).then_inc(s_gelu, 1)
            act.wait_ge(s_small, 48)

            def square(n):
                ch, mo = glu[n]
                lo, ln = TOK_CHUNKS[ch]
                act.wait_ge(s_mix, n + 1)
                if n >= 3:
                    act.wait_ge(s_added, added(n - 2))
                dst = ssq[:, 0, lo:lo + ln] if mo == 0 else sq[:, n % 2, 0:ln]
                act.activation(dst, gT[:, mo, lo:lo + ln], ACT.Square).then_inc(s_sq, 1)

            def high(j):
                at, hi, _ = place(j)
                act.wait_ge(s_raw[j % 3], 16 * loads(j))
                scale = beta[:, j:j + 1] if PIECES[j][0] == "out" else 1.0
                act.activation(hi, at, ACT.Copy, scale=scale).then_inc(s_high, 1)

            for n, (ch, mo) in enumerate(glu):
                lo, ln = TOK_CHUNKS[ch]
                act.wait_ge(s_glu, n + 1)
                if n >= 2:
                    act.wait_ge(s_mix, n - 1)
                act.activation(sig[:, n % 2, 0:ln], pl[:, n % 4, 0:ln], ACT.Sigmoid,
                               bias=bglu[:, mo:mo + 1]).then_inc(s_sig, 1)
                if n:
                    square(n - 1)
                for j in AFTER[n]:
                    high(j)
            square(len(glu) - 1)
            act.wait_ge(s_ss, 1)
            act.activation(w.rr[:, :, :].rearrange("p a b -> p (a b)"), pm[:, 0:2 * N_TILES], ACT.Sqrt,
                           bias=w.eps[:, 0:1], scale=1.0 / D_HALF).then_inc(s_rt, 1)

        @block.gpsimd
        def _(pool):
            link = chain(pool, s_g)
            link(pool.memset(gT[:, :, N_TOK:], 0.0))
            link(pool.memset(ycT[:, :, N_TOK:], 0.0))
            link(pool.memset(ssq[:, :, N_TOK:], 0.0))
            link(pool.memset(ones[:, :], 1.0))
            link(pool.memset(w.eps[:, 0:1], RMS_EPS))
            pool.memset(w.eps[:, 1:2], LN_EPS).then_inc(s_const, 1)
            for lo, ln in TOK_CHUNKS:
                total = ssq[:, 1, lo:lo + ln]
                for c in range(KH):
                    y = ycT[:, c, lo:lo + ln]
                    link(pool.tensor_tensor(sqt[:, 0:ln] if c else total, y, y, ALU.mult))
                    if c:
                        link(pool.tensor_tensor(total, total, sqt[:, 0:ln], ALU.add))
            pool.sem_inc(s_ysq, 1)
            for j in range(KD, len(PIECES)):
                at, hi, lo = place(j)
                pool.wait_ge(s_high, j + 1)
                pool.tensor_tensor(lo, at, hi.bitcast(F32), ALU.subtract).then_inc(s_low_pool, 1)

        @block.tensor
        def _(pe):
            def squares(part, tiles):
                for i in tiles:
                    mm = pe.matmul(pm[:, 2 * i + part:2 * i + part + 1], ssq[:, part, i * P:(i + 1) * P], ones[:, :],
                                   start=True, stop=True)
                return mm

            pe.wait_ge(s_wg, 16)
            pe.wait_ge(s_gelu, KH)
            per = CW // P
            for n, (ch, mo) in enumerate(glu):
                lo, ln = TOK_CHUNKS[ch]
                if n >= 4:
                    pe.wait_ge(s_sig, n - 3)
                for k in range(KH):
                    mm = pe.matmul(pl[:, n % 4, 0:ln], w_glu[:, k, mo * P:(mo + 1) * P],
                                   gn[:, k, lo:lo + ln], start=(k == 0), stop=(k == KH - 1))
                mm.then_inc(s_glu, 1)
                if n == 2 * KH + 1:
                    pe.wait_ge(s_ysq, 1)
                    squares(1, range(N_TILES))
                if mo == 2 and ch:
                    pe.wait_ge(s_added, added(KH * ch - 1))
                    squares(0, range(per * (ch - 1), per * ch))
            pe.wait_ge(s_added, added(len(glu) - 1))
            squares(0, range(per * 2, N_TILES)).then_inc(s_ss, 1)

        @block.vector
        def _(v):
            link = chain(v, s_v)
            tt, stt = v.tensor_tensor, v.scalar_tensor_tensor
            v.wait_ge(s_const, 1)
            v.wait_ge(s_gelu, KH)

            def add_square(n):
                ch, mo = glu[n]
                lo, ln = TOK_CHUNKS[ch]
                v.wait_ge(s_sq, n + 1)
                if mo:
                    if n >= 2:
                        v.wait_ge(s_added, added(n - 1))
                    tt(ssq[:, 0, lo:lo + ln], ssq[:, 0, lo:lo + ln], sq[:, n % 2, 0:ln], ALU.add).then_inc(s_added, 1)

            def low(j):
                at, hi, lo = place(j)
                v.wait_ge(s_high, j + 1)
                stt(out=lo, in0=at, scalar=beta[:, j:j + 1], in1=hi.bitcast(F32), op0=ALU.mult,
                    op1=ALU.subtract).then_inc(s_low_dve, 1)

            for n, (ch, mo) in enumerate(glu):
                lo, ln = TOK_CHUNKS[ch]
                v.wait_ge(s_sig, n + 1)
                tt(gT[:, mo, lo:lo + ln], gn[:, mo, lo:lo + ln], sig[:, n % 2, 0:ln], ALU.mult).then_inc(s_mix, 1)
                if n:
                    add_square(n - 1)
                    for j in AFTER[n - 1]:
                        if j < KD:
                            low(j)
            add_square(len(glu) - 1)
            v.wait_ge(s_rt, 1)
            link(v.reciprocal(w.rr[:, :, :], w.rr[:, :, :]))


def project_stage(nc, io, keep, w):
    with ExitStack() as ctx:
        m = Pools(nc, ctx, "proj")
        gT, ycT = keep.gT, keep.ycT
        lng, lnb = m.sb("lng", [P, D]), m.sb("lnb", [P, D])
        in_h, in_l = m.sb("in_h", [P, 2, KD, P], F32R), m.sb("in_l", [P, 2, KD, P], F32R)
        res = m.sb("res", [P, D])
        x = m.sb("x", [P, 3, D])
        x_h, x_l = m.sb("x_h", [P, KD, P], F32R), m.sb("x_l", [P, KD, P], F32R)
        stats = m.sb("stats", [P, 2, 6])
        mv = m.sb("mv", [P, 2])
        rs = m.sb("rs", [P, 2])
        sg = m.sb("sg", [P, D_EXP])
        hid = m.sb("hid", [P, D_EXP])
        hid_h, hid_l = m.sb("hid_h", [P, 2, P], F32R), m.sb("hid_l", [P, 2, P], F32R)
        po = m.ps("po", [P, 2, 2, 512])
        pt = m.ps("pt", [P, 2, 512])
        pg = m.ps("pg", [P, 512])
        pm = m.ps("pm", [P, 512])
        s_ln, s_v = m.sem("ln"), m.sem("vch")
        s_res, s_tok, s_acc = m.sem("res"), [m.sem(f"tok{k}") for k in range(3)], [
            m.sem(f"acc{k}") for k in range(3)]
        s_inh, s_inl, s_po, s_z, s_zd, s_std, s_rstd, s_nm, s_gain, s_x = (
            m.sem(n) for n in ("inh", "inl", "po", "z", "zd", "std", "rstd", "nm", "gain", "x"))
        s_tr, s_xh, s_xl, s_rl, s_lg, s_pg, s_silu, s_hid, s_ht, s_hh, s_hl, s_pd, s_ao = (
            m.sem(n) for n in ("tr", "xh", "xl", "rl", "lg", "pg", "silu", "hid", "ht", "hh", "hl", "pd", "ao"))
        block = ctx.enter_context(nc.Block())
        steps = range(N_TILES + 2)

        @block.sync
        def _(sp):
            sp.dma_start(res[:, :], io.resid[0:P, :]).then_inc(s_res, 16)
            sp.dma_start(lng[:, :], io.ln1_g[0].partition_broadcast(P)).then_inc(s_ln, 16)
            sp.dma_start(lnb[:, :], io.ln1_b[0].partition_broadcast(P)).then_inc(s_ln, 16)
            for i in range(1, N_TILES):
                sp.wait_ge(s_z, 2 * i)
                sp.dma_start(res[:, :], io.resid[i * P:(i + 1) * P, :]).then_inc(s_res, 16)

        @block.scalar
        def _(act):
            def in_high(i):
                if i >= 2:
                    act.wait_ge(s_po, 2 * (i - 1))
                for part, src in enumerate((gT, ycT)):
                    act.activation(in_h[:, i % 2, KH * part:KH * (part + 1), :], src[:, :, i * P:(i + 1) * P],
                                   ACT.Copy).then_inc(s_inh, 1)

            def hid_high(i):
                act.wait_ge(s_ht, i + 1)
                if i:
                    act.wait_ge(s_pd, 2 * i)
                act.activation(hid_h[:, :, :], pm[:, 128:384].rearrange("p (k t) -> p k t", k=2),
                               ACT.Copy).then_inc(s_hh, 1)

            def x_high(i):
                if i:
                    act.wait_ge(s_pg, i)
                for h in range(2):
                    act.wait_ge(s_tr, 2 * i + h + 1)
                    act.activation(x_h[:, 4 * h:4 * h + 4, :], pt[:, h, :].rearrange("p (k t) -> p k t", k=4),
                                   ACT.Copy).then_inc(s_xh, 1)

            def normalise(i):
                act.wait_ge(s_zd, i + 1)
                act.activation(rs[:, 0:1], mv[:, 1:2], ACT.Sqrt, bias=w.eps[:, 1:2]).then_inc(s_std, 1)
                act.wait_ge(s_rstd, i + 1)
                act.activation(x[:, i % 3, :], x[:, i % 3, :], ACT.Identity, bias=rs[:, 1:2],
                               scale=rs[:, 0:1]).then_inc(s_nm, 1)

            def silu(i):
                act.wait_ge(s_rl, i + 1)
                act.activation(keep.scores[:, i, :], pm[:, 0:N_EXP], ACT.Copy).then_inc(s_lg, 1)
                act.wait_ge(s_pg, i + 1)
                if i:
                    act.wait_ge(s_hid, i)
                act.activation(sg[:, :], pg[:, 0:D_EXP], ACT.Silu).then_inc(s_silu, 1)

            in_high(0)
            for i in steps:
                if i + 1 < N_TILES:
                    in_high(i + 1)
                if i >= 2:
                    hid_high(i - 2)
                if 1 <= i <= N_TILES:
                    x_high(i - 1)
                if i < N_TILES:
                    normalise(i)
                if 1 <= i <= N_TILES:
                    silu(i - 1)

        @block.gpsimd
        def _(pool):
            pool.wait_ge(s_ln, 32)
            for i in steps:
                if i < N_TILES:
                    pool.wait_ge(s_gain, i + 1)
                    pool.tensor_tensor(x[:, i % 3, :], x[:, i % 3, :], lnb[:, :], ALU.add).then_inc(s_x, 1)
                    pool.wait_ge(s_x, i + 1)
                    pool.dma_start(io.tok[i * P:(i + 1) * P, :], x[:, i % 3, :]).then_inc(s_tok[i % 3], 16)
                if i >= 2:
                    j = i - 2
                    pool.wait_ge(s_ao, 2 * j + 2)
                    pool.dma_start(io.acc[j * P:(j + 1) * P, :], x[:, j % 3, :]).then_inc(s_acc[j % 3], 16)
            for k in range(3):
                pool.wait_ge(s_tok[k], 16 * len(range(k, N_TILES, 3)))
                pool.wait_ge(s_acc[k], 16 * len(range(k, N_TILES, 3)))

        @block.tensor
        def _(pe):
            def split_product(out, a, b, free):
                (ah, al), (bh, bl) = a, b
                terms = [(s[:, k, :], t[:, k, free]) for k in range(ah.shape[1])
                         for s, t in ((ah, bh), (ah, bl), (al, bh))]
                for i, (s, t) in enumerate(terms):
                    mm = pe.matmul(out, s, t, start=(i == 0), stop=(i == len(terms) - 1))
                return mm

            def project(i, h):
                n = 2 * i + h
                pe.wait_ge(s_inl, i + 1)
                if n >= 2:
                    pe.wait_ge(s_z, n - 1)
                for part in range(2):
                    ks = slice(KH * part, KH * (part + 1))
                    mm = split_product(po[:, n % 2, part, :], (in_h[:, i % 2, ks, :], in_l[:, i % 2, ks, :]),
                                       (w.out_h[:, ks, :], w.out_l[:, ks, :]), slice(512 * h, 512 * (h + 1)))
                mm.then_inc(s_po, 1)

            def turn_hid(i):
                pe.wait_ge(s_hid, i + 1)
                if i:
                    pe.wait_ge(s_hl, i)
                for k in range(2):
                    tr = pe.transpose(pm[:, 128 + k * P:128 + (k + 1) * P], hid[:, k * P:(k + 1) * P], keep.ident[:, :])
                tr.then_inc(s_ht, 1)

            def turn_x(i):
                pe.wait_ge(s_x, i + 1)
                for h in range(2):
                    if i >= 2:
                        pe.wait_ge(s_ao, 2 * (i - 2) + h + 1)
                    for k in range(4):
                        tr = pe.transpose(pt[:, h, k * P:(k + 1) * P], x[:, i % 3, (4 * h + k) * P:(4 * h + k + 1) * P],
                                          keep.ident[:, :])
                    tr.then_inc(s_tr, 1)

            def down(i):
                pe.wait_ge(s_hl, i + 1)
                if i + 1 < N_TILES:
                    pe.wait_ge(s_xl, i + 2)
                else:
                    pe.wait_ge(s_ao, 2 * i)
                for h in range(2):
                    split_product(pt[:, h, :], (hid_h, hid_l), (w.dn_h, w.dn_l),
                                  slice(512 * h, 512 * (h + 1))).then_inc(s_pd, 1)

            def enter(i):
                pe.wait_ge(s_xl, i + 1)
                if i:
                    pe.wait_ge(s_lg, i)
                    pe.wait_ge(s_hid, i)
                split_product(pm[:, 0:N_EXP], (x_h, x_l), (w.rt_h, w.rt_l), slice(0, N_EXP)).then_inc(s_rl, 1)
                split_product(pg[:, :], (x_h, x_l), (w.in_h, w.in_l), slice(0, 2 * D_EXP)).then_inc(s_pg, 1)

            for i in steps:
                if i < N_TILES:
                    project(i, 0)
                if i >= 2:
                    turn_hid(i - 2)
                if 1 <= i <= N_TILES:
                    turn_x(i - 1)
                if i < N_TILES:
                    project(i, 1)
                if i >= 2:
                    down(i - 2)
                if 1 <= i <= N_TILES:
                    enter(i - 1)

        @block.vector
        def _(v):
            link = chain(v, s_v)
            tt, stt = v.tensor_tensor, v.scalar_tensor_tensor

            def in_low(i):
                for part, src in enumerate((gT, ycT)):
                    ks = slice(KH * part, KH * (part + 1))
                    v.wait_ge(s_inh, 2 * i + part + 1)
                    low = tt(in_l[:, i % 2, ks, :], src[:, :, i * P:(i + 1) * P], in_h[:, i % 2, ks, :].bitcast(F32),
                             ALU.subtract)
                low.then_inc(s_inl, 1)

            def total(i, h):
                n = 2 * i + h
                cols = slice(512 * h, 512 * (h + 1))
                if h == 0:
                    v.wait_ge(s_res, 16 * (i + 1))
                    if i >= 3:
                        v.wait_ge(s_acc[i % 3], 16 * (i // 3))
                v.wait_ge(s_po, n + 1)
                z = x[:, i % 3, cols]
                link(stt(out=z, in0=po[:, n % 2, 0, :], scalar=w.rr[:, i, 0:1], in1=res[:, cols],
                         op0=ALU.mult, op1=ALU.add))
                link(stt(out=z, in0=po[:, n % 2, 1, :], scalar=w.rr[:, i, 1:2], in1=z, op0=ALU.mult, op1=ALU.add), s_z)
                link(v.bn_stats(stats[:, h, :], z))

            def norm(i):
                link(v.bn_aggr(mv[:, :], stats[:, :, :]), s_zd)
                v.wait_ge(s_std, i + 1)
                link(v.reciprocal(rs[:, 0:1], rs[:, 0:1]))
                link(stt(out=rs[:, 1:2], in0=mv[:, 0:1], scalar=-1.0, in1=rs[:, 0:1], op0=ALU.mult, op1=ALU.mult),
                     s_rstd)
                v.wait_ge(s_nm, i + 1)
                if i == 0:
                    v.wait_ge(s_ln, 32)
                tt(x[:, i % 3, :], x[:, i % 3, :], lng[:, :], ALU.mult).then_inc(s_gain, 1)

            def hid_low(i):
                v.wait_ge(s_hh, i + 1)
                tt(hid_l[:, :, :], pm[:, 128:384].rearrange("p (k t) -> p k t", k=2), hid_h[:, :, :].bitcast(F32),
                   ALU.subtract).then_inc(s_hl, 1)

            def x_low(i):
                for h in range(2):
                    v.wait_ge(s_xh, 2 * i + h + 1)
                    low = tt(x_l[:, 4 * h:4 * h + 4, :], pt[:, h, :].rearrange("p (k t) -> p k t", k=4),
                             x_h[:, 4 * h:4 * h + 4, :].bitcast(F32), ALU.subtract)
                low.then_inc(s_xl, 1)

            def hidden(i):
                v.wait_ge(s_silu, i + 1)
                if i:
                    v.wait_ge(s_ht, i)
                tt(hid[:, :], sg[:, :], pg[:, D_EXP:], ALU.mult).then_inc(s_hid, 1)

            def add_shared(i):
                v.wait_ge(s_tok[i % 3], 16 * (i // 3 + 1))
                for h in range(2):
                    cols = slice(512 * h, 512 * (h + 1))
                    v.wait_ge(s_pd, 2 * i + h + 1)
                    stt(out=x[:, i % 3, cols], in0=x[:, i % 3, cols], scalar=ALPHA, in1=pt[:, h, :], op0=ALU.mult,
                        op1=ALU.add).then_inc(s_ao, 1)

            in_low(0)
            for i in steps:
                if i < N_TILES:
                    total(i, 0)
                if i >= 2:
                    hid_low(i - 2)
                if 1 <= i <= N_TILES:
                    x_low(i - 1)
                if i + 1 < N_TILES:
                    in_low(i + 1)
                if i < N_TILES:
                    total(i, 1)
                    norm(i)
                if i >= 2:
                    add_shared(i - 2)
                if 1 <= i <= N_TILES:
                    hidden(i - 1)


def routing_stage(nc, io, keep, rt):
    with ExitStack() as ctx:
        m = Pools(nc, ctx, "route")
        NT, NE, NG = N_TILES, N_EXP, N_EGRP
        bias = m.sb("bias", [P, NE])
        sc = m.sb("sc", [P, NT, NE])
        sel = m.sb("sel", [P, NT, NE])
        g8 = m.sb("g8", [P, NT, NG, 8])
        gs = m.sb("gs", [P, NT, NG])
        gt, ge = m.sb("gt", [P, NT, NG, NG]), m.sb("ge", [P, NT, NG, NG])
        lower = m.sb("lower", [P, NG, NG])
        gm = m.sb("gm", [P, NT, NG])
        pen = m.sb("pen", [P, NT, NG])
        t8 = m.sb("t8", [P, NT, 8])
        i8 = m.sb("i8", [P, NT, 8], mybir.dt.uint32)
        f8 = m.sb("f8", [P, NT, 8])
        iota_e = m.sb("iota_e", [P, NE])
        hot = m.sb("hot", [P, NT, NE, TOP_K])
        mask = m.sb("mask", [P, NT, NE])
        mask_b = m.sb("mask_b", [P, NT, NE], BF16)
        wsum = m.sb("wsum", [P, NT])
        wt = m.sb("wt", [P, NT, NE])
        rest = m.sb("rest", [P, NT, NE])
        upper = m.sb("upper", [P, P], BF16)
        ones_b = m.sb("ones_b", [P, P], BF16)
        carry = m.sb("carry", [P, NT + 1, NE])
        pos = m.sb("pos", [P, NT, NE])
        nblk, ends, cmp = m.sb("nblk", [P, NE]), m.sb("ends", [P, NE]), m.sb("cmp", [P, NE])
        one_e = m.sb("one_e", [P, NE])
        row = m.sb("row", [P, 1])
        eo, jo, over, tmp1 = (m.sb(n, [P, 1]) for n in ("eo", "jo", "over", "tmp1"))
        evens = m.sb("evens", [1, 64])
        tabf = m.sb("tabf", [1, 4, P])
        odds = m.sb("odds", [1, NE // 2])
        isodd = m.sb("isodd", [1, P, NE // 2])
        slot_i = m.sb("slot_i", [P, P * SLOT_SETS], I32)
        ps = m.ps("ps", [P, 4, 512])
        pt = m.ps("pt", [P, 512])
        s_bias, s_const, s_g, s_v = m.sem("bias"), m.sem("const"), m.sem("gch"), m.sem("vch")
        s_sig, s_mask, s_pos, s_eo, s_t, s_split, s_lg = (m.sem(n) for n in ("sig", "mask", "pos", "eo", "t", "split", "lg"))
        block = ctx.enter_context(nc.Block())
        HALVES = [(0, 5), (5, 4)]

        @block.sync
        def _(sp):
            sp.dma_start(bias[:, :], io.router_bias[0].partition_broadcast(P)).then_inc(s_bias, 16)

        @block.scalar
        def _(act):
            act.activation(sc[:, :, :], keep.scores[:, :, :], ACT.Sigmoid).then_inc(s_sig, 1)

        @block.gpsimd
        def _(pool):
            link = chain(pool, s_g)
            link(pool.memset(lower[:, :, :], 1.0))
            link(pool.affine_select(out=lower[:, :, :], in_=lower[:, :, :], compare_op=ALU.is_gt, fill=0.0, base=0,
                                    pattern=[[1, NG], [-1, NG]], channel_multiplier=0))
            link(pool.iota(slot_i[:, :], pattern=[[1, P * SLOT_SETS]], base=0, channel_multiplier=0))
            link(pool.tensor_copy(rt.slot[:, :], slot_i[:, :]))
            link(pool.tensor_copy(iota_e[:, :], rt.slot[:, 0:NE]))
            link(pool.iota(slot_i[:, 0:1], pattern=[[1, 1]], base=0, channel_multiplier=1))
            link(pool.tensor_copy(row[:, :], slot_i[:, 0:1]))
            link(pool.tensor_scalar(rt.dummy[:, :], row[:, :], float(ROWS), None, ALU.add))
            link(pool.memset(one_e[:, :], 1.0))
            link(pool.tensor_scalar(evens[:, :], rt.slot[0:1, 0:64], 2.0, 1.5, ALU.mult, ALU.add))
            for tile in range(NT):
                link(pool.memset(rt.vals[:, 0, tile, 1:2], float(tile)))
            link(pool.tensor_copy(rt.vals[:, 0, :, 0:1], row[:, 0:1].unsqueeze(1).to_broadcast([P, NT, 1])))
            link(pool.memset(rt.vals[:, 0, :, 2:3], 1.0))
            link(pool.tensor_copy(rt.vals[:, 1, :, 0:3], rt.vals[:, 0, :, 0:3]))
            link(pool.memset(ones_b[:, :], 1.0))
            link(pool.affine_select(out=upper[:, :], in_=ones_b[:, :], compare_op=ALU.is_gt, fill=0.0, base=0,
                                    pattern=[[1, P]], channel_multiplier=-1))
            pool.memset(rt.tab[:, :, :], 0).then_inc(s_const, 1)

        @block.tensor
        def _(pe):
            pe.wait_ge(s_mask, 1)
            for k, (lo, n) in enumerate(HALVES):
                pe.matmul(ps[:, k, 0:n * NE], upper[:, :], mask_b[:, lo:lo + n, :].rearrange("p a b -> p (a b)"),
                          start=True, stop=True)
                mm = pe.matmul(ps[:, 2 + k, 0:n * NE], ones_b[:, :],
                               mask_b[:, lo:lo + n, :].rearrange("p a b -> p (a b)"), start=True, stop=True)
            mm.then_inc(s_pos, 1)
            pe.wait_ge(s_eo, 1)
            pe.transpose(pt[0:1, 0:P], eo[:, 0:1], keep.ident[:, :])
            pe.transpose(pt[0:1, P:2 * P], jo[:, 0:1], keep.ident[:, :]).then_inc(s_t, 1)

        @block.vector
        def _(v):
            link = chain(v, s_v)
            tt, ts, stt = v.tensor_tensor, v.tensor_scalar, v.scalar_tensor_tensor
            v.wait_ge(s_bias, 16)
            v.wait_ge(s_sig, 1)
            v.wait_ge(s_const, 1)
            link(tt(sel[:, :, :], sc[:, :, :], bc(bias[:, :], 1, NT), ALU.add))
            per = NE // NG
            for i in range(NT):
                for g in range(NG):
                    mx = v.max(g8[:, i, g, :], sel[:, i, per * g:per * (g + 1)])
            link(mx)
            link(tt(gs[:, :, :], g8[:, :, :, 0], g8[:, :, :, 1], ALU.add))
            other, own = bc(gs[:, :, :], 2, NG), bc(gs[:, :, :], 3, NG)
            tt(gt[:, :, :, :], other, own, ALU.is_gt)
            link(tt(ge[:, :, :, :], other, own, ALU.is_equal))
            for i in range(NT):
                lo = tt(ge[:, i, :, :], ge[:, i, :, :], lower[:, :, :], ALU.mult)
            link(lo)
            link(tt(gt[:, :, :, :], gt[:, :, :, :], ge[:, :, :, :], ALU.add))
            link(v.reduce_sum(gm[:, :, :], gt[:, :, :, :], axis=mybir.AxisListType.X))
            link(ts(gm[:, :, :], gm[:, :, :], TOP_GROUPS - 0.5, None, ALU.is_lt))
            link(ts(pen[:, :, :], gm[:, :, :], 1e30, -1e30, ALU.mult, ALU.add))
            sel4 = sel[:, :, :].rearrange("p t (g e) -> p (t g) e", g=NG)
            gmf, penf = (bc(a[:, :, :].rearrange("p t g -> p (t g)"), 2, per) for a in (gm, pen))
            link(tt(sel4, sel4, gmf, ALU.mult))
            link(tt(sel4, sel4, penf, ALU.add))
            for i in range(NT):
                mx = v.max(t8[:, i, :], sel[:, i, :])
            link(mx)
            for i in range(NT):
                mx = v.max_index(i8[:, i, :], t8[:, i, :], sel[:, i, :])
            link(mx)
            link(v.tensor_copy(f8[:, :, :], i8[:, :, :]))
            for i in range(NT):
                eq = tt(hot[:, i, :, :], bc(f8[:, i, 0:TOP_K], 1, NE), bc(iota_e[:, :], 2, TOP_K), ALU.is_equal)
            link(eq)
            link(v.reduce_sum(mask[:, :, :], hot[:, :, :, :], axis=mybir.AxisListType.X))
            link(v.memset(mask[LAST_ROWS:P, NT - 1, :], 0.0))
            link(v.tensor_copy(mask_b[:, :, :], mask[:, :, :]), s_mask)
            link(tt(wt[:, :, :], sc[:, :, :], mask[:, :, :], ALU.mult))
            link(v.reduce_sum(wsum[:, :], wt[:, :, :], axis=mybir.AxisListType.X))
            link(ts(wsum[:, :], wsum[:, :], 1e-30, None, ALU.max))
            link(v.reciprocal(wsum[:, :], wsum[:, :]))
            link(tt(wt[:, :, :], wt[:, :, :], bc(wsum[:, :], 2, NE), ALU.mult))
            link(ts(wt[:, :, :], wt[:, :, :], ROUTED_SCALE, None, ALU.mult))
            src = wt
            for k in range(3):
                link(v.tensor_copy(rt.parts[:, :, :, k], src[:, :, :]))
                if k < 2:
                    link(tt(rest[:, :, :], src[:, :, :], rt.parts[:, :, :, k], ALU.subtract))
                    src = rest
            v.wait_ge(s_pos, 1)
            link(v.memset(carry[:, 0, :], 0.0))
            for i in range(NT):
                k, o = (0, i) if i < 5 else (1, i - 5)
                link(tt(carry[:, i + 1, :], carry[:, i, :], ps[:, 2 + k, o * NE:(o + 1) * NE], ALU.add))
            for k, (lo, n) in enumerate(HALVES):
                p = tt(pos[:, lo:lo + n, :], ps[:, k, 0:n * NE].rearrange("p (a b) -> p a b", a=n),
                       carry[:, lo:lo + n, :], ALU.add)
            link(p)
            link(ts(pos[:, :, :], pos[:, :, :], 1.0, None, ALU.add))
            link(tt(pos[:, :, :], pos[:, :, :], mask[:, :, :], ALU.mult))
            link(ts(rt.posm[:, :, :], pos[:, :, :], -1.0, None, ALU.add))
            cnt = carry[:, NT, :]
            link(v.memset(nblk[:, :], 1.0))
            for j in range(1, NT):
                link(ts(cmp[:, :], cnt, float(P * j) + 0.5, None, ALU.is_gt))
                link(tt(nblk[:, :], nblk[:, :], cmp[:, :], ALU.add))
            link(v.tensor_tensor_scan(ends[:, :], one_e[:, :], nblk[:, :], 0.0, ALU.mult, ALU.add))
            link(ts(cmp[:, :], ends[:, :], row[:, 0:1], None, ALU.is_le))
            link(v.reduce_sum(eo[:, :], cmp[:, :], axis=mybir.AxisListType.X))
            link(tt(cmp[:, :], cmp[:, :], nblk[:, :], ALU.mult))
            link(v.reduce_sum(tmp1[:, :], cmp[:, :], axis=mybir.AxisListType.X))
            link(tt(jo[:, :], row[:, :], tmp1[:, :], ALU.subtract))
            link(tt(over[:, :], row[:, :], ends[:, NE - 1:NE], ALU.is_ge))
            link(ts(eo[:, :], eo[:, :], float(NE - 1), None, ALU.min))
            link(ts(over[:, :], over[:, :], 1000.0, None, ALU.mult))
            link(tt(jo[:, :], jo[:, :], over[:, :], ALU.add))
            link(ts(jo[:, :], jo[:, :], float(SLOT_SETS - 1), None, ALU.min))
            link(ts(jo[:, :], jo[:, :], float(P), None, ALU.mult), s_eo)
            v.wait_ge(s_t, 1)
            for k in range(2):
                link(v.tensor_copy(tabf[0:1, k, 0:P], pt[0:1, k * P:(k + 1) * P]))
            odd = rt.slot[0:1, 0:NE // 2]
            link(ts(odds[:, :], odd, 2.0, 1.0, ALU.mult, ALU.add))
            link(tt(isodd[:, :, :], bc(tabf[0:1, 0, 0:P], 2, NE // 2), bc(odds[:, :], 1, P), ALU.is_equal))
            link(v.reduce_sum(tabf[0:1, 2, 0:P], isodd[:, :, :], axis=mybir.AxisListType.X))
            link(v.tensor_copy(tabf[0:1, 3, 0:NE], ends[0:1, :]))
            link(v.tensor_copy(rt.tab[0:1, 0:3, 0:P], tabf[:, 0:3, 0:P]))
            link(v.tensor_copy(rt.tab[0:1, 3, 0:NE], tabf[:, 3, 0:NE]))
            link(tt(evens[:, :], evens[:, :], ends[0:1, NE - 1:NE].to_broadcast([1, 64]), ALU.is_lt))
            link(v.reduce_sum(tmp1[0:1, :], evens[:, :], axis=mybir.AxisListType.X))
            link(ts(tmp1[0:1, :], tmp1[0:1, :], 2.0, None, ALU.mult))
            link(v.tensor_copy(rt.tab[0:1, 4, 0:1], tmp1[0:1, :]))


def expert_stage(nc, io, keep, rt):
    with ExitStack() as ctx:
        m = Pools(nc, ctx, "moe")
        raw_up = m.sb("raw_up", [P, 2, KD, 2 * D_EXP])
        raw_dn = m.sb("raw_dn", [P, 2, 2, D])
        up_h, up_l = m.sb("up_h", [P, 2, KD, 2 * D_EXP], F32R), m.sb("up_l", [P, 2, KD, 2 * D_EXP], F32R)
        dn_h, dn_l = m.sb("dn_h", [P, 2, 2, D], F32R), m.sb("dn_l", [P, 2, 2, D], F32R)
        pick = m.sb("pick", [P, 2, N_TILES, P], BF16)
        info = m.sb("info", [P, 8])
        tmp = m.sb("tmp", [P, 2])
        idx_g, idx_s = m.sb("idx_g", [P, 2], I32), m.sb("idx_s", [P, 2], I32)
        new, cur = m.sb("new", [P, 2, 2]), m.sb("cur", [P, 2, 2])
        xg = m.sb("xg", [P, 2, D])
        x_h, x_l = m.sb("x_h", [P, 2, KD, P], F32R), m.sb("x_l", [P, 2, KD, P], F32R)
        sg = m.sb("sg", [P, 2, D_EXP])
        hid = m.sb("hid", [P, 2, D_EXP])
        hid_h, hid_l = m.sb("hid_h", [P, 2, 2, P], F32R), m.sb("hid_l", [P, 2, 2, P], F32R)
        y = m.sb("y", [P, 2, D])
        p_gu = m.ps("p_gu", [P, 2, 512])
        p_dn = m.ps("p_dn", [P, 2, 512])
        p_tr = m.ps("p_tr", [P, 2, 512])
        p_ht = m.ps("p_ht", [P, 512])
        p_im = m.ps("p_im", [P, 512])
        up_done, down_done, x_turned, info_done, hid_turned = (m.sem(n) for n in ("gu", "dn", "tr", "im", "ht"))
        silu_done, xh_done, y_act, up_h_done, dn_h_done, hidh_done = (
            m.sem(n) for n in ("silu", "xh", "ya", "uph", "dnh", "hh"))
        pick_done, hid_done, xl_done, hidl_done, idx_done, y_dve, up_l_dve, dn_l_dve, s_v, s_cur = (
            m.sem(n) for n in ("pick", "hid", "xl", "hl", "ix", "yd", "upl", "dnl", "vch", "cur_s"))
        up_l_pool, dn_l_pool = m.sem("uplp"), m.sem("dnlp")
        gathered = [m.sem("ga0"), m.sem("ga1")]
        added = [m.sem("sc0"), m.sem("sc1")]
        gate_in, up_in, down_in = m.sem("wg"), m.sem("wu"), m.sem("wd")
        go, act_go, sp_go, zeroed = m.sem("go"), m.sem("act_go"), m.sem("sp_go"), m.sem("zeroed")
        block = ctx.enter_context(nc.Block())
        w_g = io.w_gate[0].rearrange("e (k p) n -> e p k n", p=P)
        w_u = io.w_up[0].rearrange("e (k p) n -> e p k n", p=P)
        w_d = io.w_down[0].rearrange("e (k p) n -> e p k n", p=P)
        HEAD = 3
        DVE_K = 5

        def wait(eng, sem, value):
            if not isinstance(value, int) or value > 0:
                eng.wait_ge(sem, value)

        def dma_count(n, par):
            return n * 8 + (16 - 8 * par)

        def over_blocks(eng, body):
            last = eng.value_load(rt.tab[0:1, 4, 0:1], min_val=N_EXP, max_val=P - 8)
            for n in range(HEAD):
                body(n, n % 2)
            with eng.Fori(2, last, 2) as b:
                for u in (1, 2):
                    body(b + u, u % 2)
            return last

        def entry(eng, k, n, top):
            ap = rt.tab[0:1, k, n:n + 1] if isinstance(n, int) else rt.tab[0:1, k, bass.ds(n, 1)]
            return eng.value_load(ap, min_val=0, max_val=top)

        @block.sync
        def _(sp):
            def gate_up(e, par, until):
                wait(sp, up_l_dve, until)
                wait(sp, up_l_pool, until)
                sp.sem_inc(sp_go, 1)
                for half, src, sem in ((0, w_g, gate_in), (1, w_u, up_in)):
                    wait(sp, sem, e * 16)
                    sp.sem_inc(sp_go, 1)
                    src = src[e:e + 1] if isinstance(e, int) else src[bass.ds(e, 1)]
                    sp.dma_start(raw_up[:, par, :, D_EXP * half:D_EXP * (half + 1)],
                                 src.rearrange("a p k n -> (a p) k n")).then_inc(sem, 16)

            def down(e, par, until):
                wait(sp, dn_l_dve, until)
                wait(sp, dn_l_pool, until)
                sp.sem_inc(sp_go, 1)
                wait(sp, down_in, e * 16)
                sp.sem_inc(sp_go, 1)
                src = w_d[e:e + 1] if isinstance(e, int) else w_d[bass.ds(e, 1)]
                sp.dma_start(raw_dn[:, par, :, :], src.rearrange("a p k n -> (a p) k n")).then_inc(down_in, 16)

            for e in range(2):
                gate_up(e, e, 0)
                down(e, e, 0)
            with sp.Fori(2, N_EXP - 1, 2) as b:
                for u in range(2):
                    until = entry(sp, 3, b + (u - 2), P)
                    gate_up(b + u, u, until)
                    down(b + u, u, until)

        @block.scalar
        def _(act):
            def up_high(n, par):
                e, slot = entry(act, 0, n, N_EXP - 1), entry(act, 2, n, 1)
                wait(act, up_done, n - 1)
                wait(act, gate_in, e * 16 + 16)
                wait(act, up_in, e * 16 + 16)
                act.sem_inc(act_go, 1)
                for lo, hi in ((0, DVE_K), (DVE_K, KD)):
                    act.activation(up_h[:, par, lo:hi, :],
                                   raw_up[:, bass.ds(slot, 1), lo:hi, :].rearrange("p a k n -> p (a k) n"),
                                   ACT.Copy).then_inc(up_h_done, 1)

            def down_high(n, par):
                e, slot = entry(act, 0, n, N_EXP - 1), entry(act, 2, n, 1)
                wait(act, down_done, n - 1)
                wait(act, down_in, e * 16 + 16)
                act.sem_inc(act_go, 1)
                for k in range(2):
                    act.activation(dn_h[:, par, k, :],
                                   raw_dn[:, bass.ds(slot, 1), k, :].rearrange("p a n -> p (a n)"),
                                   ACT.Copy).then_inc(dn_h_done, 1)

            def silu(n, par):
                wait(act, up_done, n + 1)
                wait(act, hid_done, n - 1)
                act.activation(sg[:, par, :], p_gu[:, par, 0:D_EXP], ACT.Silu).then_inc(silu_done, 1)

            def y_out(n, par):
                wait(act, down_done, n + 1)
                wait(act, added[par], dma_count(n - 2, par) if not isinstance(n, int) else 16 * (n // 2))
                act.activation(y[:, par, 0:512], p_dn[:, 0, :], ACT.Copy).then_inc(y_act, 1)

            def x_high(n, par):
                wait(act, x_turned, n + 1)
                wait(act, up_done, n - 1)
                for h in range(2):
                    act.activation(x_h[:, par, 4 * h:4 * h + 4, :], p_tr[:, h, :].rearrange("p (k t) -> p k t", k=4),
                                   ACT.Copy).then_inc(xh_done, 1)

            def hid_high(n, par):
                wait(act, hid_turned, n + 1)
                wait(act, down_done, n - 1)
                act.activation(hid_h[:, par, :, :], p_ht[:, 0:2 * P].rearrange("p (k t) -> p k t", k=2),
                               ACT.Copy).then_inc(hidh_done, 1)

            def body(n, par):
                first = isinstance(n, int) and n == 0
                if first:
                    up_high(0, 0)
                    x_high(0, 0)
                up_high(n + 1, 1 - par)
                silu(n, par)
                x_high(n + 1, 1 - par)
                down_high(n, par)
                if not first:
                    y_out(n - 1, 1 - par)
                hid_high(n, par)
            last = over_blocks(act, body)
            y_out(last + 0, 0)

        @block.gpsimd
        def _(pool):
            bound = pool.to_reg(N_TOK - 1)

            def gather(n, par):
                wait(pool, idx_done, n + 1)
                wait(pool, x_turned, n - 1)
                pool.sem_inc(go, 1)
                pool.indirect_dma_start(out=xg[:, par, :], out_offset=None, in_=io.tok,
                                        in_offset=bass.IndirectOffsetOnAxis(ap=idx_g[:, par:par + 1], axis=0),
                                        bounds_check=bound, oob_is_err=False).then_inc(gathered[par], 16)

            def scatter(n, par):
                wait(pool, y_act, n + 1)
                wait(pool, y_dve, n + 1)
                wait(pool, added[1 - par], dma_count(n - 1, 1 - par) if not isinstance(n, int) or n else 0)
                pool.sem_inc(go, 1)
                pool.indirect_dma_start(out=io.acc, in_=y[:, par, :], in_offset=None,
                                        out_offset=bass.IndirectOffsetOnAxis(ap=idx_s[:, par:par + 1], axis=0),
                                        bounds_check=bound, oob_is_err=False,
                                        compute_op=ALU.add).then_inc(added[par], 16)

            def up_low(n, par):
                slot = entry(pool, 2, n, 1)
                wait(pool, up_h_done, n * 2 + 2)
                pool.sem_inc(go, 1)
                pool.tensor_tensor(up_l[:, par, DVE_K:, :],
                                   raw_up[:, bass.ds(slot, 1), DVE_K:, :].rearrange("p a k n -> p (a k) n"),
                                   up_h[:, par, DVE_K:, :].bitcast(F32), ALU.subtract).then_inc(up_l_pool, 1)

            def down_low(n, par):
                slot = entry(pool, 2, n, 1)
                wait(pool, dn_h_done, n * 2 + 2)
                pool.sem_inc(go, 1)
                pool.tensor_tensor(dn_l[:, par, 1, :],
                                   raw_dn[:, bass.ds(slot, 1), 1, :].rearrange("p a n -> p (a n)"),
                                   dn_h[:, par, 1, :].bitcast(F32), ALU.subtract).then_inc(dn_l_pool, 1)

            def body(n, par):
                first = isinstance(n, int) and n == 0
                if first:
                    gather(0, 0)
                    gather(1, 1)
                    up_low(0, 0)
                    gather(2, 0)
                up_low(n + 1, 1 - par)
                down_low(n, par)
                if not first:
                    scatter(n - 1, 1 - par)
                gather(n + 3, 1 - par)
            pool.memset(xg[:, :, :], 0.0).then_inc(zeroed, 1)
            pool.wait_ge(zeroed, 1)
            last = over_blocks(pool, body)
            scatter(last + 0, 0)
            wait(pool, added[0], dma_count(last, 0))
            wait(pool, gathered[0], dma_count(last + 2, 0))
            wait(pool, gathered[1], dma_count(last + 3, 1))

        @block.tensor
        def _(pe):
            def split_product(out, a, b, free):
                (ah, al), (bh, bl) = a, b
                terms = [(x[:, k, :], w[:, k, free]) for k in range(ah.shape[1])
                         for x, w in ((ah, bh), (ah, bl), (al, bh))]
                for i, (x, w) in enumerate(terms):
                    mm = pe.matmul(out, x, w, start=(i == 0), stop=(i == len(terms) - 1))
                return mm

            def up(n, par):
                wait(pe, up_l_dve, n + 1)
                wait(pe, up_l_pool, n + 1)
                wait(pe, xl_done, n + 1)
                wait(pe, hid_done, n - 1)
                split_product(p_gu[:, par, :], (x_h[:, par], x_l[:, par]), (up_h[:, par], up_l[:, par]),
                              slice(0, 2 * D_EXP)).then_inc(up_done, 1)

            def down(n, par):
                wait(pe, dn_l_dve, n + 1)
                wait(pe, dn_l_pool, n + 1)
                wait(pe, hidl_done, n + 1)
                wait(pe, y_act, n)
                wait(pe, y_dve, n)
                for h in range(2):
                    mm = split_product(p_dn[:, h, :], (hid_h[:, par], hid_l[:, par]), (dn_h[:, par], dn_l[:, par]),
                                       slice(512 * h, 512 * (h + 1)))
                mm.then_inc(down_done, 1)

            def turn_x(n, par):
                wait(pe, gathered[par], dma_count(n, par))
                wait(pe, xl_done, n)
                for k in range(KD):
                    tr = pe.transpose(p_tr[:, k // 4, (k % 4) * P:(k % 4 + 1) * P], xg[:, par, k * P:(k + 1) * P],
                                      keep.ident[:, :])
                tr.then_inc(x_turned, 1)

            def look_up(n, par):
                wait(pe, pick_done, n + 1)
                wait(pe, idx_done, n)
                for k in range(N_TILES):
                    mm = pe.matmul(p_im[:, 0:6], pick[:, par, k, :], rt.vals[:, par, k, :], start=(k == 0),
                                   stop=(k == N_TILES - 1))
                mm.then_inc(info_done, 1)

            def turn_hid(n, par):
                wait(pe, hid_done, n + 1)
                wait(pe, hidl_done, n)
                for k in range(2):
                    tr = pe.transpose(p_ht[:, k * P:(k + 1) * P], hid[:, par, k * P:(k + 1) * P], keep.ident[:, :])
                tr.then_inc(hid_turned, 1)

            def body(n, par):
                first = isinstance(n, int) and n == 0
                if first:
                    for k in range(3):
                        look_up(k, k % 2)
                    turn_x(0, 0)
                up(n, par)
                turn_x(n + 1, 1 - par)
                look_up(n + 3, 1 - par)
                if not first:
                    down(n - 1, 1 - par)
                turn_hid(n, par)
            last = over_blocks(pe, body)
            down(last + 0, 0)

        @block.vector
        def _(v):
            tt, ts, stt = v.tensor_tensor, v.tensor_scalar, v.scalar_tensor_tensor

            def choose(n, par):
                e = entry(v, 0, n, N_EXP - 1)
                j = entry(v, 1, n, P * (SLOT_SETS - 1))
                wait(v, info_done, n - 1)
                tt(pick[:, par, :, :], bc(rt.slot[:, bass.ds(j, P)], 1, N_TILES),
                   rt.posm[:, :, bass.ds(e, 1)].to_broadcast([P, N_TILES, P]), ALU.is_equal)
                v.tensor_copy(rt.vals[:, par, :, 3:6].unsqueeze(2), rt.parts[:, :, bass.ds(e, 1), :]).then_inc(pick_done, 1)

            def index(n, par):
                count = [0]

                def link(ins):
                    count[0] += 1
                    ins.then_inc(s_v, 1)
                    v.wait_ge(s_v, n * LINKS + count[0])
                wait(v, info_done, n + 1)
                wait(v, hid_done, n - 3)
                wait(v, y_dve, n - 3)
                wait(v, gathered[par], dma_count(n - 2, par) if not isinstance(n, int) else 16 * (n // 2))
                if not isinstance(n, int) or n >= 2:
                    v.tensor_copy(cur[:, par, :], new[:, par, :])
                link(v.tensor_copy(info[:, 0:6], p_im[:, 0:6]))
                ts(tmp[:, 0:1], info[:, 2:3], -1.0, 1.0, ALU.mult, ALU.add)
                stt(out=tmp[:, 1:2], in0=info[:, 1:2], scalar=float(P), in1=info[:, 0:1], op0=ALU.mult, op1=ALU.add)
                link(tt(new[:, par, 1:2], info[:, 3:4], info[:, 4:5], ALU.add))
                tt(new[:, par, 1:2], new[:, par, 1:2], info[:, 5:6], ALU.add)
                link(stt(out=new[:, par, 0:1], in0=tmp[:, 0:1], scalar=rt.dummy[:, 0:1], in1=tmp[:, 1:2],
                         op0=ALU.mult, op1=ALU.add))
                v.tensor_copy(idx_g[:, par:par + 1], new[:, par, 0:1]).then_inc(idx_done, 1)
                wait(v, idx_done, n + 1)

            LINKS = 3

            def hidden(n, par):
                wait(v, silu_done, n + 1)
                wait(v, hid_turned, n - 1)
                stt(out=hid[:, par, :], in0=sg[:, par, :], scalar=cur[:, par, 1:2], in1=p_gu[:, par, D_EXP:],
                    op0=ALU.mult, op1=ALU.mult).then_inc(hid_done, 1)

            def up_low(n, par):
                slot = entry(v, 2, n, 1)
                wait(v, up_h_done, n * 2 + 1)
                tt(up_l[:, par, 0:DVE_K, :], raw_up[:, bass.ds(slot, 1), 0:DVE_K, :].rearrange("p a k n -> p (a k) n"),
                   up_h[:, par, 0:DVE_K, :].bitcast(F32), ALU.subtract).then_inc(up_l_dve, 1)

            def down_low(n, par):
                slot = entry(v, 2, n, 1)
                wait(v, dn_h_done, n * 2 + 1)
                tt(dn_l[:, par, 0, :], raw_dn[:, bass.ds(slot, 1), 0, :].rearrange("p a n -> p (a n)"),
                   dn_h[:, par, 0, :].bitcast(F32), ALU.subtract).then_inc(dn_l_dve, 1)

            def x_low(n, par):
                for h in range(2):
                    wait(v, xh_done, n * 2 + (h + 1))
                    low = tt(x_l[:, par, 4 * h:4 * h + 4, :], p_tr[:, h, :].rearrange("p (k t) -> p k t", k=4),
                             x_h[:, par, 4 * h:4 * h + 4, :].bitcast(F32), ALU.subtract)
                low.then_inc(xl_done, 1)

            def y_out(n, par):
                wait(v, down_done, n + 1)
                wait(v, added[par], dma_count(n - 2, par) if not isinstance(n, int) else 16 * (n // 2))
                v.tensor_copy(idx_s[:, par:par + 1], cur[:, par, 0:1])
                v.tensor_copy(y[:, par, 512:], p_dn[:, 1, :]).then_inc(y_dve, 1)

            def hid_low(n, par):
                wait(v, hidh_done, n + 1)
                tt(hid_l[:, par, :, :], p_ht[:, 0:2 * P].rearrange("p (k t) -> p k t", k=2),
                   hid_h[:, par, :, :].bitcast(F32), ALU.subtract).then_inc(hidl_done, 1)

            def body(n, par):
                first = isinstance(n, int) and n == 0
                if first:
                    for k in range(2):
                        choose(k, k)
                    for k in range(3):
                        index(k, k % 2)
                        if k == 0:
                            choose(2, 0)
                    up_low(0, 0)
                    x_low(0, 0)
                choose(n + 3, 1 - par)
                up_low(n + 1, 1 - par)
                hidden(n, par)
                x_low(n + 1, 1 - par)
                down_low(n, par)
                if not first:
                    y_out(n - 1, 1 - par)
                index(n + 3, 1 - par)
                hid_low(n, par)
            last = over_blocks(v, body)
            y_out(last + 0, 0)


def final_stage(nc, io, keep):
    with ExitStack() as ctx:
        m = Pools(nc, ctx, "final")
        x = m.sb("x", [P, N_TILES, D])
        lng, lnb = m.sb("lng", [P, D]), m.sb("lnb", [P, D])
        stats = m.sb("stats", [P, N_TILES, 2, 6])
        mv = m.sb("mv", [P, N_TILES, 2])
        rs = m.sb("rs", [P, N_TILES, 2])
        eps = m.sb("eps", [P, 1])
        s_x = [m.sem(f"x{i}") for i in range(N_TILES)]
        s_ln, s_eps, s_stat, s_std, s_rs, s_nm, s_gain, s_y, s_out, s_v = (
            m.sem(n) for n in ("ln", "eps", "stat", "std", "rs", "nm", "gain", "y", "out", "vch"))
        block = ctx.enter_context(nc.Block())

        @block.sync
        def _(sp):
            for i in range(N_TILES):
                sp.dma_start(x[:, i, :], io.acc[i * P:(i + 1) * P, :]).then_inc(s_x[i], 16)
            for i in range(N_TILES):
                sp.wait_ge(s_y, i + 1)
                if i < N_TILES - 1:
                    sp.dma_start(io.out_y_p[0, i * P:(i + 1) * P, :], x[:, i, :]).then_inc(s_out, 16)
                else:
                    sp.dma_start(io.out_y_s[0], x[0:LAST_ROWS, i, :]).then_inc(s_out, 16)
            sp.wait_ge(s_out, 16 * N_TILES)

        @block.gpsimd
        def _(pool):
            pool.memset(eps[:, :], LN_EPS).then_inc(s_eps, 1)
            pool.wait_ge(s_ln, 32)
            for i in range(N_TILES):
                pool.wait_ge(s_gain, i + 1)
                pool.tensor_tensor(x[:, i, :], x[:, i, :], lnb[:, :], ALU.add).then_inc(s_y, 1)

        @block.scalar
        def _(act):
            act.dma_start(lng[:, :], io.ln2_g[0].partition_broadcast(P)).then_inc(s_ln, 16)
            act.dma_start(lnb[:, :], io.ln2_b[0].partition_broadcast(P)).then_inc(s_ln, 16)
            act.wait_ge(s_eps, 1)
            for i in range(N_TILES):
                act.wait_ge(s_stat, i + 1)
                act.activation(rs[:, i, 0:1], mv[:, i, 1:2], ACT.Sqrt, bias=eps[:, 0:1]).then_inc(s_std, 1)
                act.wait_ge(s_rs, i + 1)
                act.activation(x[:, i, :], x[:, i, :], ACT.Identity, bias=rs[:, i, 1:2],
                               scale=rs[:, i, 0:1]).then_inc(s_nm, 1)

        @block.vector
        def _(v):
            link = chain(v, s_v)

            def scale(i):
                v.wait_ge(s_std, i + 1)
                link(v.reciprocal(rs[:, i, 0:1], rs[:, i, 0:1]))
                v.scalar_tensor_tensor(out=rs[:, i, 1:2], in0=mv[:, i, 0:1], scalar=-1.0, in1=rs[:, i, 0:1],
                                       op0=ALU.mult, op1=ALU.mult).then_inc(s_rs, 1)

            def gain(i):
                v.wait_ge(s_nm, i + 1)
                if i == 0:
                    v.wait_ge(s_ln, 32)
                v.tensor_tensor(x[:, i, :], x[:, i, :], lng[:, :], ALU.mult).then_inc(s_gain, 1)

            for i in range(N_TILES):
                v.wait_ge(s_x[i], 16)
                v.bn_stats(stats[:, i, 0, :], x[:, i, 0:512])
                link(v.bn_stats(stats[:, i, 1, :], x[:, i, 512:]))
                v.bn_aggr(mv[:, i, :], stats[:, i, :, :]).then_inc(s_stat, 1)
                if i:
                    gain(i - 1)
                scale(i)
            gain(N_TILES - 1)


def build(nc, args):
    io = Names()
    io.x_prompt, io.x_sample, io.state_ssm_re = args["x_prompt"], args["x_sample"], args["state_ssm_re"]
    io.state_ssm_im, io.cache_conv, io.ln_in_g = args["state_ssm_im"], args["cache_conv"], args["ln_in_g"]
    io.ln_in_b, io.w_in, io.lam_re = args["ln_in_b"], args["w_in"], args["lam_re"]
    io.lam_im, io.log_dt, io.ssm_b_re = args["lam_im"], args["log_dt"], args["ssm_b_re"]
    io.ssm_b_im, io.ssm_c_re, io.ssm_c_im = args["ssm_b_im"], args["ssm_c_re"], args["ssm_c_im"]
    io.ssm_d, io.w_glu, io.b_glu = args["ssm_d"], args["w_glu"], args["b_glu"]
    io.conv_w, io.beta_ssm, io.beta_conv = args["conv_w"], args["beta_ssm"], args["beta_conv"]
    io.w_out, io.ln1_g, io.ln1_b = args["w_out"], args["ln1_g"], args["ln1_b"]
    io.w_router, io.router_bias, io.w_gate = args["w_router"], args["router_bias"], args["w_gate"]
    io.w_up, io.w_down, io.ws_gate = args["w_up"], args["w_down"], args["ws_gate"]
    io.ws_up, io.ws_down, io.ln2_g = args["ws_up"], args["ws_down"], args["ln2_g"]
    io.ln2_b, io.out_y_p, io.out_y_s = args["ln2_b"], args["out_y_p"], args["out_y_s"]
    io.out_ssm_re_p, io.out_ssm_im_p, io.out_conv_p = args["out_ssm_re_p"], args["out_ssm_im_p"], args["out_conv_p"]
    io.out_ssm_re_s, io.out_ssm_im_s, io.out_conv_s = args["out_ssm_re_s"], args["out_ssm_im_s"], args["out_conv_s"]

    def dram(name, shape):
        return nc.dram_tensor(name, shape, F32, kind="Internal").ap()

    io.resid = dram("resid", (ROWS, D))
    io.ud = dram("ud", (D_HALF, N_TOK))
    io.yd = dram("yd", (D_HALF, N_TOK))
    io.tok = dram("tok", (ROWS, D))
    io.acc = dram("acc", (ROWS, D))
    with ExitStack() as ctx:
        m = Pools(nc, ctx, "keep")
        keep = Names()
        keep.ident = m.sb("ident", [P, P])
        keep.scores = m.sb("scores", [P, N_TILES, N_EXP])
        with ExitStack() as half:
            h = Pools(nc, half, "keep")
            keep.gT = h.sb("gT", [P, KH, ROWS])
            keep.ycT = h.sb("ycT", [P, KH, ROWS])
            with ExitStack() as first:
                f = Pools(nc, first, "co")
                keep.hT = f.sb("hT", [P, KD, N_TOK])
                co = Names()
                co.sign = f.sb("sign", [P, 1])
                co.pr = f.sb("pr", [P, GROUPS, T + 1])
                co.pi = f.sb("pi", [P, GROUPS, T + 1])
                co.prs = f.sb("prs", [P, GROUPS, T + 1])
                co.npi = f.sb("npi", [P, GROUPS, T + 1])
                co.nsi = f.sb("nsi", [P, GROUPS, T + 1])
                co.bb = f.sb("bb", [P, GROUPS, GC])
                co.bbsw = f.sb("bbsw", [P, GROUPS, GC])
                co.cs = f.sb("cs", [P, KH * P])
                co.csw = f.sb("csw", [P, KH * P])
                co.h0 = f.sb("h0", [P, GROUPS])
                co.ah0 = f.sb("ah0", [P, GROUPS])
                co.er = f.sb("er", [P, GROUPS, 7])
                co.eis = f.sb("eis", [P, GROUPS, 7])
                co.decay = f.sb("decay", [P, GROUPS])
                trunk_stage(nc, io, keep, co)
                mixing_stage(nc, io, keep, co)
            output_stage(nc, io, keep)
        with ExitStack() as moe:
            r = Pools(nc, moe, "rt")
            rt = Names()
            rt.slot = r.sb("slot", [P, P * SLOT_SETS])
            rt.dummy = r.sb("dummy", [P, 1])
            rt.vals = r.sb("vals", [P, 2, N_TILES, 6], BF16)
            rt.parts = r.sb("parts", [P, N_TILES, N_EXP, 3], BF16)
            rt.posm = r.sb("posm", [P, N_TILES, N_EXP])
            rt.tab = r.sb("tab", [1, 5, P + 8], I32)
            routing_stage(nc, io, keep, rt)
            expert_stage(nc, io, keep, rt)
        final_stage(nc, io, keep)
    return


_INS = ['x_prompt', 'x_sample', 'state_ssm_re', 'state_ssm_im', 'cache_conv', 'ln_in_g', 'ln_in_b', 'w_in', 'lam_re',
        'lam_im', 'log_dt', 'ssm_b_re', 'ssm_b_im', 'ssm_c_re', 'ssm_c_im', 'ssm_d', 'w_glu', 'b_glu', 'conv_w',
        'beta_ssm', 'beta_conv', 'w_out', 'ln1_g', 'ln1_b', 'w_router', 'router_bias', 'w_gate', 'w_up', 'w_down',
        'ws_gate', 'ws_up', 'ws_down', 'ln2_g', 'ln2_b']
_OUTS = [("out_y_p", (1, 1024, 1024)), ("out_y_s", (1, 64, 1024)),
         ("out_ssm_re_p", (1, 1, 32, 64)), ("out_ssm_im_p", (1, 1, 32, 64)), ("out_conv_p", (1, 1, 2, 512)),
         ("out_ssm_re_s", (1, 1, 32, 64)), ("out_ssm_im_s", (1, 1, 32, 64)), ("out_conv_s", (1, 1, 2, 512))]


def kernel(**inputs):
    import numpy as _np
    import concourse.bacc as _bacc
    from concourse import mybir as _mybir
    from concourse.bass_utils import run_bass_kernel_spmd as _run

    nc = _bacc.Bacc("TRN2", target_bir_lowering=False, num_devices=1)
    arrays, args = {}, {}
    for name in _INS:
        a = _np.ascontiguousarray(inputs[name])
        arrays[f"in_{name}_dram"] = a
        args[name] = nc.dram_tensor(f"in_{name}_dram", a.shape, _mybir.dt.from_np(a.dtype), kind="ExternalInput").ap()
    for name, shape in _OUTS:
        args[name] = nc.dram_tensor(f"{name}_dram", shape, _mybir.dt.from_np(_np.dtype("float32")),
                                    kind="ExternalOutput").ap()
    build(nc, args)
    r = _run(nc, [arrays], core_ids=[0])
    return tuple(r.results[0][f"{name}_dram"] for name, _ in _OUTS)
```

```python
from contextlib import ExitStack

import numpy as np
import concourse.bass as bass
from concourse import mybir

ALU = mybir.AluOpType
ACT = mybir.ActivationFunctionType
F32 = mybir.dt.float32
F32R = mybir.dt.float32r
I32 = mybir.dt.int32
BF16 = mybir.dt.bfloat16

P = 128
D = 1024
KD = D // P
N_PROMPT = 1024
N_SAMPLE = 64
N_TOK = N_PROMPT + N_SAMPLE
N_TILES = (N_TOK + P - 1) // P
LAST_ROWS = N_TOK - (N_TILES - 1) * P
ROWS = N_TILES * P
D_HALF = 512
KH = D_HALF // P
GROUPS = 32
GC = 16
STATE = 64
GT = P // GC
T = 8
NK = N_TOK // T
NKP = N_PROMPT // T
N_EXP = 64
N_EGRP = 8
TOP_GROUPS = 4
TOP_K = 6
D_EXP = 256
ROUTED_SCALE = 2.5
IN_RING = 3
UP_SLOTS = 3
SLOT_SETS = N_TILES + 1
CW = 384
TOK_CHUNKS = [(0, CW), (CW, CW), (2 * CW, N_TOK - 2 * CW)]
ALPHA = 2.0 ** 0.25
LN_EPS = 1e-5
RMS_EPS = 1e-6
TWO_PI_HI = 6.28125
TWO_PI_MID = 0.0019350051879882812
TWO_PI_LO = 3.019915981956753e-07
ROUND = 12582912.0
PI_BELOW = 3.1415925
TRIPLES = [(0, 3), (3, 3), (6, 2)]


class Names:
    pass


def chain(eng, own):
    count = {}

    def link(ins, sem=own):
        count[sem] = count.get(sem, 0) + 1
        ins.then_inc(sem, 1)
        eng.wait_ge(sem, count[sem])
    return link


def bc(ap, axis, n):
    shape = list(ap.shape)
    shape.insert(axis, n)
    return ap.unsqueeze(axis).to_broadcast(shape)


class Pools:

    def __init__(self, nc, ctx, stage):
        self.nc, self.ctx, self.stage, self.sems = nc, ctx, stage, []
        ctx.callback(self.clear)

    def sb(self, name, shape, dt=F32):
        return self.ctx.enter_context(self.nc.sbuf_tensor(f"{self.stage}_{name}", shape, dt))

    def ps(self, name, shape, dt=F32):
        return self.ctx.enter_context(self.nc.psum_tensor(f"{self.stage}_{name}", shape, dt))

    def sem(self, name):
        self.sems.append(self.nc.alloc_semaphore(f"{self.stage}_{name}"))
        return self.sems[-1]

    def clear(self):
        if self.sems:
            self.nc.clear_and_free_semaphores(self.sems)
            self.nc.all_engine_barrier()


def trunk_stage(nc, io, keep, co):
    with ExitStack() as ctx:
        m = Pools(nc, ctx, "trunk")
        x = m.sb("x", [P, N_TILES, D])
        lng, lnb = m.sb("lng", [P, D]), m.sb("lnb", [P, D])
        stats = m.sb("stats", [P, N_TILES, 2, 6])
        mv = m.sb("mv", [P, N_TILES, 2])
        rs = m.sb("rs", [P, N_TILES, 2])
        eps = m.sb("eps", [P, 1])
        ones_sq = m.sb("ones_sq", [P, P])
        rows = m.sb("rows", [GROUPS, 5, P])
        ldt = m.sb("ldt", [GROUPS, 1])
        crow = m.sb("crow", [P, KH, P])
        crow_sw = m.sb("crow_sw", [P, KH, P])
        par = m.sb("par", [P, 5, GROUPS])
        t = m.sb("t", [P, 12, GROUPS])
        ang = m.sb("ang", [P, 2, GROUPS])
        tb, tb_sw = m.sb("tb", [P, 2, GROUPS, GC]), m.sb("tb_sw", [P, 2, GROUPS, GC])
        bs = m.sb("bs", [P, GROUPS, GC])
        bsw = m.sb("bsw", [P, GROUPS, GC])
        pst = m.ps("pst", [P, 4, 4, P])
        pso = m.ps("pso", [P, 3, 512])
        s_x = [m.sem(f"x{i}") for i in range(N_TILES)]
        s_ln, s_par, s_b, s_c = m.sem("ln"), m.sem("par"), m.sem("b"), m.sem("c")
        s_const, s_pool = m.sem("const"), m.sem("pool")
        s_stat, s_std, s_rs = m.sem("stat"), m.sem("std"), m.sem("rs")
        s_norm, s_gain, s_h, s_tr, s_ev = m.sem("norm"), m.sem("gain"), m.sem("h"), m.sem("tr"), m.sem("ev")
        s_kept = m.sem("kept")
        s_rows, s_part, s_parc = m.sem("rows"), m.sem("part"), m.sem("parc")
        s_dt, s_arg, s_mag, s_ang, s_sin, s_bsw = (m.sem(n) for n in ("dt", "arg", "mag", "ang", "sin", "bsw"))
        s_v = m.sem("v")
        block = ctx.enter_context(nc.Block())

        def dup(dst, src, order):
            return [(dst[:, 64 * h:64 * h + 64], src[w]) for h, w in enumerate(order)]

        @block.sync
        def _(sp):
            for i in range(2):
                sp.dma_start(x[:, i, :], io.x_prompt[0, i * P:(i + 1) * P, :]).then_inc(s_x[i], 16)
            h0 = (io.state_ssm_re[0, 0], io.state_ssm_im[0, 0])
            lr = (io.lam_re[0],) * 2
            li = (io.lam_im[0],) * 2
            for k, (src, order) in enumerate((
                    (lr, (0, 1)), (li, (0, 1)), (h0, (0, 1)), (h0, (1, 0)))):
                slot = (0, 1, 3, 4)[k]
                for dst, s in dup(rows[:, slot, :], src, order):
                    sp.dma_start(dst, s).then_inc(s_par, 16)
            with nc.allow_non_contiguous_dma(reason="a column of step sizes"):
                sp.dma_start(ldt[:, :], io.log_dt.rearrange("a g -> g a")).then_inc(s_par, 16)
            for i in range(2, N_TILES - 1):
                sp.dma_start(x[:, i, :], io.x_prompt[0, i * P:(i + 1) * P, :]).then_inc(s_x[i], 16)
            sp.dma_start(x[0:LAST_ROWS, N_TILES - 1, :], io.x_sample[0]).then_inc(s_x[N_TILES - 1], 16)
            for i in range(IN_RING):
                sp.dma_start(co.win[:, i, :, :],
                             io.w_in[0].rearrange("(k p) n -> p k n", p=P)[:, :, i * P:(i + 1) * P]).then_inc(co.s_w[i], 16)
            for i in range(N_TILES):
                sp.wait_ge(s_h, i + 1)
                sp.dma_start(io.resid[i * P:(i + 1) * P, :], x[:, i, :]).then_inc(s_kept, 16)
            sp.wait_ge(s_kept, 16 * N_TILES)

        @block.scalar
        def _(act):
            act.dma_start(bs[0:64, :, :], io.ssm_b_re[0].rearrange("g p c -> p g c")).then_inc(s_b, 16)
            act.dma_start(bs[64:128, :, :], io.ssm_b_im[0].rearrange("g p c -> p g c")).then_inc(s_b, 16)
            act.dma_start(lng[:, :], io.ln_in_g.partition_broadcast(P)).then_inc(s_ln, 16)
            act.dma_start(lnb[:, :], io.ln_in_b.partition_broadcast(P)).then_inc(s_ln, 16)
            c_re = io.ssm_c_re[0].rearrange("(m g) c p -> (g c) m p", m=KH)
            c_im = io.ssm_c_im[0].rearrange("(m g) c p -> (g c) m p", m=KH)
            act.dma_start(crow[:, :, 0:64], c_re).then_inc(s_c, 16)
            act.dma_start(crow[:, :, 64:128], c_im).then_inc(s_c, 16)
            act.dma_start(crow_sw[:, :, 0:64], c_im).then_inc(s_c, 16)
            act.dma_start(crow_sw[:, :, 64:128], c_re).then_inc(s_c, 16)
            act.wait_ge(s_parc, 1)
            act.activation(t[:, 0, :], par[:, 2, :], ACT.Exp).then_inc(s_dt, 1)
            act.wait_ge(s_arg, 1)
            act.activation(t[:, 2, :], t[:, 1, :], ACT.Exp).then_inc(s_mag, 1)
            act.wait_ge(s_ang, 1)
            act.activation(t[:, 4:6, :], ang[:, :, :], ACT.Sin).then_inc(s_sin, 1)
            act.wait_ge(s_const, 1)

            def turned(i):
                for half in range(2):
                    n = 2 * i + half
                    act.wait_ge(s_tr, n + 1)
                    w = P if i < N_TILES - 1 else LAST_ROWS
                    act.activation(keep.hT[:, 4 * half:4 * half + 4, i * P:i * P + w],
                                   pst[:, n % 4, :, 0:w], ACT.Copy).then_inc(s_ev, 1)

            for i in range(N_TILES):
                act.wait_ge(s_stat, i + 1)
                act.activation(rs[:, i, 0:1], mv[:, i, 1:2], ACT.Sqrt, bias=eps[:, 0:1]).then_inc(s_std, 1)
                act.wait_ge(s_rs, i + 1)
                act.activation(x[:, i, :], x[:, i, :], ACT.Identity, bias=rs[:, i, 1:2],
                               scale=rs[:, i, 0:1]).then_inc(s_norm, 1)
                if i >= 2:
                    turned(i - 2)
            for i in range(N_TILES - 2, N_TILES):
                turned(i)
            for k, dst in enumerate((co.cs, co.csw)):
                act.wait_ge(s_part, 2 + k)
                act.activation(dst[:, :], pso[:, 1 + k, :], ACT.Copy)

        @block.gpsimd
        def _(pool):
            link = chain(pool, s_pool)
            link(pool.memset(x[64:128, N_TILES - 1, :], 0.0))
            link(pool.memset(ones_sq[:, :], 1.0))
            link(pool.affine_select(out=keep.ident[:, :], in_=ones_sq[:, :], compare_op=ALU.is_equal, fill=0.0,
                                    base=0, pattern=[[-1, P]], channel_multiplier=1))
            link(pool.memset(eps[:, :], LN_EPS))
            link(pool.memset(co.sign[64:128, :], -1.0))
            pool.memset(co.sign[0:64, :], 1.0).then_inc(s_const, 1)
            pool.wait_ge(s_const, 1)
            for i in range(N_TILES):
                pool.wait_ge(s_gain, i + 1)
                if i == 0:
                    pool.wait_ge(s_ln, 32)
                pool.tensor_tensor(x[:, i, :], x[:, i, :], lnb[:, :], ALU.add).then_inc(s_h, 1)
            pool.wait_ge(s_b, 32)
            pool.wait_ge(s_bsw, 1)
            qr, nqi = bc(t[:, 0, :], 2, GC), bc(t[:, 1, :], 2, GC)
            link(pool.tensor_tensor(tb_sw[:, 0], bsw[:, :, :], qr, ALU.mult))
            link(pool.tensor_tensor(tb_sw[:, 1], bs[:, :, :], nqi, ALU.mult))
            link(pool.tensor_tensor(co.bbsw[:, :, :], tb_sw[:, 0], tb_sw[:, 1], ALU.subtract))

        @block.tensor
        def _(pe):
            pe.wait_ge(s_const, 1)
            pe.wait_ge(s_rows, 1)
            for k in range(5):
                tr = pe.transpose(pso[:, 0, k * GROUPS:(k + 1) * GROUPS], rows[:, k, :],
                                  keep.ident[0:GROUPS, 0:GROUPS])
            tr.then_inc(s_part, 1)
            pe.wait_ge(s_c, 64)
            for v, src in enumerate((crow, crow_sw)):
                for k in range(KH):
                    tr = pe.transpose(pso[:, 1 + v, k * P:(k + 1) * P], src[:, k, :], keep.ident[:, :])
                tr.then_inc(s_part, 1)
            for i in range(N_TILES):
                pe.wait_ge(s_h, i + 1)
                for half in range(2):
                    n = 2 * i + half
                    if n >= 4:
                        pe.wait_ge(s_ev, n - 3)
                    for k in range(4):
                        c = (4 * half + k) * P
                        tr = pe.transpose(pst[:, n % 4, k, :], x[:, i, c:c + P], keep.ident[:, :])
                    tr.then_inc(s_tr, 1)

        @block.vector
        def _(v):
            link = chain(v, s_v)
            tt, ts, stt = v.tensor_tensor, v.tensor_scalar, v.scalar_tensor_tensor

            def cmul(outr, outi, ar, ai, br, bi, tmp):
                tt(tmp[0], ar, br, ALU.mult)
                tt(tmp[1], ai, bi, ALU.mult)
                tt(tmp[2], ar, bi, ALU.mult)
                link(tt(tmp[3], ai, br, ALU.mult))
                tt(outr, tmp[0], tmp[1], ALU.subtract)
                link(tt(outi, tmp[2], tmp[3], ALU.add))

            def stats_of(i):
                v.wait_ge(s_x[i], 16)
                v.bn_stats(stats[:, i, 0, :], x[:, i, 0:512])
                link(v.bn_stats(stats[:, i, 1, :], x[:, i, 512:]))
                v.bn_aggr(mv[:, i, :], stats[:, i, :, :]).then_inc(s_stat, 1)

            for i in range(2):
                stats_of(i)
            v.wait_ge(s_par, 16 * 9)
            link(v.tensor_copy(rows[:, 2, :], ldt[:, 0:1].to_broadcast([GROUPS, P])))
            v.sem_inc(s_rows, 1)
            v.wait_ge(s_part, 1)
            v.tensor_copy(par[:, :, :], pso[:, 0, 0:5 * GROUPS].rearrange("p (a g) -> p a g", a=5)).then_inc(s_parc, 1)
            v.wait_ge(s_parc, 1)
            lr, li, h0, h0sw = (par[:, k, :] for k in (0, 1, 3, 4))
            v.wait_ge(s_dt, 1)
            tt(t[:, 1, :], lr, t[:, 0, :], ALU.mult).then_inc(s_arg, 1)
            link(tt(t[:, 3, :], li, t[:, 0, :], ALU.mult))
            th = t[:, 3, :]
            for k in range(2):
                n = t[:, 6 + k, :]
                link(ts(n, th, float(1 / (2 * np.pi)), 0.25 * k, ALU.mult, ALU.add))
                link(ts(n, n, ROUND, None, ALU.add))
                link(ts(n, n, ROUND, None, ALU.subtract))
                link(stt(out=ang[:, k, :], in0=n, scalar=-TWO_PI_HI, in1=th, op0=ALU.mult, op1=ALU.add))
                link(stt(out=ang[:, k, :], in0=n, scalar=-TWO_PI_MID, in1=ang[:, k, :], op0=ALU.mult, op1=ALU.add))
                link(stt(out=ang[:, k, :], in0=n, scalar=-TWO_PI_LO, in1=ang[:, k, :], op0=ALU.mult, op1=ALU.add))
                if k:
                    link(ts(ang[:, k, :], ang[:, k, :], float(np.pi / 2), None, ALU.add))
                link(ts(ang[:, k, :], ang[:, k, :], PI_BELOW, -PI_BELOW, ALU.min, ALU.max))
            v.sem_inc(s_ang, 1)
            v.wait_ge(s_sin, 1)
            v.wait_ge(s_mag, 1)
            sin, cos, mag = t[:, 4, :], t[:, 5, :], t[:, 2, :]
            tmp = [t[:, k, :] for k in (8, 9, 10, 11)]

            def unit(c, s):
                tt(tmp[0], c, c, ALU.mult)
                link(tt(tmp[1], s, s, ALU.mult))
                link(tt(tmp[2], tmp[0], tmp[1], ALU.add))
                link(ts(tmp[2], tmp[2], -0.5, 1.5, ALU.mult, ALU.add))
                tt(c, c, tmp[2], ALU.mult)
                link(tt(s, s, tmp[2], ALU.mult))

            def scale_of(i):
                v.wait_ge(s_std, i + 1)
                link(v.reciprocal(rs[:, i, 0:1], rs[:, i, 0:1]))
                stt(out=rs[:, i, 1:2], in0=mv[:, i, 0:1], scalar=-1.0, in1=rs[:, i, 0:1], op0=ALU.mult,
                    op1=ALU.mult).then_inc(s_rs, 1)

            def gain_of(i):
                v.wait_ge(s_ln, 32)
                v.wait_ge(s_norm, i + 1)
                tt(x[:, i, :], x[:, i, :], lng[:, :], ALU.mult).then_inc(s_gain, 1)

            def layer_norm(step):
                if 2 <= step < N_TILES:
                    stats_of(step)
                if 1 <= step <= N_TILES:
                    scale_of(step - 1)
                if step >= 2:
                    gain_of(step - 2)

            unit(cos, sin)
            layer_norm(1)
            pr, pi = co.pr, co.pi
            v.memset(pr[:, :, 0], 1.0)
            v.memset(pi[:, :, 0], 0.0)
            tt(pr[:, :, 1], mag, cos, ALU.mult)
            link(tt(pi[:, :, 1], mag, sin, ALU.mult))
            cmul(pr[:, :, 2], pi[:, :, 2], pr[:, :, 1], pi[:, :, 1], pr[:, :, 1], pi[:, :, 1], tmp)
            layer_norm(2)
            for lo in (1, 2):
                cmul(pr[:, :, 2 + lo], pi[:, :, 2 + lo], pr[:, :, lo], pi[:, :, lo], pr[:, :, 2], pi[:, :, 2], tmp)
                layer_norm(2 + lo)
            for lo in (1, 2, 3, 4):
                cmul(pr[:, :, 4 + lo], pi[:, :, 4 + lo], pr[:, :, lo], pi[:, :, lo], pr[:, :, 4], pi[:, :, 4], tmp)
                layer_norm(4 + lo)
            den, ar1 = t[:, 6, :], t[:, 7, :]
            ai = pi[:, :, 1]
            tt(tmp[0], lr, lr, ALU.mult)
            link(tt(tmp[1], li, li, ALU.mult))
            link(tt(den, tmp[0], tmp[1], ALU.add))
            v.reciprocal(den, den)
            link(ts(ar1, pr[:, :, 1], -1.0, None, ALU.add))
            layer_norm(9)
            tt(tmp[0], ar1, lr, ALU.mult)
            tt(tmp[1], ai, li, ALU.mult)
            tt(tmp[2], ai, lr, ALU.mult)
            link(tt(tmp[3], ar1, li, ALU.mult))
            tt(tmp[0], tmp[0], tmp[1], ALU.add)
            link(tt(tmp[2], tmp[3], tmp[2], ALU.subtract))
            qr, nqi = t[:, 0, :], t[:, 1, :]
            tt(qr, tmp[0], den, ALU.mult)
            link(tt(nqi, tmp[2], den, ALU.mult))
            layer_norm(10)
            v.wait_ge(s_const, 1)
            sg = co.sign[:, 0:1]
            link(ts(nqi, nqi, sg, None, ALU.mult))
            tt(co.nsi[:, :, :], pi[:, :, :], sg.unsqueeze(2).to_broadcast([P, GROUPS, 9]), ALU.mult)
            tt(co.prs[:, :, :], pr[:, :, :], sg.unsqueeze(2).to_broadcast([P, GROUPS, 9]), ALU.mult)
            link(ts(co.npi[:, :, :], pi[:, :, :], -1.0, None, ALU.mult))
            v.wait_ge(s_b, 32)
            v.tensor_copy(bsw[0:64, :, :], bs[64:128, :, :])
            link(v.tensor_copy(bsw[64:128, :, :], bs[0:64, :, :]))
            v.sem_inc(s_bsw, 1)
            qrb, nqb = bc(qr, 2, GC), bc(nqi, 2, GC)
            tt(tb[:, 0], bs[:, :, :], qrb, ALU.mult)
            link(tt(tb[:, 1], bsw[:, :, :], nqb, ALU.mult))
            link(tt(co.bb[:, :, :], tb[:, 0], tb[:, 1], ALU.add))
            tt(tmp[0], h0, pr[:, :, 8], ALU.mult)
            link(tt(tmp[1], h0sw, co.nsi[:, :, 8], ALU.mult))
            v.tensor_copy(co.h0[:, :], h0)
            link(tt(co.ah0[:, :], tmp[0], tmp[1], ALU.subtract))
            v.tensor_copy(co.turn[:, 0, :], cos)
            v.tensor_copy(co.turn[:, 1, :], sin)
            v.tensor_copy(co.turn[:, 2, :], mag)


def mixing_stage(nc, io, keep, co):
    with ExitStack() as ctx:
        m = Pools(nc, ctx, "mix")
        RING = IN_RING
        hT = keep.hT
        gT, ycT = keep.gT[:, :, 0:N_TOK], keep.ycT[:, :, 0:N_TOK]
        win = co.win
        v_sb = m.sb("v", [P, N_TOK])
        gb = m.sb("gb", [P, N_TOK])
        cv = m.sb("cv", [P, N_TOK + 4])
        SAMPLE = N_PROMPT + 2
        cacheT = m.sb("cacheT", [P, KH, 2])
        taps = m.sb("taps", [P, KH, 3])
        u = m.sb("u", [P, GT, NK])
        bt = m.sb("bt", [P, GT, P])
        btsw = m.sb("btsw", [P, GT, P])
        bp = m.sb("bp", [P, GT, P])
        c1 = m.sb("c1", [P, GT, (T + 1) * GC])
        c2 = m.sb("c2", [P, GT, T * GC])
        toep = m.sb("toep", [P, GT, P])
        kf = m.sb("kf", [GC, GT, 2 * T, GC])
        dd = m.sb("dd", [GC, GROUPS, GC])
        t1, t2 = m.sb("t1", [P, GT * (T + 1) * GC]), m.sb("t2", [P, GT * (T + 1) * GC])
        cos, sin, dec = (m.sb(n, [P, GT, NK]) for n in ("cos", "sin", "dec"))
        q1, q2 = m.sb("q1", [P, GT * NKP // 2]), m.sb("q2", [P, GT * NKP // 2])
        w, g = m.sb("w", [P, GT, NK]), m.sb("g", [P, GT, NK])
        hc, hs = m.sb("hc", [P, GT, NK]), m.sb("hs", [P, GT, NK])
        y = m.sb("y", [P, GT, NK])
        fin = m.sb("fin", [P, 2, 2, GROUPS])
        swap = m.sb("swap", [P, P])
        fo = m.sb("fo", [GROUPS, 2, P])
        proj = m.ps("proj", [P, 3, 512])
        sb = m.ps("ssm", [P, 4, 512])
        misc = m.ps("misc", [P, 512])

        s_w = co.s_w
        s_small, s_const = m.sem("small"), m.sem("const")
        s_proj, s_pact, s_pdve = m.sem("proj"), m.sem("pact"), m.sem("pdve")
        s_uout = [m.sem(f"uout{c}") for c in range(KH)]
        s_uin, s_yout, s_yin = m.sem("uin"), m.sem("yout"), m.sem("yin")
        s_bp, s_bpt, s_bt, s_c, s_k, s_kev, s_kdma, s_toep = (
            m.sem(n) for n in ("bp", "bpt", "bt", "c", "k", "kev", "kdma", "toep"))
        s_tab, s_bu, s_app, s_hch, s_y, s_yev = (m.sem(n) for n in ("tab", "bu", "app", "hch", "y", "yev"))
        s_rot, s_cv, s_conv = m.sem("rot"), m.sem("cv"), m.sem("conv")
        s_cvout, s_fin, s_finp, s_finc, s_out = m.sem("cvout"), m.sem("fin"), m.sem("finp"), m.sem("finc"), m.sem("out")
        s_v, s_g, s_decay = m.sem("vch"), m.sem("gch"), m.sem("decay")
        block = ctx.enter_context(nc.Block())

        order = [("u", 0), ("u", 1), ("u", 2), ("T", 0), ("u", 3), ("S", 0), ("v", 0), ("gc", 0), ("Y", 0),
                 ("T", 1), ("gb", 0), ("S", 1), ("v", 1), ("gc", 1), ("Y", 1),
                 ("T", 2), ("gb", 1), ("S", 2), ("v", 2), ("gc", 2), ("Y", 2),
                 ("T", 3), ("gb", 2), ("S", 3), ("v", 3), ("gc", 3), ("Y", 3), ("gb", 3)]
        column = {"u": 0, "gb": KH, "gc": 2 * KH, "v": 3 * KH}
        tiles = [o for o in order if o[0] in column]
        emptied, act_n, dve_n = [], 0, 0
        for kind, _ in tiles:
            for _ in TOK_CHUNKS:
                if kind == "gc":
                    dve_n += 1
                    emptied.append((s_pdve, dve_n))
                else:
                    act_n += 1
                    emptied.append((s_pact, act_n))
        first = {o: 3 * i for i, o in enumerate(tiles)}
        pact_after = {o: emptied[first[o] + 2][1] for o in tiles}

        @block.sync
        def _(sp):
            def weight(i):
                kind, c = tiles[i]
                if i >= RING:
                    sp.wait_ge(s_proj, 3 * (i - RING) + 3)
                col = (column[kind] + c) * P
                sp.dma_start(win[:, i % RING, :, :],
                             io.w_in[0].rearrange("(k p) n -> p k n", p=P)[:, :, col:col + P]).then_inc(s_w[i % RING], 16)

            sent = [RING]

            def weights(n):
                while sent[0] < min(n, len(tiles)):
                    weight(sent[0])
                    sent[0] += 1
            with nc.allow_non_contiguous_dma(reason="per-channel rows"):
                sp.dma_start(cacheT[:, :, 0], io.cache_conv[0, 0, 0].rearrange("(c p) -> p c", p=P)).then_inc(s_small, 16)
                sp.dma_start(cacheT[:, :, 1], io.cache_conv[0, 0, 1].rearrange("(c p) -> p c", p=P)).then_inc(s_small, 16)
                for k in range(3):
                    sp.dma_start(taps[:, :, k], io.conv_w[0, k].rearrange("(c p) -> p c", p=P)).then_inc(s_small, 16)
            sp.dma_start(dd[:, :, :], io.ssm_d[0].rearrange("(g c) -> g c", c=GC).partition_broadcast(GC)).then_inc(s_small, 16)
            done = 0
            for kind, c in order:
                if kind in column:
                    done += 1
                if kind == "u":
                    sp.wait_ge(s_pact, pact_after[("u", c)])
                    sp.dma_start(io.ud[c * P:(c + 1) * P, :], gT[:, c, :]).then_inc(s_uout[c], 16)
                if kind == "T":
                    sp.wait_ge(s_uout[c], 16)
                    if c:
                        sp.wait_ge(s_y, 3 * c)
                    ud = io.ud[c * P:(c + 1) * P, :].rearrange("(g c) (s k) -> s c g k", g=GT, s=T)
                    for s in range(T):
                        sp.dma_start(u[GC * s:GC * (s + 1), :, :], ud[s]).then_inc(s_uin, 16)
                if kind == "S":
                    sp.wait_ge(s_kdma, c + 1)
                    for s in range(T):
                        sp.dma_start(toep[GC * s:GC * (s + 1), :, :].rearrange("p g (t c) -> p g t c", c=GC),
                                     kf[:, :, T - s:2 * T - s, :]).then_inc(s_toep, 16)
                if kind == "Y":
                    sp.wait_ge(s_yev, 3 * (c + 1))
                    yd = io.yd[c * P:(c + 1) * P, :].rearrange("(g c) (t k) -> t c g k", g=GT, t=T)
                    for s in range(T):
                        sp.dma_start(yd[s], y[GC * s:GC * (s + 1), :, :]).then_inc(s_yout, 16)
                    sp.wait_ge(s_yout, 16 * T * (c + 1))
                    sp.dma_start(gT[:, c, :], io.yd[c * P:(c + 1) * P, :]).then_inc(s_yin, 16)
                weights(done + 3)
            n_out = 0
            sp.wait_ge(s_finc, 2)
            for k, (re, im) in enumerate(((io.out_ssm_re_p, io.out_ssm_im_p), (io.out_ssm_re_s, io.out_ssm_im_s))):
                sp.dma_start(re[0, 0], fo[:, k, 0:STATE]).then_inc(s_out, 16)
                sp.dma_start(im[0, 0], fo[:, k, STATE:P]).then_inc(s_out, 16)
                n_out += 2
            sp.wait_ge(s_out, 16 * n_out)
            sp.wait_ge(s_cvout, 16 * 4 * KH)
            sp.wait_ge(s_yin, 16 * KH)

        @block.scalar
        def _(act):
            n = 0
            for kind, c in order:
                if kind in ("u", "v", "gb"):
                    for (lo, ln) in TOK_CHUNKS:
                        i = first[(kind, c)] + TOK_CHUNKS.index((lo, ln))
                        act.wait_ge(s_proj, i + 1)
                        src = proj[:, i % 3, 0:ln]
                        if kind == "u":
                            dst = gT[:, c, :].rearrange("p (s k) -> p k s", s=T)[:, lo // T:(lo + ln) // T, :]
                            src = src.rearrange("p (k s) -> p k s", s=T)
                        elif kind == "v":
                            dst = v_sb[:, lo:lo + ln]
                            if c and lo == 0:
                                act.wait_ge(s_cv, c)
                        else:
                            dst = gb[:, lo:lo + ln]
                            if c and lo == 0:
                                act.wait_ge(s_conv, c)
                        act.activation(dst, src, ACT.Copy).then_inc(s_pact, 1)
                if kind == "T":
                    if c:
                        act.wait_ge(s_bu, 3 * c)
                    for h in range(2):
                        act.wait_ge(s_bpt, 2 * c + h + 1)
                        src = sb[:, h, :].rearrange("p (g q) -> p g q", g=4)
                        act.activation(bt[:, 4 * h:4 * h + 4, :], src, ACT.Copy).then_inc(s_bt, 1)
                        act.activation(btsw[:, 4 * h:4 * h + 4, 0:64], src[:, :, 64:128], ACT.Copy).then_inc(s_bt, 1)
                        act.activation(btsw[:, 4 * h:4 * h + 4, 64:128], src[:, :, 0:64], ACT.Copy).then_inc(s_bt, 1)
                if kind == "Y":
                    if c:
                        act.wait_ge(s_yout, 16 * T * c)
                    for j, (g0, gn) in enumerate(TRIPLES):
                        act.wait_ge(s_y, 3 * c + j + 1)
                        act.activation(y[:, g0:g0 + gn, :], sb[:, j, 0:gn * NK].rearrange("p (g k) -> p g k", g=gn),
                                       ACT.Copy).then_inc(s_yev, 1)

        @block.gpsimd
        def _(pool):
            link = chain(pool, s_g)
            def product(outr, outi, ar, ai, br, bi, t):
                link(pool.tensor_tensor(t[0], ar, br, ALU.mult))
                link(pool.tensor_tensor(t[1], ai, bi, ALU.mult))
                link(pool.tensor_tensor(t[2], ar, bi, ALU.mult))
                link(pool.tensor_tensor(t[3], ai, br, ALU.mult))
                link(pool.tensor_tensor(outr, t[0], t[1], ALU.subtract))
                link(pool.tensor_tensor(outi, t[2], t[3], ALU.add))

            def unit(c, s, t):
                link(pool.tensor_tensor(t[0], c, c, ALU.mult))
                link(pool.tensor_tensor(t[1], s, s, ALU.mult))
                link(pool.tensor_tensor(t[2], t[0], t[1], ALU.add))
                link(pool.tensor_scalar(t[2], t[2], -0.5, 1.5, ALU.mult, ALU.add))
                link(pool.tensor_tensor(c, c, t[2], ALU.mult))
                link(pool.tensor_tensor(s, s, t[2], ALU.mult))

            cr, ci, mg = (co.turn[:, k, :] for k in range(3))
            tmp = [q1[:, k * GROUPS:(k + 1) * GROUPS] for k in range(4)]
            for k in range(3):
                link(pool.tensor_tensor(mg, mg, mg, ALU.mult))
                product(cr, ci, cr, ci, cr, ci, tmp)
                unit(cr, ci, tmp)
            pool.tensor_copy(co.decay[:, :], mg).then_inc(s_decay, 1)
            for lvl in range(7):
                link(pool.tensor_copy(co.er[:, :, lvl], cr))
                link(pool.tensor_scalar(co.eis[:, :, lvl], ci, co.sign[:, 0:1], None, ALU.mult))
                if lvl < 6:
                    product(cr, ci, cr, ci, cr, ci, tmp)
                    unit(cr, ci, tmp)
            link(pool.memset(cv[:, 0:2], 0.0))
            link(pool.memset(hc[:, :, 0:1], 0.0))
            link(pool.memset(hs[:, :, 0:1], 0.0))
            link(pool.memset(hs[:, :, NKP:NKP + 1], 0.0))
            link(pool.memset(swap[:, :], 0.0))
            link(pool.affine_select(out=swap[:, :], in_=swap[:, :], compare_op=ALU.not_equal, fill=-1.0,
                                    base=-64, pattern=[[-1, P]], channel_multiplier=1))
            link(pool.affine_select(out=swap[:, :], in_=swap[:, :], compare_op=ALU.not_equal, fill=1.0,
                                    base=64, pattern=[[-1, P]], channel_multiplier=1))
            pool.wait_ge(s_small, 16 * 6)
            pool.tensor_tensor(dd[:, :, :], dd[:, :, :], bc(keep.ident[0:GC, 0:GC], 1, GROUPS),
                               ALU.mult).then_inc(s_const, 1)
            pool.wait_ge(s_const, 1)

            def new_cache(c):
                pool.wait_ge(s_cv, c + 1)
                with nc.allow_non_contiguous_dma(reason="a few columns"):
                    for dst, col in ((io.out_conv_p, N_PROMPT), (io.out_conv_s, N_TOK + 2)):
                        for k in range(2):
                            pool.dma_start(dst[0, 0, k, c * P:(c + 1) * P].rearrange("(p a) -> p a", a=1),
                                           cv[:, col + k:col + k + 1]).then_inc(s_cvout, 16)

            for c in range(KH):
                gs = slice(GT * c, GT * (c + 1))
                if c >= 2:
                    new_cache(c - 2)
                if c:
                    pool.wait_ge(s_app, c)
                link(pool.memset(cos[:, :, 0:1], 1.0))
                link(pool.memset(sin[:, :, 0:1], 0.0))
                for lvl in range(7):
                    n = 1 << lvl
                    er, ei = bc(co.er[:, gs, lvl], 2, n), bc(co.eis[:, gs, lvl], 2, n)
                    a, b = (t[:, 0:GT * n].rearrange("p (g k) -> p g k", g=GT) for t in (q1, q2))
                    link(pool.tensor_tensor(a, cos[:, :, 0:n], er, ALU.mult))
                    link(pool.tensor_tensor(b, sin[:, :, 0:n], ei, ALU.mult))
                    link(pool.tensor_tensor(cos[:, :, n:2 * n], a, b, ALU.subtract))
                    link(pool.tensor_tensor(a, sin[:, :, 0:n], er, ALU.mult))
                    link(pool.tensor_tensor(b, cos[:, :, 0:n], ei, ALU.mult))
                    link(pool.tensor_tensor(sin[:, :, n:2 * n], a, b, ALU.add))
                link(pool.tensor_copy(cos[:, :, NKP:NK], cos[:, :, 0:NK - NKP]))
                pool.tensor_copy(sin[:, :, NKP:NK], sin[:, :, 0:NK - NKP]).then_inc(s_tab, 1)
                pool.wait_ge(s_tab, c + 1)
            new_cache(KH - 2)
            new_cache(KH - 1)

        @block.tensor
        def _(pe):
            pn = 0
            for kind, c in order:
                if kind in column:
                    i = tiles.index((kind, c))
                    pe.wait_ge(s_w[i % RING], 16 * (i // RING + 1))
                    for lo, ln in TOK_CHUNKS:
                        if pn >= 3:
                            pe.wait_ge(*emptied[pn - 3])
                        for k in range(KD):
                            mm = pe.matmul(proj[:, pn % 3, 0:ln], win[:, i % RING, k, :], hT[:, k, lo:lo + ln],
                                           start=(k == 0), stop=(k == KD - 1))
                        mm.then_inc(s_proj, 1)
                        pn += 1
                if kind == "T":
                    pe.wait_ge(s_bp, c + 1)
                    if c:
                        pe.wait_ge(s_yev, 3 * c)
                    for h in range(2):
                        for q in range(4):
                            tr = pe.transpose(sb[:, h, q * P:(q + 1) * P], bp[:, 4 * h + q, :], keep.ident[:, :])
                        tr.then_inc(s_bpt, 1)
                if kind == "S":
                    pe.wait_ge(s_c, c + 1)
                    for h in range(2):
                        for q in range(4):
                            gi = 4 * h + q
                            mm = pe.matmul(sb[0:GC, 2 + h, q * P:(q + 1) * P], co.bb[:, GT * c + gi, :],
                                           c1[:, gi, 0:T * GC], start=True, stop=True)
                    mm.then_inc(s_k, 1)
                    pe.wait_ge(s_bt, 6 * (c + 1))
                    pe.wait_ge(s_uin, 16 * T * (c + 1))
                    for j, (g0, gn) in enumerate(TRIPLES):
                        a, b = (0, 1) if j % 2 == 0 else (2, 3)
                        if j == 1:
                            pe.wait_ge(s_kev, c + 1)
                        if j == 2:
                            pe.wait_ge(s_hch, 3 * c + 1)
                        for q in range(gn):
                            pe.matmul(sb[:, a, q * NK:(q + 1) * NK], bt[:, g0 + q, :], u[:, g0 + q, :],
                                      start=True, stop=True)
                        for q in range(gn):
                            mm = pe.matmul(sb[:, b, q * NK:(q + 1) * NK], btsw[:, g0 + q, :], u[:, g0 + q, :],
                                           start=True, stop=True)
                        mm.then_inc(s_bu, 1)
                if kind == "Y":
                    pe.wait_ge(s_toep, 16 * T * (c + 1))
                    pe.wait_ge(s_rot, c + 1)
                    for j, (g0, gn) in enumerate(TRIPLES):
                        for q in range(gn):
                            o, gi = sb[:, j, q * NK:(q + 1) * NK], g0 + q
                            pe.matmul(o, toep[:, gi, :], u[:, gi, :], start=True, stop=False)
                            pe.matmul(o, c1[:, gi, GC:(T + 1) * GC], hc[:, gi, :], start=False, stop=False)
                            mm = pe.matmul(o, c2[:, gi, :], hs[:, gi, :], start=False, stop=True)
                        mm.then_inc(s_y, 1)
            pe.wait_ge(s_fin, KH)
            for k in range(2):
                pe.matmul(misc[0:GROUPS, k * P:(k + 1) * P], fin[:, k, 0, :], keep.ident[:, :], start=True, stop=False)
                mm = pe.matmul(misc[0:GROUPS, k * P:(k + 1) * P], fin[:, k, 1, :], swap[:, :], start=False, stop=True)
            mm.then_inc(s_finp, 1)

        @block.vector
        def _(v):
            link = chain(v, s_v)
            tt, ts, stt = v.tensor_tensor, v.tensor_scalar, v.scalar_tensor_tensor
            v.wait_ge(s_small, 16 * 6)
            link(v.memset(kf[:, :, :, :], 0.0))

            def coefficients(c):
                gs = slice(GT * c, GT * (c + 1))
                a = t1[:, 0:GT * T * GC].rearrange("p (g s c) -> p g s c", g=GT, s=T)
                b = t2[:, 0:GT * T * GC].rearrange("p (g s c) -> p g s c", g=GT, s=T)

                def shaped(x, n):
                    return x[:, 0:GT * n * GC].rearrange("p (g s c) -> p g s c", g=GT, s=n)

                if c:
                    v.wait_ge(s_bpt, 2 * c)
                tt(a, bc(co.bb[:, gs, :], 2, T), bc(co.pr[:, gs, 0:T][:, :, ::-1], 3, GC), ALU.mult)
                link(tt(b, bc(co.bbsw[:, gs, :], 2, T), bc(co.nsi[:, gs, 0:T][:, :, ::-1], 3, GC), ALU.mult))
                link(tt(bp[:, :, :].rearrange("p g (s c) -> p g s c", c=GC), a, b, ALU.subtract), s_bp)
                if c:
                    v.wait_ge(s_y, 3 * c)
                cs = co.cs[:, P * c:P * (c + 1)].rearrange("p (g c) -> p g c", c=GC)
                csw = co.csw[:, P * c:P * (c + 1)].rearrange("p (g c) -> p g c", c=GC)
                a9, b9 = shaped(t1, T + 1), shaped(t2, T + 1)
                link(tt(a9, bc(cs, 2, T + 1), bc(co.prs[:, gs, :], 3, GC), ALU.mult))
                link(tt(b9, bc(csw, 2, T + 1), bc(co.npi[:, gs, :], 3, GC), ALU.mult))
                link(tt(c1[:, :, :].rearrange("p g (s c) -> p g s c", c=GC), a9, b9, ALU.add))
                tt(a, bc(cs, 2, T), bc(co.npi[:, gs, 1:], 3, GC), ALU.mult)
                link(tt(b, bc(csw, 2, T), bc(co.prs[:, gs, 1:], 3, GC), ALU.mult))
                link(tt(c2[:, :, :].rearrange("p g (s c) -> p g s c", c=GC), a, b, ALU.subtract), s_c)
                v.wait_ge(s_decay, 1)
                link(v.tensor_copy(dec[:, :, :], bc(co.decay[:, gs], 2, NK)))
                v.memset(dec[:, :, 0:1], 0.0)
                link(v.memset(dec[:, :, NKP:NKP + 1], 0.0))

            def lags(c):
                gs = slice(GT * c, GT * (c + 1))
                v.wait_ge(s_k, c + 1)
                v.wait_ge(s_const, 1)
                if c:
                    v.wait_ge(s_toep, 16 * T * c)
                for h in range(2):
                    cp = v.tensor_copy(kf[:, 4 * h:4 * h + 4, T:2 * T, :],
                                       sb[0:GC, 2 + h, :].rearrange("p (g s c) -> p g s c", g=4, s=T))
                cp.then_inc(s_kev, 1)
                v.wait_ge(s_kev, c + 1)
                tt(kf[:, :, T, :], kf[:, :, T, :], dd[:, gs, :], ALU.add).then_inc(s_kdma, 1)

            def scan(c):
                gs = slice(GT * c, GT * (c + 1))
                v.wait_ge(s_tab, c + 1)
                for j, (g0, gn) in enumerate(TRIPLES):
                    a, b = (0, 1) if j % 2 == 0 else (2, 3)
                    v.wait_ge(s_bu, 3 * c + j + 1)
                    x1 = t1[:, g0 * NK:(g0 + gn) * NK].rearrange("p (g k) -> p g k", g=gn)
                    x2 = t2[:, g0 * NK:(g0 + gn) * NK].rearrange("p (g k) -> p g k", g=gn)
                    pa = sb[:, a, 0:gn * NK].rearrange("p (g k) -> p g k", g=gn)
                    pb = sb[:, b, 0:gn * NK].rearrange("p (g k) -> p g k", g=gn)
                    tt(x1, pa, cos[:, g0:g0 + gn, :], ALU.mult)
                    link(tt(x2, pb, sin[:, g0:g0 + gn, :], ALU.mult), s_hch)
                flat = [x[:, 0:GT * NK].rearrange("p (g k) -> p g k", g=GT) for x in (t1, t2)]
                link(tt(w[:, :, :], flat[0], flat[1], ALU.add))
                link(tt(w[:, :, NKP], w[:, :, NKP], co.ah0[:, gs], ALU.add))
                link(v.tensor_tensor_scan(g[:, :, :].rearrange("p g k -> p (g k)"),
                                          dec[:, :, :].rearrange("p g k -> p (g k)"),
                                          w[:, :, :].rearrange("p g k -> p (g k)"), 0.0, ALU.mult, ALU.add))
                if c == 0:
                    v.wait_ge(s_const, 1)
                for dst, tab in ((hc, cos), (hs, sin)):
                    tt(dst[:, :, 1:NKP], g[:, :, 0:NKP - 1], tab[:, :, 0:NKP - 1], ALU.mult)
                    tt(dst[:, :, NKP + 1:NK], g[:, :, NKP:NK - 1], tab[:, :, NKP:NK - 1], ALU.mult)
                for k, last in enumerate((NKP - 1, NK - 1)):
                    tt(fin[:, k, 0, gs], g[:, :, last], cos[:, :, last], ALU.mult)
                    f = tt(fin[:, k, 1, gs], g[:, :, last], sin[:, :, last], ALU.mult)
                link(f, s_app)
                link(v.tensor_copy(hc[:, :, NKP], co.h0[:, gs]), s_rot)
                for k in range(2):
                    f = ts(fin[:, k, 1, gs], fin[:, k, 1, gs], co.sign[:, 0:1], None, ALU.mult)
                link(f, s_fin)

            def gate(c):
                for j, (lo, ln) in enumerate(TOK_CHUNKS):
                    i = first[("gc", c)] + j
                    v.wait_ge(s_proj, i + 1)
                    if j == 0:
                        v.wait_ge(s_pact, pact_after[("v", c)])
                        if c:
                            v.wait_ge(s_cvout, 16 * 4 * c)
                    for a, b, shift in ((lo, min(lo + ln, N_PROMPT), 2), (max(lo, N_PROMPT), lo + ln, 4)):
                        if a < b:
                            mu = tt(cv[:, a + shift:b + shift], proj[:, i % 3, a - lo:b - lo], v_sb[:, a:b], ALU.mult)
                    link(mu, s_pdve)
                link(v.tensor_copy(cv[:, SAMPLE:SAMPLE + 2], cacheT[:, c, :]), s_cv)

            def conv(c):
                v.wait_ge(s_const, 1)
                x = t1[:, 0:N_TOK + 2]
                n = N_TOK + 2
                link(ts(x, cv[:, 0:n], taps[:, c, 0:1], None, ALU.mult))
                link(stt(out=x, in0=cv[:, 1:n + 1], scalar=taps[:, c, 1:2], in1=x, op0=ALU.mult, op1=ALU.add))
                link(stt(out=x, in0=cv[:, 2:n + 2], scalar=taps[:, c, 2:3], in1=x, op0=ALU.mult, op1=ALU.add))
                v.wait_ge(s_pact, pact_after[("gb", c)])
                tt(ycT[:, c, 0:N_PROMPT], t1[:, 0:N_PROMPT], gb[:, 0:N_PROMPT], ALU.mult)
                link(tt(ycT[:, c, N_PROMPT:N_TOK], t1[:, SAMPLE:SAMPLE + N_SAMPLE], gb[:, N_PROMPT:N_TOK],
                        ALU.mult), s_conv)

            for kind, c in order:
                if kind == "T":
                    coefficients(c)
                if kind == "S":
                    lags(c)
                    scan(c)
                if kind == "gc":
                    gate(c)
                if kind == "gb":
                    conv(c)
            v.wait_ge(s_finp, 1)
            v.tensor_copy(fo[:, :, :].rearrange("p a b -> p (a b)"), misc[0:GROUPS, 0:2 * P]).then_inc(s_finc, 2)


def output_stage(nc, io, keep):
    with ExitStack() as ctx:
        m = Pools(nc, ctx, "out")
        w = Names()
        w.out_h, w.out_l = m.sb("wo_h", [P, KD, D], F32R), m.sb("wo_l", [P, KD, D], F32R)
        w.in_h, w.in_l = m.sb("wi_h", [P, KD, 2 * D_EXP], F32R), m.sb("wi_l", [P, KD, 2 * D_EXP], F32R)
        w.dn_h, w.dn_l = m.sb("wd_h", [P, 2, D], F32R), m.sb("wd_l", [P, 2, D], F32R)
        w.rt_h, w.rt_l = m.sb("wr_h", [P, KD, N_EXP], F32R), m.sb("wr_l", [P, KD, N_EXP], F32R)
        w.eps = m.sb("eps", [P, 2])
        w.rr = m.sb("rr", [P, N_TILES, 2])
        gate_stage(nc, io, keep, w)
        project_stage(nc, io, keep, w)


def gate_stage(nc, io, keep, w):
    with ExitStack() as ctx:
        m = Pools(nc, ctx, "glu")
        gT, ycT = keep.gT, keep.ycT
        gn = m.sb("gn", [P, KH, N_TOK])
        w_glu = m.sb("w_glu", [P, KH, D_HALF])
        bglu = m.sb("bglu", [P, KH])
        beta = m.sb("beta", [P, KD])
        sig = m.sb("sig", [P, 2, CW])
        sq = m.sb("sq", [P, 2, CW])
        sqt = keep.scores[:, :, :].rearrange("p t e -> p (t e)")
        raw = m.sb("raw", [P, 3, D])
        ssq = m.sb("ssq", [P, 2, ROWS])
        ones = m.sb("ones", [P, 1])
        pl = m.ps("pl", [P, 4, 512])
        pm = m.ps("pm", [P, 512])
        s_wg, s_small = m.sem("wg"), m.sem("small")
        s_raw = [m.sem(f"raw{k}") for k in range(3)]
        s_const, s_g, s_v = m.sem("const"), m.sem("gch"), m.sem("vch")
        s_gelu, s_glu, s_sig, s_mix, s_sq, s_added = (m.sem(n) for n in ("gelu", "glu", "sig", "mix", "sq", "added"))
        s_ysq, s_ss, s_rt, s_high = (m.sem(n) for n in ("ysq", "ss", "rt", "high"))
        s_low_dve, s_low_pool = m.sem("lowv"), m.sem("lowp")
        block = ctx.enter_context(nc.Block())
        glu = [(ch, mo) for ch in range(len(TOK_CHUNKS)) for mo in range(KH)]

        def added(n):
            return (KH - 1) * (n // KH) + n % KH

        PIECES = [("out", k) for k in range(KD)] + [("rt", 0)] + [("in", k) for k in range(KD // 2)] + [("dn", 0), ("dn", 1)]
        AFTER = [range(0), range(0, 1), range(1, 2), range(2, 4), range(4, 5), range(5, 7), range(7, 8), range(8, 10),
                 range(10, 11), range(11, 12), range(12, 13), range(13, 15)]
        DVE_PIECES = KD + 3

        def place(j):
            kind, k = PIECES[j]
            at = raw[:, j % 3, :]
            if kind == "out":
                return at, w.out_h[:, k, :], w.out_l[:, k, :]
            if kind == "dn":
                return at, w.dn_h[:, k, :], w.dn_l[:, k, :]
            if kind == "in":
                pair = slice(2 * k, 2 * k + 2)
                return at.rearrange("p (k n) -> p k n", k=2), w.in_h[:, pair, :], w.in_l[:, pair, :]
            return (at[:, 0:KD * N_EXP].rearrange("p (k n) -> p k n", k=KD), w.rt_h[:, :, :], w.rt_l[:, :, :])

        def loads(j):
            return sum(2 if PIECES[i][0] == "in" else 1 for i in range(j % 3, j + 1, 3))

        @block.sync
        def _(sp):
            sp.dma_start(w_glu[:, :, :], io.w_glu[0].rearrange("(k p) n -> p k n", p=P)).then_inc(s_wg, 16)
            with nc.allow_non_contiguous_dma(reason="per-channel rows"):
                sp.dma_start(bglu[:, :], io.b_glu[0].rearrange("(c p) -> p c", p=P)).then_inc(s_small, 16)
                sp.dma_start(beta[:, 0:KH], io.beta_ssm[0].rearrange("(c p) -> p c", p=P)).then_inc(s_small, 16)
                sp.dma_start(beta[:, KH:KD], io.beta_conv[0].rearrange("(c p) -> p c", p=P)).then_inc(s_small, 16)
            sources = {"out": io.w_out, "dn": io.ws_down}
            for j, (kind, k) in enumerate(PIECES):
                if j >= 3:
                    if j - 3 < DVE_PIECES:
                        sp.wait_ge(s_low_dve, j - 2)
                    else:
                        sp.wait_ge(s_low_pool, j - 2 - DVE_PIECES)
                at = place(j)[0]
                if kind == "in":
                    for half, src in enumerate((io.ws_gate, io.ws_up)):
                        src = src[0].rearrange("(k p) n -> p k n", p=P)[:, 2 * k:2 * k + 2, :]
                        sp.dma_start(at[:, :, D_EXP * half:D_EXP * (half + 1)], src).then_inc(s_raw[j % 3], 16)
                elif kind == "rt":
                    sp.dma_start(at, io.w_router[0].rearrange("(k p) n -> p k n", p=P)).then_inc(s_raw[j % 3], 16)
                else:
                    sp.dma_start(at, sources[kind][0, k * P:(k + 1) * P, :]).then_inc(s_raw[j % 3], 16)

        @block.scalar
        def _(act):
            act.wait_ge(s_const, 1)
            for c in range(KH):
                act.activation(gn[:, c, :].rearrange("p (k s) -> p s k", s=T),
                               gT[:, c, 0:N_TOK].rearrange("p (s k) -> p s k", s=T),
                               ACT.Gelu_apprx_tanh).then_inc(s_gelu, 1)
            act.wait_ge(s_small, 48)

            def square(n):
                ch, mo = glu[n]
                lo, ln = TOK_CHUNKS[ch]
                act.wait_ge(s_mix, n + 1)
                if n >= 3:
                    act.wait_ge(s_added, added(n - 2))
                dst = ssq[:, 0, lo:lo + ln] if mo == 0 else sq[:, n % 2, 0:ln]
                act.activation(dst, gT[:, mo, lo:lo + ln], ACT.Square).then_inc(s_sq, 1)

            def high(j):
                at, hi, _ = place(j)
                act.wait_ge(s_raw[j % 3], 16 * loads(j))
                scale = beta[:, j:j + 1] if PIECES[j][0] == "out" else 1.0
                act.activation(hi, at, ACT.Copy, scale=scale).then_inc(s_high, 1)

            for n, (ch, mo) in enumerate(glu):
                lo, ln = TOK_CHUNKS[ch]
                act.wait_ge(s_glu, n + 1)
                if n >= 2:
                    act.wait_ge(s_mix, n - 1)
                act.activation(sig[:, n % 2, 0:ln], pl[:, n % 4, 0:ln], ACT.Sigmoid,
                               bias=bglu[:, mo:mo + 1]).then_inc(s_sig, 1)
                if n:
                    square(n - 1)
                if n == len(glu) - 1:
                    square(n)
                for j in AFTER[n]:
                    high(j)
            act.wait_ge(s_ss, 1)
            act.activation(w.rr[:, :, :].rearrange("p a b -> p (a b)"), pm[:, 0:2 * N_TILES], ACT.Sqrt,
                           bias=w.eps[:, 0:1], scale=1.0 / D_HALF).then_inc(s_rt, 1)

        @block.gpsimd
        def _(pool):
            link = chain(pool, s_g)
            link(pool.memset(gT[:, :, N_TOK:], 0.0))
            link(pool.memset(ycT[:, :, N_TOK:], 0.0))
            link(pool.memset(ssq[:, :, N_TOK:], 0.0))
            link(pool.memset(ones[:, :], 1.0))
            link(pool.memset(w.eps[:, 0:1], RMS_EPS))
            pool.memset(w.eps[:, 1:2], LN_EPS).then_inc(s_const, 1)
            for lo, ln in TOK_CHUNKS:
                total = ssq[:, 1, lo:lo + ln]
                for c in range(KH):
                    y = ycT[:, c, lo:lo + ln]
                    link(pool.tensor_tensor(sqt[:, 0:ln] if c else total, y, y, ALU.mult))
                    if c:
                        link(pool.tensor_tensor(total, total, sqt[:, 0:ln], ALU.add))
            pool.sem_inc(s_ysq, 1)
            for j in range(DVE_PIECES, len(PIECES)):
                at, hi, lo = place(j)
                pool.wait_ge(s_high, j + 1)
                pool.tensor_tensor(lo, at, hi.bitcast(F32), ALU.subtract).then_inc(s_low_pool, 1)

        @block.tensor
        def _(pe):
            def squares(part, tiles):
                for i in tiles:
                    mm = pe.matmul(pm[:, 2 * i + part:2 * i + part + 1], ssq[:, part, i * P:(i + 1) * P], ones[:, :],
                                   start=True, stop=True)
                return mm

            pe.wait_ge(s_wg, 16)
            pe.wait_ge(s_gelu, KH)
            per = CW // P
            for n, (ch, mo) in enumerate(glu):
                lo, ln = TOK_CHUNKS[ch]
                if n >= 4:
                    pe.wait_ge(s_sig, n - 3)
                for k in range(KH):
                    mm = pe.matmul(pl[:, n % 4, 0:ln], w_glu[:, k, mo * P:(mo + 1) * P],
                                   gn[:, k, lo:lo + ln], start=(k == 0), stop=(k == KH - 1))
                mm.then_inc(s_glu, 1)
                if n == 2 * KH + 1:
                    pe.wait_ge(s_ysq, 1)
                    squares(1, range(N_TILES))
                if mo == KH - 1 and ch:
                    pe.wait_ge(s_added, added(KH * ch - 1))
                    squares(0, range(per * (ch - 1), per * ch))
            pe.wait_ge(s_added, added(len(glu) - 1))
            squares(0, range(per * 2, N_TILES)).then_inc(s_ss, 1)

        @block.vector
        def _(v):
            link = chain(v, s_v)
            tt, stt = v.tensor_tensor, v.scalar_tensor_tensor
            v.wait_ge(s_const, 1)
            v.wait_ge(s_gelu, KH)

            def add_square(n):
                ch, mo = glu[n]
                lo, ln = TOK_CHUNKS[ch]
                v.wait_ge(s_sq, n + 1)
                if mo:
                    if n >= 2:
                        v.wait_ge(s_added, added(n - 1))
                    tt(ssq[:, 0, lo:lo + ln], ssq[:, 0, lo:lo + ln], sq[:, n % 2, 0:ln], ALU.add).then_inc(s_added, 1)

            def low(j):
                at, hi, lo = place(j)
                v.wait_ge(s_high, j + 1)
                if PIECES[j][0] == "out":
                    stt(out=lo, in0=at, scalar=beta[:, j:j + 1], in1=hi.bitcast(F32), op0=ALU.mult,
                        op1=ALU.subtract).then_inc(s_low_dve, 1)
                else:
                    tt(lo, at, hi.bitcast(F32), ALU.subtract).then_inc(s_low_dve, 1)

            for n, (ch, mo) in enumerate(glu):
                lo, ln = TOK_CHUNKS[ch]
                v.wait_ge(s_sig, n + 1)
                tt(gT[:, mo, lo:lo + ln], gn[:, mo, lo:lo + ln], sig[:, n % 2, 0:ln], ALU.mult).then_inc(s_mix, 1)
                if n:
                    add_square(n - 1)
                for j in AFTER[n]:
                    if j < DVE_PIECES:
                        low(j)
            add_square(len(glu) - 1)
            v.wait_ge(s_rt, 1)
            link(v.reciprocal(w.rr[:, :, :], w.rr[:, :, :]))


def project_stage(nc, io, keep, w):
    with ExitStack() as ctx:
        m = Pools(nc, ctx, "proj")
        gT, ycT = keep.gT, keep.ycT
        lng, lnb = m.sb("lng", [P, D]), m.sb("lnb", [P, D])
        in_h, in_l = m.sb("in_h", [P, 2, KD, P], F32R), m.sb("in_l", [P, 2, KD, P], F32R)
        res = m.sb("res", [P, D])
        x = m.sb("x", [P, 3, D])
        x_h, x_l = m.sb("x_h", [P, KD, P], F32R), m.sb("x_l", [P, KD, P], F32R)
        stats = m.sb("stats", [P, 2, 6])
        mv = m.sb("mv", [P, 2])
        rs = m.sb("rs", [P, 2])
        sg = m.sb("sg", [P, D_EXP])
        hid = m.sb("hid", [P, D_EXP])
        hid_h, hid_l = m.sb("hid_h", [P, 2, P], F32R), m.sb("hid_l", [P, 2, P], F32R)
        po = m.ps("po", [P, 2, 2, 512])
        pt = m.ps("pt", [P, 2, 512])
        pg = m.ps("pg", [P, 512])
        pm = m.ps("pm", [P, 512])
        s_ln, s_v = m.sem("ln"), m.sem("vch")
        s_res, s_tok, s_acc = m.sem("res"), [m.sem(f"tok{k}") for k in range(3)], [
            m.sem(f"acc{k}") for k in range(3)]
        s_alpha = m.sem("alpha")
        s_inh, s_inl, s_po, s_z, s_zd, s_std, s_rstd, s_nm, s_gain, s_x = (
            m.sem(n) for n in ("inh", "inl", "po", "z", "zd", "std", "rstd", "nm", "gain", "x"))
        s_tr, s_xh, s_xl, s_rl, s_lg, s_pg, s_silu, s_hid, s_ht, s_hh, s_hl, s_pd, s_ao = (
            m.sem(n) for n in ("tr", "xh", "xl", "rl", "lg", "pg", "silu", "hid", "ht", "hh", "hl", "pd", "ao"))
        block = ctx.enter_context(nc.Block())
        steps = range(N_TILES + 2)

        @block.sync
        def _(sp):
            sp.dma_start(res[:, :], io.resid[0:P, :]).then_inc(s_res, 16)
            sp.dma_start(lng[:, :], io.ln1_g[0].partition_broadcast(P)).then_inc(s_ln, 16)
            sp.dma_start(lnb[:, :], io.ln1_b[0].partition_broadcast(P)).then_inc(s_ln, 16)
            for i in range(1, N_TILES):
                sp.wait_ge(s_z, 2 * i)
                sp.dma_start(res[:, :], io.resid[i * P:(i + 1) * P, :]).then_inc(s_res, 16)

        @block.scalar
        def _(act):
            def in_high(i):
                if i >= 2:
                    act.wait_ge(s_po, 2 * (i - 1))
                for part, src in enumerate((gT, ycT)):
                    act.activation(in_h[:, i % 2, KH * part:KH * (part + 1), :], src[:, :, i * P:(i + 1) * P],
                                   ACT.Copy).then_inc(s_inh, 1)

            def hid_high(i):
                act.wait_ge(s_ht, i + 1)
                if i:
                    act.wait_ge(s_pd, 2 * i)
                act.activation(hid_h[:, :, :], pm[:, 128:384].rearrange("p (k t) -> p k t", k=2),
                               ACT.Copy).then_inc(s_hh, 1)

            def x_high(i):
                if i:
                    act.wait_ge(s_pg, i)
                for h in range(2):
                    act.wait_ge(s_tr, 2 * i + h + 1)
                    act.activation(x_h[:, 4 * h:4 * h + 4, :], pt[:, h, :].rearrange("p (k t) -> p k t", k=4),
                                   ACT.Copy).then_inc(s_xh, 1)

            def normalise(i):
                act.wait_ge(s_zd, i + 1)
                act.activation(rs[:, 0:1], mv[:, 1:2], ACT.Sqrt, bias=w.eps[:, 1:2]).then_inc(s_std, 1)
                act.wait_ge(s_rstd, i + 1)
                act.activation(x[:, i % 3, :], x[:, i % 3, :], ACT.Identity, bias=rs[:, 1:2],
                               scale=rs[:, 0:1]).then_inc(s_nm, 1)

            def silu(i):
                act.wait_ge(s_rl, i + 1)
                act.activation(keep.scores[:, i, :], pm[:, 0:N_EXP], ACT.Copy).then_inc(s_lg, 1)
                act.wait_ge(s_pg, i + 1)
                if i:
                    act.wait_ge(s_hid, i)
                act.activation(sg[:, :], pg[:, 0:D_EXP], ACT.Silu).then_inc(s_silu, 1)

            def residual(i):
                act.wait_ge(s_res, 16 * (i + 1))
                act.mul(res[:, :], res[:, :], ALPHA).then_inc(s_alpha, 1)

            in_high(0)
            residual(0)
            for i in steps:
                if i + 1 < N_TILES:
                    in_high(i + 1)
                if i >= 2:
                    hid_high(i - 2)
                if 1 <= i <= N_TILES:
                    x_high(i - 1)
                if i < N_TILES:
                    normalise(i)
                if 1 <= i <= N_TILES:
                    silu(i - 1)
                if i + 1 < N_TILES:
                    residual(i + 1)

        @block.gpsimd
        def _(pool):
            pool.wait_ge(s_ln, 32)
            for i in steps:
                if i < N_TILES:
                    pool.wait_ge(s_gain, i + 1)
                    pool.tensor_tensor(x[:, i % 3, :], x[:, i % 3, :], lnb[:, :], ALU.add).then_inc(s_x, 1)
                    pool.wait_ge(s_x, i + 1)
                    pool.dma_start(io.tok[i * P:(i + 1) * P, :], x[:, i % 3, :]).then_inc(s_tok[i % 3], 16)
                if i >= 2:
                    j = i - 2
                    pool.wait_ge(s_ao, 2 * j + 2)
                    pool.dma_start(io.acc[j * P:(j + 1) * P, :], x[:, j % 3, :]).then_inc(s_acc[j % 3], 16)
            for k in range(3):
                pool.wait_ge(s_tok[k], 16 * len(range(k, N_TILES, 3)))
                pool.wait_ge(s_acc[k], 16 * len(range(k, N_TILES, 3)))

        @block.tensor
        def _(pe):
            def split_product(out, a, b, free):
                (ah, al), (bh, bl) = a, b
                terms = [(s[:, k, :], t[:, k, free]) for k in range(ah.shape[1])
                         for s, t in ((ah, bh), (ah, bl), (al, bh))]
                for i, (s, t) in enumerate(terms):
                    mm = pe.matmul(out, s, t, start=(i == 0), stop=(i == len(terms) - 1))
                return mm

            def project(i, h):
                n = 2 * i + h
                pe.wait_ge(s_inl, i + 1)
                if n >= 2:
                    pe.wait_ge(s_z, n - 1)
                for part in range(2):
                    ks = slice(KH * part, KH * (part + 1))
                    mm = split_product(po[:, n % 2, part, :], (in_h[:, i % 2, ks, :], in_l[:, i % 2, ks, :]),
                                       (w.out_h[:, ks, :], w.out_l[:, ks, :]), slice(512 * h, 512 * (h + 1)))
                mm.then_inc(s_po, 1)

            def turn_hid(i):
                pe.wait_ge(s_hid, i + 1)
                if i:
                    pe.wait_ge(s_hl, i)
                for k in range(2):
                    tr = pe.transpose(pm[:, 128 + k * P:128 + (k + 1) * P], hid[:, k * P:(k + 1) * P], keep.ident[:, :])
                tr.then_inc(s_ht, 1)

            def turn_x(i):
                pe.wait_ge(s_x, i + 1)
                for h in range(2):
                    if i >= 2:
                        pe.wait_ge(s_ao, 2 * (i - 2) + h + 1)
                    for k in range(4):
                        tr = pe.transpose(pt[:, h, k * P:(k + 1) * P], x[:, i % 3, (4 * h + k) * P:(4 * h + k + 1) * P],
                                          keep.ident[:, :])
                    tr.then_inc(s_tr, 1)

            def down(i):
                pe.wait_ge(s_hl, i + 1)
                if i + 1 < N_TILES:
                    pe.wait_ge(s_xl, i + 2)
                else:
                    pe.wait_ge(s_ao, 2 * i)
                for h in range(2):
                    split_product(pt[:, h, :], (hid_h, hid_l), (w.dn_h, w.dn_l),
                                  slice(512 * h, 512 * (h + 1))).then_inc(s_pd, 1)

            def enter(i):
                pe.wait_ge(s_xl, i + 1)
                if i:
                    pe.wait_ge(s_lg, i)
                    pe.wait_ge(s_hid, i)
                split_product(pm[:, 0:N_EXP], (x_h, x_l), (w.rt_h, w.rt_l), slice(0, N_EXP)).then_inc(s_rl, 1)
                split_product(pg[:, :], (x_h, x_l), (w.in_h, w.in_l), slice(0, 2 * D_EXP)).then_inc(s_pg, 1)

            for i in steps:
                if i < N_TILES:
                    project(i, 0)
                if i >= 2:
                    turn_hid(i - 2)
                if 1 <= i <= N_TILES:
                    turn_x(i - 1)
                if i < N_TILES:
                    project(i, 1)
                if i >= 2:
                    down(i - 2)
                if 1 <= i <= N_TILES:
                    enter(i - 1)

        @block.vector
        def _(v):
            link = chain(v, s_v)
            tt, stt = v.tensor_tensor, v.scalar_tensor_tensor

            def in_low(i):
                for part, src in enumerate((gT, ycT)):
                    ks = slice(KH * part, KH * (part + 1))
                    v.wait_ge(s_inh, 2 * i + part + 1)
                    low = tt(in_l[:, i % 2, ks, :], src[:, :, i * P:(i + 1) * P], in_h[:, i % 2, ks, :].bitcast(F32),
                             ALU.subtract)
                low.then_inc(s_inl, 1)

            def total(i, h):
                n = 2 * i + h
                cols = slice(512 * h, 512 * (h + 1))
                if h == 0:
                    v.wait_ge(s_alpha, i + 1)
                    if i >= 3:
                        v.wait_ge(s_acc[i % 3], 16 * (i // 3))
                v.wait_ge(s_po, n + 1)
                z = x[:, i % 3, cols]
                link(stt(out=z, in0=po[:, n % 2, 0, :], scalar=w.rr[:, i, 0:1], in1=res[:, cols],
                         op0=ALU.mult, op1=ALU.add))
                link(stt(out=z, in0=po[:, n % 2, 1, :], scalar=w.rr[:, i, 1:2], in1=z, op0=ALU.mult, op1=ALU.add), s_z)
                link(v.bn_stats(stats[:, h, :], z))

            def norm(i):
                link(v.bn_aggr(mv[:, :], stats[:, :, :]), s_zd)
                v.wait_ge(s_std, i + 1)
                link(v.reciprocal(rs[:, 0:1], rs[:, 0:1]))
                link(stt(out=rs[:, 1:2], in0=mv[:, 0:1], scalar=-1.0, in1=rs[:, 0:1], op0=ALU.mult, op1=ALU.mult),
                     s_rstd)
                v.wait_ge(s_nm, i + 1)
                if i == 0:
                    v.wait_ge(s_ln, 32)
                tt(x[:, i % 3, :], x[:, i % 3, :], lng[:, :], ALU.mult).then_inc(s_gain, 1)

            def hid_low(i):
                v.wait_ge(s_hh, i + 1)
                tt(hid_l[:, :, :], pm[:, 128:384].rearrange("p (k t) -> p k t", k=2), hid_h[:, :, :].bitcast(F32),
                   ALU.subtract).then_inc(s_hl, 1)

            def x_low(i):
                for h in range(2):
                    v.wait_ge(s_xh, 2 * i + h + 1)
                    low = tt(x_l[:, 4 * h:4 * h + 4, :], pt[:, h, :].rearrange("p (k t) -> p k t", k=4),
                             x_h[:, 4 * h:4 * h + 4, :].bitcast(F32), ALU.subtract)
                low.then_inc(s_xl, 1)

            def hidden(i):
                v.wait_ge(s_silu, i + 1)
                if i:
                    v.wait_ge(s_ht, i)
                tt(hid[:, :], sg[:, :], pg[:, D_EXP:], ALU.mult).then_inc(s_hid, 1)

            def add_shared(i):
                v.wait_ge(s_tok[i % 3], 16 * (i // 3 + 1))
                for h in range(2):
                    cols = slice(512 * h, 512 * (h + 1))
                    v.wait_ge(s_pd, 2 * i + h + 1)
                    stt(out=x[:, i % 3, cols], in0=x[:, i % 3, cols], scalar=ALPHA, in1=pt[:, h, :], op0=ALU.mult,
                        op1=ALU.add).then_inc(s_ao, 1)

            in_low(0)
            for i in steps:
                if i < N_TILES:
                    total(i, 0)
                if i >= 2:
                    hid_low(i - 2)
                if 1 <= i <= N_TILES:
                    x_low(i - 1)
                if i + 1 < N_TILES:
                    in_low(i + 1)
                if i < N_TILES:
                    total(i, 1)
                    norm(i)
                if i >= 2:
                    add_shared(i - 2)
                if 1 <= i <= N_TILES:
                    hidden(i - 1)


def routing_stage(nc, io, keep, rt):
    with ExitStack() as ctx:
        m = Pools(nc, ctx, "route")
        NT, NE, NG = N_TILES, N_EXP, N_EGRP
        bias = m.sb("bias", [P, NE])
        sc = m.sb("sc", [P, NT, NE])
        BIG, TAKEN = 3e38, -2e38
        sel = m.sb("sel", [P, NT, NE + 2])
        left = m.sb("left", [P, NT, NE + 2])
        g8 = m.sb("g8", [P, NT, NG, 8])
        gs = m.sb("gs", [P, NT, NG])
        gt, ge = m.sb("gt", [P, NT, NG, NG]), m.sb("ge", [P, NT, NG, NG])
        lower = m.sb("lower", [P, NG, NG])
        gm = m.sb("gm", [P, NT, NG])
        pen = m.sb("pen", [P, NT, NG])
        t8 = m.sb("t8", [P, NT, 8])
        mask = m.sb("mask", [P, NT, NE])
        mask_b = m.sb("mask_b", [P, NT, NE], BF16)
        wsum = m.sb("wsum", [P, NT])
        wt = m.sb("wt", [P, NT, NE])
        rest = m.sb("rest", [P, NT, NE])
        upper = m.sb("upper", [P, P], BF16)
        ones_b = m.sb("ones_b", [P, P], BF16)
        pos = m.sb("pos", [P, NT, NE])
        limits = m.sb("limits", [P, NT - 1])
        above = m.sb("above", [P, NE, NT - 1])
        nblk, ends, cmp = m.sb("nblk", [P, NE]), m.sb("ends", [P, NE]), m.sb("cmp", [P, NE])
        one_e = m.sb("one_e", [P, NE])
        row = m.sb("row", [P, 1])
        eo, jo, over, tmp1 = (m.sb(n, [P, 1]) for n in ("eo", "jo", "over", "tmp1"))
        evens = m.sb("evens", [1, 64])
        tabf = m.sb("tabf", [1, 4, P])
        whole = m.sb("whole", [P, 1])
        odd, third = m.sb("odd", [P, 1]), m.sb("third", [P, 1])
        slot_i = m.sb("slot_i", [P, P * SLOT_SETS], I32)
        ps = m.ps("ps", [P, 3, 512])
        pt = m.ps("pt", [P, 512])
        s_bias, s_const, s_g, s_v = m.sem("bias"), m.sem("const"), m.sem("gch"), m.sem("vch")
        s_sig, s_mask, s_pos, s_eo, s_t = (m.sem(n) for n in ("sig", "mask", "pos", "eo", "t"))
        s_lower, s_sum = m.sem("lower"), m.sem("sum")
        block = ctx.enter_context(nc.Block())
        HALVES = [(0, 5), (5, 4)]

        @block.sync
        def _(sp):
            sp.dma_start(bias[:, :], io.router_bias[0].partition_broadcast(P)).then_inc(s_bias, 16)
            for e in range(UP_SLOTS):
                for side, src, sem in ((0, io.w_gate, rt.gate_in), (1, io.w_up, rt.up_in)):
                    if e:
                        sp.wait_ge(sem, 16 * e)
                    sp.dma_start(rt.raw_up[:, e, :, D_EXP * side:D_EXP * (side + 1)],
                                 src[0, e].rearrange("(k p) n -> p k n", p=P)).then_inc(sem, 16)
                if e == 1:
                    sp.wait_ge(rt.down_in, 16)
                if e < 2:
                    sp.dma_start(rt.raw_dn[:, e, :, :], io.w_down[0, e].rearrange("(k p) n -> p k n", p=P)).then_inc(
                        rt.down_in, 16)

        @block.scalar
        def _(act):
            act.activation(sc[:, :, :], keep.scores[:, :, :], ACT.Sigmoid).then_inc(s_sig, 1)

        @block.gpsimd
        def _(pool):
            link = chain(pool, s_g)
            link(pool.memset(lower[:, :, :], 1.0))
            link(pool.affine_select(out=lower[:, :, :], in_=lower[:, :, :], compare_op=ALU.is_gt, fill=0.0, base=0,
                                    pattern=[[1, NG], [-1, NG]], channel_multiplier=0))
            pool.sem_inc(s_lower, 1)
            link(pool.iota(slot_i[:, :], pattern=[[1, P * SLOT_SETS]], base=0, channel_multiplier=0))
            link(pool.tensor_copy(rt.slot[:, :], slot_i[:, :]))
            link(pool.tensor_scalar(limits[:, :], rt.slot[:, 0:NT - 1], float(P), float(P) + 0.5, ALU.mult, ALU.add))
            link(pool.iota(slot_i[:, 0:1], pattern=[[1, 1]], base=0, channel_multiplier=1))
            link(pool.tensor_copy(row[:, :], slot_i[:, 0:1]))
            link(pool.tensor_scalar(rt.dummy[:, :], row[:, :], float(ROWS), None, ALU.add))
            link(pool.memset(one_e[:, :], 1.0))
            link(pool.tensor_scalar(evens[:, :], rt.slot[0:1, 0:64], 2.0, 1.5, ALU.mult, ALU.add))
            for tile in range(NT):
                link(pool.memset(rt.vals[:, 0, tile, 1:2], float(tile)))
            link(pool.tensor_copy(rt.vals[:, 0, :, 0:1], row[:, 0:1].unsqueeze(1).to_broadcast([P, NT, 1])))
            link(pool.memset(rt.vals[:, 0, :, 2:3], 1.0))
            link(pool.tensor_copy(rt.vals[:, 1, :, 0:3], rt.vals[:, 0, :, 0:3]))
            link(pool.memset(ones_b[:, :], 1.0))
            link(pool.affine_select(out=upper[:, :], in_=ones_b[:, :], compare_op=ALU.is_gt, fill=0.0, base=0,
                                    pattern=[[1, P]], channel_multiplier=-1))
            pool.memset(rt.tab[:, :, :], 0).then_inc(s_const, 1)
            pool.wait_ge(s_sum, 1)
            link(pool.tensor_tensor(wt[:, :, :], wt[:, :, :], bc(wsum[:, :], 2, NE), ALU.mult))
            src = wt
            for k in range(3):
                link(pool.tensor_copy(rt.parts[:, :, :, k], src[:, :, :]))
                if k < 2:
                    link(pool.tensor_tensor(rest[:, :, :], src[:, :, :], rt.parts[:, :, :, k], ALU.subtract))
                    src = rest

        @block.tensor
        def _(pe):
            pe.wait_ge(s_const, 1)
            pe.wait_ge(s_mask, 1)
            for k, (lo, n) in enumerate(HALVES):
                pe.matmul(ps[:, k, 0:n * NE], upper[:, :], mask_b[:, lo:lo + n, :].rearrange("p a b -> p (a b)"),
                          start=True, stop=False)
                for j in range(lo + n - 1):
                    a = max(j + 1, lo)
                    for i in range(a, lo + n):
                        pe.matmul(ps[:, k, (i - lo) * NE:(i - lo + 1) * NE], ones_b[:, :], mask_b[:, j, :],
                                  start=False, stop=(j == lo + n - 2))
            for j in range(NT):
                mm = pe.matmul(ps[:, 2, 0:NE], ones_b[:, :], mask_b[:, j, :], start=(j == 0), stop=(j == NT - 1))
            mm.then_inc(s_pos, 1)
            pe.wait_ge(s_eo, 1)
            pe.transpose(pt[0:1, 0:P], eo[:, 0:1], keep.ident[:, :])
            pe.transpose(pt[0:1, P:2 * P], jo[:, 0:1], keep.ident[:, :])
            pe.transpose(pt[0:1, 2 * P:3 * P], odd[:, 0:1], keep.ident[:, :])
            pe.transpose(pt[0:1, 3 * P:4 * P], third[:, 0:1], keep.ident[:, :]).then_inc(s_t, 1)

        @block.vector
        def _(v):
            link = chain(v, s_v)
            tt, ts, stt = v.tensor_tensor, v.tensor_scalar, v.scalar_tensor_tensor
            v.wait_ge(s_bias, 16)
            v.wait_ge(s_sig, 1)
            link(v.memset(sel[:, :, NE:], BIG))
            link(tt(sel[:, :, 0:NE], sc[:, :, :], bc(bias[:, :], 1, NT), ALU.add))
            per = NE // NG
            for i in range(NT):
                for g in range(NG):
                    mx = v.max(g8[:, i, g, :], sel[:, i, per * g:per * (g + 1)])
            link(mx)
            link(tt(gs[:, :, :], g8[:, :, :, 0], g8[:, :, :, 1], ALU.add))
            other, own = bc(gs[:, :, :], 2, NG), bc(gs[:, :, :], 3, NG)
            tt(gt[:, :, :, :], other, own, ALU.is_gt)
            link(tt(ge[:, :, :, :], other, own, ALU.is_equal))
            v.wait_ge(s_lower, 1)
            for i in range(NT):
                lo = tt(ge[:, i, :, :], ge[:, i, :, :], lower[:, :, :], ALU.mult)
            link(lo)
            link(tt(gt[:, :, :, :], gt[:, :, :, :], ge[:, :, :, :], ALU.add))
            link(v.reduce_sum(gm[:, :, :], gt[:, :, :, :], axis=mybir.AxisListType.X))
            link(ts(gm[:, :, :], gm[:, :, :], TOP_GROUPS - 0.5, None, ALU.is_lt))
            link(ts(pen[:, :, :], gm[:, :, :], 1e30, -1e30, ALU.mult, ALU.add))
            sel4 = sel[:, :, 0:NE].rearrange("p t (g e) -> p t g e", g=NG)
            link(tt(sel4, sel4, bc(gm[:, :, :], 3, per), ALU.mult))
            link(tt(sel4, sel4, bc(pen[:, :, :], 3, per), ALU.add))
            for i in range(NT):
                mx = v.max(t8[:, i, :], sel[:, i, 0:NE])
            link(mx)
            link(v.memset(t8[:, :, TOP_K:], BIG))
            for i in range(NT):
                mr = v.match_replace(left[:, i, :], t8[:, i, :], sel[:, i, :], TAKEN)
            link(mr)
            link(ts(mask[:, :, :], left[:, :, 0:NE], TAKEN / 2, None, ALU.is_lt))
            link(v.memset(mask[LAST_ROWS:P, NT - 1, :], 0.0))
            link(v.tensor_copy(mask_b[:, :, :], mask[:, :, :]), s_mask)
            link(tt(wt[:, :, :], sc[:, :, :], mask[:, :, :], ALU.mult))
            link(v.reduce_sum(wsum[:, :], wt[:, :, :], axis=mybir.AxisListType.X))
            link(ts(wsum[:, :], wsum[:, :], 1e-30, None, ALU.max))
            link(v.reciprocal(wsum[:, :], wsum[:, :]))
            link(ts(wsum[:, :], wsum[:, :], ROUTED_SCALE, None, ALU.mult), s_sum)
            v.wait_ge(s_pos, 1)
            v.wait_ge(s_const, 1)
            link(tt(above[:, :, :], bc(ps[:, 2, 0:NE], 2, NT - 1), bc(limits[:, :], 1, NE), ALU.is_gt))
            link(v.reduce_sum(nblk[:, :], above[:, :, :], axis=mybir.AxisListType.X))
            link(ts(nblk[:, :], nblk[:, :], 1.0, None, ALU.add))
            link(v.tensor_tensor_scan(ends[:, :], one_e[:, :], nblk[:, :], 0.0, ALU.mult, ALU.add))
            link(ts(cmp[:, :], ends[:, :], row[:, 0:1], None, ALU.is_le))
            link(v.reduce_sum(eo[:, :], cmp[:, :], axis=mybir.AxisListType.X))
            link(tt(cmp[:, :], cmp[:, :], nblk[:, :], ALU.mult))
            link(v.reduce_sum(tmp1[:, :], cmp[:, :], axis=mybir.AxisListType.X))
            link(tt(jo[:, :], row[:, :], tmp1[:, :], ALU.subtract))
            link(tt(over[:, :], row[:, :], ends[:, NE - 1:NE], ALU.is_ge))
            link(ts(eo[:, :], eo[:, :], float(NE - 1), None, ALU.min))
            for slot, n in ((odd, 2), (third, 3)):
                link(ts(whole[:, :], eo[:, :], 1.0 / n, 0.5 / n - 0.5, ALU.mult, ALU.add))
                link(ts(whole[:, :], whole[:, :], ROUND, None, ALU.add))
                link(ts(whole[:, :], whole[:, :], ROUND, None, ALU.subtract))
                link(stt(out=slot[:, :], in0=whole[:, :], scalar=-float(n), in1=eo[:, :], op0=ALU.mult, op1=ALU.add))
            link(ts(over[:, :], over[:, :], 1000.0, None, ALU.mult))
            link(tt(jo[:, :], jo[:, :], over[:, :], ALU.add))
            link(ts(jo[:, :], jo[:, :], float(SLOT_SETS - 1), None, ALU.min))
            link(ts(jo[:, :], jo[:, :], float(P), None, ALU.mult), s_eo)
            for k, (lo, n) in enumerate(HALVES):
                p = ts(pos[:, lo:lo + n, :], ps[:, k, 0:n * NE].rearrange("p (a b) -> p a b", a=n), 1.0, None, ALU.add)
            link(p)
            link(tt(pos[:, :, :], pos[:, :, :], mask[:, :, :], ALU.mult))
            link(ts(rt.posm[:, :, :], pos[:, :, :], -1.0, None, ALU.add))
            v.wait_ge(s_t, 1)
            link(v.tensor_copy(rt.tab[0:1, 0:4, 0:P], pt[0:1, 0:4 * P].rearrange("p (k n) -> p k n", k=4)))
            link(v.tensor_copy(tabf[0:1, 3, 0:NE], ends[0:1, :]))
            link(v.tensor_copy(rt.tab[0:1, 4, 0:NE], tabf[:, 3, 0:NE]))
            link(tt(evens[:, :], evens[:, :], ends[0:1, NE - 1:NE].to_broadcast([1, 64]), ALU.is_lt))
            link(v.reduce_sum(tmp1[0:1, :], evens[:, :], axis=mybir.AxisListType.X))
            link(ts(tmp1[0:1, :], tmp1[0:1, :], 2.0, None, ALU.mult))
            link(v.tensor_copy(rt.tab[0:1, 5, 0:1], tmp1[0:1, :]))


def expert_stage(nc, io, keep, rt):
    with ExitStack() as ctx:
        m = Pools(nc, ctx, "moe")
        raw_up, raw_dn = rt.raw_up, rt.raw_dn
        up_h, up_l = m.sb("up_h", [P, 2, KD, 2 * D_EXP], F32R), m.sb("up_l", [P, 2, KD, 2 * D_EXP], F32R)
        dn_h, dn_l = m.sb("dn_h", [P, 2, D], F32R), m.sb("dn_l", [P, 2, D], F32R)
        pick = m.sb("pick", [P, 2, N_TILES, P], BF16)
        info = m.sb("info", [P, 8])
        tmp = m.sb("tmp", [P, 2])
        idx_g, idx_s = m.sb("idx_g", [P, 2], I32), m.sb("idx_s", [P, 2], I32)
        new, cur = m.sb("new", [P, 2, 2]), m.sb("cur", [P, 2, 2])
        xg = m.sb("xg", [P, 2, D])
        x_h, x_l = m.sb("x_h", [P, 2, KD, P], F32R), m.sb("x_l", [P, 2, KD, P], F32R)
        sg = m.sb("sg", [P, 2, D_EXP])
        hid = m.sb("hid", [P, 2, D_EXP])
        hid_h, hid_l = m.sb("hid_h", [P, 2, 2, P], F32R), m.sb("hid_l", [P, 2, 2, P], F32R)
        y = m.sb("y", [P, 2, D])
        p_gu = m.ps("p_gu", [P, 2, 512])
        p_dn = m.ps("p_dn", [P, 2, 512])
        p_tr = m.ps("p_tr", [P, 2, 512])
        p_ht = m.ps("p_ht", [P, 512])
        p_im = m.ps("p_im", [P, 512])
        up_done, down_done, x_turned, info_done, hid_turned = (m.sem(n) for n in ("gu", "dn", "tr", "im", "ht"))
        silu_done, xh_done, y_act, up_h_done, dn_h_done, hidh_done = (
            m.sem(n) for n in ("silu", "xh", "ya", "uph", "dnh", "hh"))
        pick_done, hid_done, xl_done, hidl_done, idx_done, rows_done, up_l_dve, dn_l_dve, s_v = (
            m.sem(n) for n in ("pick", "hid", "xl", "hl", "ix", "rows", "upl", "dnl", "vch"))
        up_l_pool, dn_l_pool = m.sem("uplp"), m.sem("dnlp")
        gathered = [m.sem("ga0"), m.sem("ga1")]
        added = [m.sem("sc0"), m.sem("sc1")]
        gate_in, up_in, down_in = rt.gate_in, rt.up_in, rt.down_in
        go, act_go, sp_go, zeroed = m.sem("go"), m.sem("act_go"), m.sem("sp_go"), m.sem("zeroed")
        block = ctx.enter_context(nc.Block())
        w_g = io.w_gate[0].rearrange("e (k p) n -> e p k n", p=P)
        w_u = io.w_up[0].rearrange("e (k p) n -> e p k n", p=P)
        w_d = io.w_down[0].rearrange("e (k p) n -> e p k n", p=P)
        HEAD = 3
        DVE_K = 5

        def wait(eng, sem, value):
            if not isinstance(value, int) or value > 0:
                eng.wait_ge(sem, value)

        def dma_count(n, par):
            return n * 8 + (16 - 8 * par)

        def over_blocks(eng, body):
            last = eng.value_load(rt.tab[0:1, 5, 0:1], min_val=N_EXP, max_val=P - 8)
            for n in range(HEAD):
                body(n, n % 2)
            with eng.Fori(2, last, 2) as b:
                for u in (1, 2):
                    body(b + u, u % 2)
            return last

        def entry(eng, k, n, top):
            ap = rt.tab[0:1, k, n:n + 1] if isinstance(n, int) else rt.tab[0:1, k, bass.ds(n, 1)]
            return eng.value_load(ap, min_val=0, max_val=top)

        @block.sync
        def _(sp):
            def gate_up(e, par, until):
                wait(sp, up_l_dve, until)
                wait(sp, up_l_pool, until)
                sp.sem_inc(sp_go, 1)
                for half, src, sem in ((0, w_g, gate_in), (1, w_u, up_in)):
                    wait(sp, sem, e * 16)
                    sp.sem_inc(sp_go, 1)
                    src = src[e:e + 1] if isinstance(e, int) else src[bass.ds(e, 1)]
                    sp.dma_start(raw_up[:, par, :, D_EXP * half:D_EXP * (half + 1)],
                                 src.rearrange("a p k n -> (a p) k n")).then_inc(sem, 16)

            def down(e, par, until):
                wait(sp, dn_l_dve, until)
                wait(sp, dn_l_pool, until)
                sp.sem_inc(sp_go, 1)
                wait(sp, down_in, e * 16)
                sp.sem_inc(sp_go, 1)
                src = w_d[e:e + 1] if isinstance(e, int) else w_d[bass.ds(e, 1)]
                sp.dma_start(raw_dn[:, par, :, :], src.rearrange("a p k n -> (a p) k n")).then_inc(down_in, 16)

            def step(e, u):
                until = entry(sp, 4, e - 2 if isinstance(e, int) else b + (u - 2), P)
                if not isinstance(e, int) or e + 1 < N_EXP:
                    gate_up(e + 1, u % UP_SLOTS, until)
                down(e, u % 2, until)

            steps = N_EXP - 2
            whole = steps // 6 * 6
            with sp.Fori(2, whole - 3, 6) as b:
                for u in range(6):
                    step(b + u, u)
            for e in range(2 + whole, N_EXP):
                step(e, e - 2 - whole)

        @block.scalar
        def _(act):
            def up_high(n, par, slot, half):
                lo, hi = ((0, DVE_K), (DVE_K, KD))[half]
                act.activation(up_h[:, par, lo:hi, :],
                               raw_up[:, bass.ds(slot, 1), lo:hi, :].rearrange("p a k n -> p (a k) n"),
                               ACT.Copy).then_inc(up_h_done, 1)

            def up_high_first(n, par):
                e, slot = entry(act, 0, n, N_EXP - 1), entry(act, 3, n, UP_SLOTS - 1)
                wait(act, up_done, n - 1)
                wait(act, gate_in, e * 16 + 16)
                wait(act, up_in, e * 16 + 16)
                act.sem_inc(act_go, 1)
                up_high(n, par, slot, 0)
                return slot

            def down_high(n, par):
                e, slot = entry(act, 0, n, N_EXP - 1), entry(act, 2, n, 1)
                wait(act, down_done, n)
                wait(act, down_in, e * 16 + 16)
                act.sem_inc(act_go, 1)
                for k in range(2):
                    act.activation(dn_h[:, k, :],
                                   raw_dn[:, bass.ds(slot, 1), k, :].rearrange("p a n -> p (a n)"),
                                   ACT.Copy).then_inc(dn_h_done, 1)

            def silu(n, par):
                wait(act, up_done, n + 1)
                wait(act, hid_done, n - 1)
                act.activation(sg[:, par, :], p_gu[:, par, 0:D_EXP], ACT.Silu).then_inc(silu_done, 1)

            def y_out(n, par):
                wait(act, down_done, n + 1)
                wait(act, added[par], dma_count(n - 2, par) if not isinstance(n, int) else 16 * (n // 2))
                act.activation(y[:, par, :].rearrange("p (h n) -> p h n", h=2), p_dn[:, :, :], ACT.Copy).then_inc(y_act, 1)

            def x_high(n, par):
                wait(act, x_turned, n + 1)
                wait(act, up_done, n - 1)
                for h in range(2):
                    act.activation(x_h[:, par, 4 * h:4 * h + 4, :], p_tr[:, h, :].rearrange("p (k t) -> p k t", k=4),
                                   ACT.Copy).then_inc(xh_done, 1)

            def hid_high(n, par):
                wait(act, hid_turned, n + 1)
                wait(act, down_done, n - 1)
                act.activation(hid_h[:, par, :, :], p_ht[:, 0:2 * P].rearrange("p (k t) -> p k t", k=2),
                               ACT.Copy).then_inc(hidh_done, 1)

            def body(n, par):
                first = isinstance(n, int) and n == 0
                if first:
                    for k in range(2):
                        up_high(k, k, up_high_first(k, k), 1)
                        if k == 0:
                            x_high(0, 0)
                silu(n, par)
                x_high(n + 1, 1 - par)
                slot = up_high_first(n + 2, par)
                hid_high(n, par)
                if not first:
                    y_out(n - 1, 1 - par)
                down_high(n, par)
                up_high(n + 2, par, slot, 1)
            last = over_blocks(act, body)
            y_out(last + 0, 0)

        @block.gpsimd
        def _(pool):
            bound = pool.to_reg(N_TOK - 1)

            def gather(n, par):
                wait(pool, idx_done, n + 1)
                wait(pool, x_turned, n - 1)
                pool.sem_inc(go, 1)
                pool.indirect_dma_start(out=xg[:, par, :], out_offset=None, in_=io.tok,
                                        in_offset=bass.IndirectOffsetOnAxis(ap=idx_g[:, par:par + 1], axis=0),
                                        bounds_check=bound, oob_is_err=False).then_inc(gathered[par], 16)

            def scatter(n, par):
                wait(pool, y_act, n + 1)
                wait(pool, rows_done, n + 1)
                wait(pool, added[1 - par], dma_count(n - 1, 1 - par) if not isinstance(n, int) or n else 0)
                pool.sem_inc(go, 1)
                pool.indirect_dma_start(out=io.acc, in_=y[:, par, :], in_offset=None,
                                        out_offset=bass.IndirectOffsetOnAxis(ap=idx_s[:, par:par + 1], axis=0),
                                        bounds_check=bound, oob_is_err=False,
                                        compute_op=ALU.add).then_inc(added[par], 16)

            def up_low(n, par):
                slot = entry(pool, 3, n, UP_SLOTS - 1)
                wait(pool, up_h_done, n * 2 + 2)
                pool.sem_inc(go, 1)
                pool.tensor_tensor(up_l[:, par, DVE_K:, :],
                                   raw_up[:, bass.ds(slot, 1), DVE_K:, :].rearrange("p a k n -> p (a k) n"),
                                   up_h[:, par, DVE_K:, :].bitcast(F32), ALU.subtract).then_inc(up_l_pool, 1)

            def down_low(n, par):
                slot = entry(pool, 2, n, 1)
                wait(pool, dn_h_done, n * 2 + 2)
                pool.sem_inc(go, 1)
                pool.tensor_tensor(dn_l[:, 1, :],
                                   raw_dn[:, bass.ds(slot, 1), 1, :].rearrange("p a n -> p (a n)"),
                                   dn_h[:, 1, :].bitcast(F32), ALU.subtract).then_inc(dn_l_pool, 1)

            def body(n, par):
                first = isinstance(n, int) and n == 0
                if first:
                    gather(0, 0)
                    gather(1, 1)
                    up_low(0, 0)
                    gather(2, 0)
                    up_low(1, 1)
                if not first:
                    scatter(n - 1, 1 - par)
                gather(n + 3, 1 - par)
                down_low(n, par)
                up_low(n + 2, par)
            pool.memset(xg[:, :, :], 0.0).then_inc(zeroed, 1)
            pool.wait_ge(zeroed, 1)
            last = over_blocks(pool, body)
            scatter(last + 0, 0)
            wait(pool, added[0], dma_count(last, 0))
            wait(pool, gathered[0], dma_count(last + 2, 0))
            wait(pool, gathered[1], dma_count(last + 3, 1))

        @block.tensor
        def _(pe):
            def split_product(out, a, b, free):
                (ah, al), (bh, bl) = a, b
                terms = [(x[:, k, :], w[:, k, free]) for k in range(ah.shape[1])
                         for x, w in ((ah, bh), (ah, bl), (al, bh))]
                for i, (x, w) in enumerate(terms):
                    mm = pe.matmul(out, x, w, start=(i == 0), stop=(i == len(terms) - 1))
                return mm

            def up(n, par):
                wait(pe, up_l_dve, n + 1)
                wait(pe, up_l_pool, n + 1)
                wait(pe, xl_done, n + 1)
                wait(pe, hid_done, n - 1)
                split_product(p_gu[:, par, :], (x_h[:, par], x_l[:, par]), (up_h[:, par], up_l[:, par]),
                              slice(0, 2 * D_EXP)).then_inc(up_done, 1)

            def down(n, par):
                wait(pe, dn_l_dve, n + 1)
                wait(pe, dn_l_pool, n + 1)
                wait(pe, hidl_done, n + 1)
                wait(pe, y_act, n)
                for h in range(2):
                    mm = split_product(p_dn[:, h, :], (hid_h[:, par], hid_l[:, par]), (dn_h, dn_l),
                                       slice(512 * h, 512 * (h + 1)))
                mm.then_inc(down_done, 1)

            def turn_x(n, par):
                wait(pe, gathered[par], dma_count(n, par))
                wait(pe, xl_done, n)
                for k in range(KD):
                    tr = pe.transpose(p_tr[:, k // 4, (k % 4) * P:(k % 4 + 1) * P], xg[:, par, k * P:(k + 1) * P],
                                      keep.ident[:, :])
                tr.then_inc(x_turned, 1)

            def look_up(n, par):
                wait(pe, pick_done, n + 1)
                wait(pe, idx_done, n)
                for k in range(N_TILES):
                    mm = pe.matmul(p_im[:, 0:6], pick[:, par, k, :], rt.vals[:, par, k, :], start=(k == 0),
                                   stop=(k == N_TILES - 1))
                mm.then_inc(info_done, 1)

            def turn_hid(n, par):
                wait(pe, hid_done, n + 1)
                wait(pe, hidl_done, n)
                for k in range(2):
                    tr = pe.transpose(p_ht[:, k * P:(k + 1) * P], hid[:, par, k * P:(k + 1) * P], keep.ident[:, :])
                tr.then_inc(hid_turned, 1)

            def body(n, par):
                first = isinstance(n, int) and n == 0
                if first:
                    look_up(0, 0)
                    look_up(1, 1)
                    turn_x(0, 0)
                    look_up(2, 0)
                up(n, par)
                turn_x(n + 1, 1 - par)
                look_up(n + 3, 1 - par)
                if not first:
                    down(n - 1, 1 - par)
                turn_hid(n, par)
            last = over_blocks(pe, body)
            down(last + 0, 0)

        @block.vector
        def _(v):
            tt, ts, stt = v.tensor_tensor, v.tensor_scalar, v.scalar_tensor_tensor

            def choose(n, par):
                e = entry(v, 0, n, N_EXP - 1)
                j = entry(v, 1, n, P * (SLOT_SETS - 1))
                wait(v, info_done, n - 1)
                tt(pick[:, par, :, :], bc(rt.slot[:, bass.ds(j, P)], 1, N_TILES),
                   rt.posm[:, :, bass.ds(e, 1)].to_broadcast([P, N_TILES, P]), ALU.is_equal)
                v.tensor_copy(rt.vals[:, par, :, 3:6].unsqueeze(2), rt.parts[:, :, bass.ds(e, 1), :]).then_inc(pick_done, 1)

            def index(n, par):
                count = [0]

                def link(ins):
                    count[0] += 1
                    ins.then_inc(s_v, 1)
                    v.wait_ge(s_v, n * LINKS + count[0])
                wait(v, info_done, n + 1)
                wait(v, hid_done, n - 3)
                wait(v, rows_done, n - 3)
                wait(v, gathered[par], dma_count(n - 2, par) if not isinstance(n, int) else 16 * (n // 2))
                if not isinstance(n, int) or n >= 2:
                    v.tensor_copy(cur[:, par, :], new[:, par, :])
                link(v.tensor_copy(info[:, 0:6], p_im[:, 0:6]))
                ts(tmp[:, 0:1], info[:, 2:3], -1.0, 1.0, ALU.mult, ALU.add)
                stt(out=tmp[:, 1:2], in0=info[:, 1:2], scalar=float(P), in1=info[:, 0:1], op0=ALU.mult, op1=ALU.add)
                link(tt(new[:, par, 1:2], info[:, 3:4], info[:, 4:5], ALU.add))
                tt(new[:, par, 1:2], new[:, par, 1:2], info[:, 5:6], ALU.add)
                link(stt(out=new[:, par, 0:1], in0=tmp[:, 0:1], scalar=rt.dummy[:, 0:1], in1=tmp[:, 1:2],
                         op0=ALU.mult, op1=ALU.add))
                v.tensor_copy(idx_g[:, par:par + 1], new[:, par, 0:1]).then_inc(idx_done, 1)
                wait(v, idx_done, n + 1)

            LINKS = 3

            def hidden(n, par):
                wait(v, silu_done, n + 1)
                wait(v, hid_turned, n - 1)
                stt(out=hid[:, par, :], in0=sg[:, par, :], scalar=cur[:, par, 1:2], in1=p_gu[:, par, D_EXP:],
                    op0=ALU.mult, op1=ALU.mult).then_inc(hid_done, 1)

            def up_low(n, par):
                slot = entry(v, 3, n, UP_SLOTS - 1)
                wait(v, up_h_done, n * 2 + 1)
                tt(up_l[:, par, 0:DVE_K, :], raw_up[:, bass.ds(slot, 1), 0:DVE_K, :].rearrange("p a k n -> p (a k) n"),
                   up_h[:, par, 0:DVE_K, :].bitcast(F32), ALU.subtract).then_inc(up_l_dve, 1)

            def down_low(n, par):
                slot = entry(v, 2, n, 1)
                wait(v, dn_h_done, n * 2 + 1)
                tt(dn_l[:, 0, :], raw_dn[:, bass.ds(slot, 1), 0, :].rearrange("p a n -> p (a n)"),
                   dn_h[:, 0, :].bitcast(F32), ALU.subtract).then_inc(dn_l_dve, 1)

            def x_low(n, par):
                for h in range(2):
                    wait(v, xh_done, n * 2 + (h + 1))
                    low = tt(x_l[:, par, 4 * h:4 * h + 4, :], p_tr[:, h, :].rearrange("p (k t) -> p k t", k=4),
                             x_h[:, par, 4 * h:4 * h + 4, :].bitcast(F32), ALU.subtract)
                low.then_inc(xl_done, 1)

            def scatter_rows(n, par):
                wait(v, added[par], dma_count(n - 2, par) if not isinstance(n, int) else 16 * (n // 2))
                v.tensor_copy(idx_s[:, par:par + 1], cur[:, par, 0:1]).then_inc(rows_done, 1)

            def hid_low(n, par):
                wait(v, hidh_done, n + 1)
                tt(hid_l[:, par, :, :], p_ht[:, 0:2 * P].rearrange("p (k t) -> p k t", k=2),
                   hid_h[:, par, :, :].bitcast(F32), ALU.subtract).then_inc(hidl_done, 1)

            def body(n, par):
                first = isinstance(n, int) and n == 0
                if first:
                    for k in range(2):
                        choose(k, k)
                    for k in range(2):
                        index(k, k)
                    up_low(0, 0)
                    choose(2, 0)
                    x_low(0, 0)
                    index(2, 0)
                    choose(3, 1)
                    up_low(1, 1)
                hidden(n, par)
                x_low(n + 1, 1 - par)
                if not first:
                    scatter_rows(n - 1, 1 - par)
                index(n + 3, 1 - par)
                up_low(n + 2, par)
                hid_low(n, par)
                down_low(n, par)
                choose(n + 4, par)
            last = over_blocks(v, body)
            scatter_rows(last + 0, 0)


def final_stage(nc, io, keep):
    with ExitStack() as ctx:
        m = Pools(nc, ctx, "final")
        x = m.sb("x", [P, N_TILES, D])
        lng, lnb = m.sb("lng", [P, D]), m.sb("lnb", [P, D])
        stats = m.sb("stats", [P, N_TILES, 2, 6])
        mv = m.sb("mv", [P, N_TILES, 2])
        rs = m.sb("rs", [P, N_TILES, 2])
        eps = m.sb("eps", [P, 1])
        s_x = [m.sem(f"x{i}") for i in range(N_TILES)]
        s_ln, s_eps, s_stat, s_std, s_rs, s_nm, s_gain, s_y, s_out, s_v = (
            m.sem(n) for n in ("ln", "eps", "stat", "std", "rs", "nm", "gain", "y", "out", "vch"))
        block = ctx.enter_context(nc.Block())

        @block.sync
        def _(sp):
            for i in range(N_TILES):
                sp.dma_start(x[:, i, :], io.acc[i * P:(i + 1) * P, :]).then_inc(s_x[i], 16)
            for i in range(N_TILES):
                sp.wait_ge(s_y, i + 1)
                if i < N_TILES - 1:
                    sp.dma_start(io.out_y_p[0, i * P:(i + 1) * P, :], x[:, i, :]).then_inc(s_out, 16)
                else:
                    sp.dma_start(io.out_y_s[0], x[0:LAST_ROWS, i, :]).then_inc(s_out, 16)
            sp.wait_ge(s_out, 16 * N_TILES)

        @block.gpsimd
        def _(pool):
            pool.memset(eps[:, :], LN_EPS).then_inc(s_eps, 1)
            pool.wait_ge(s_ln, 32)
            for i in range(N_TILES):
                pool.wait_ge(s_gain, i + 1)
                pool.tensor_tensor(x[:, i, :], x[:, i, :], lnb[:, :], ALU.add).then_inc(s_y, 1)

        @block.scalar
        def _(act):
            act.dma_start(lng[:, :], io.ln2_g[0].partition_broadcast(P)).then_inc(s_ln, 16)
            act.dma_start(lnb[:, :], io.ln2_b[0].partition_broadcast(P)).then_inc(s_ln, 16)
            act.wait_ge(s_eps, 1)
            for i in range(N_TILES):
                act.wait_ge(s_stat, i + 1)
                act.activation(rs[:, i, 0:1], mv[:, i, 1:2], ACT.Sqrt, bias=eps[:, 0:1]).then_inc(s_std, 1)
                act.wait_ge(s_rs, i + 1)
                act.activation(x[:, i, :], x[:, i, :], ACT.Identity, bias=rs[:, i, 1:2],
                               scale=rs[:, i, 0:1]).then_inc(s_nm, 1)

        @block.vector
        def _(v):
            link = chain(v, s_v)

            def scale(i):
                v.wait_ge(s_std, i + 1)
                link(v.reciprocal(rs[:, i, 0:1], rs[:, i, 0:1]))
                v.scalar_tensor_tensor(out=rs[:, i, 1:2], in0=mv[:, i, 0:1], scalar=-1.0, in1=rs[:, i, 0:1],
                                       op0=ALU.mult, op1=ALU.mult).then_inc(s_rs, 1)

            def gain(i):
                v.wait_ge(s_nm, i + 1)
                if i == 0:
                    v.wait_ge(s_ln, 32)
                v.tensor_tensor(x[:, i, :], x[:, i, :], lng[:, :], ALU.mult).then_inc(s_gain, 1)

            for i in range(N_TILES):
                v.wait_ge(s_x[i], 16)
                v.bn_stats(stats[:, i, 0, :], x[:, i, 0:512])
                link(v.bn_stats(stats[:, i, 1, :], x[:, i, 512:]))
                v.bn_aggr(mv[:, i, :], stats[:, i, :, :]).then_inc(s_stat, 1)
                if i:
                    gain(i - 1)
                scale(i)
            gain(N_TILES - 1)


def build(nc, args):
    io = Names()
    io.x_prompt, io.x_sample, io.state_ssm_re = args["x_prompt"], args["x_sample"], args["state_ssm_re"]
    io.state_ssm_im, io.cache_conv, io.ln_in_g = args["state_ssm_im"], args["cache_conv"], args["ln_in_g"]
    io.ln_in_b, io.w_in, io.lam_re = args["ln_in_b"], args["w_in"], args["lam_re"]
    io.lam_im, io.log_dt, io.ssm_b_re = args["lam_im"], args["log_dt"], args["ssm_b_re"]
    io.ssm_b_im, io.ssm_c_re, io.ssm_c_im = args["ssm_b_im"], args["ssm_c_re"], args["ssm_c_im"]
    io.ssm_d, io.w_glu, io.b_glu = args["ssm_d"], args["w_glu"], args["b_glu"]
    io.conv_w, io.beta_ssm, io.beta_conv = args["conv_w"], args["beta_ssm"], args["beta_conv"]
    io.w_out, io.ln1_g, io.ln1_b = args["w_out"], args["ln1_g"], args["ln1_b"]
    io.w_router, io.router_bias, io.w_gate = args["w_router"], args["router_bias"], args["w_gate"]
    io.w_up, io.w_down, io.ws_gate = args["w_up"], args["w_down"], args["ws_gate"]
    io.ws_up, io.ws_down, io.ln2_g = args["ws_up"], args["ws_down"], args["ln2_g"]
    io.ln2_b, io.out_y_p, io.out_y_s = args["ln2_b"], args["out_y_p"], args["out_y_s"]
    io.out_ssm_re_p, io.out_ssm_im_p, io.out_conv_p = args["out_ssm_re_p"], args["out_ssm_im_p"], args["out_conv_p"]
    io.out_ssm_re_s, io.out_ssm_im_s, io.out_conv_s = args["out_ssm_re_s"], args["out_ssm_im_s"], args["out_conv_s"]

    def dram(name, shape):
        return nc.dram_tensor(name, shape, F32, kind="Internal").ap()

    io.resid = dram("resid", (ROWS, D))
    io.ud = dram("ud", (D_HALF, N_TOK))
    io.yd = dram("yd", (D_HALF, N_TOK))
    io.tok = dram("tok", (ROWS, D))
    io.acc = dram("acc", (ROWS, D))
    with ExitStack() as ctx:
        m = Pools(nc, ctx, "keep")
        keep = Names()
        keep.ident = m.sb("ident", [P, P])
        keep.scores = m.sb("scores", [P, N_TILES, N_EXP])
        with ExitStack() as half:
            h = Pools(nc, half, "keep")
            keep.gT = h.sb("gT", [P, KH, ROWS])
            keep.ycT = h.sb("ycT", [P, KH, ROWS])
            with ExitStack() as first:
                f = Pools(nc, first, "co")
                keep.hT = f.sb("hT", [P, KD, N_TOK])
                co = Names()
                co.sign = f.sb("sign", [P, 1])
                co.pr = f.sb("pr", [P, GROUPS, T + 1])
                co.pi = f.sb("pi", [P, GROUPS, T + 1])
                co.prs = f.sb("prs", [P, GROUPS, T + 1])
                co.npi = f.sb("npi", [P, GROUPS, T + 1])
                co.nsi = f.sb("nsi", [P, GROUPS, T + 1])
                co.bb = f.sb("bb", [P, GROUPS, GC])
                co.bbsw = f.sb("bbsw", [P, GROUPS, GC])
                co.cs = f.sb("cs", [P, KH * P])
                co.csw = f.sb("csw", [P, KH * P])
                co.h0 = f.sb("h0", [P, GROUPS])
                co.ah0 = f.sb("ah0", [P, GROUPS])
                co.er = f.sb("er", [P, GROUPS, 7])
                co.eis = f.sb("eis", [P, GROUPS, 7])
                co.win = f.sb("win", [P, IN_RING, KD, P])
                co.s_w = [f.sem(f"w{i}") for i in range(IN_RING)]
                co.turn = f.sb("turn", [P, 3, GROUPS])
                co.decay = f.sb("decay", [P, GROUPS])
                trunk_stage(nc, io, keep, co)
                mixing_stage(nc, io, keep, co)
            output_stage(nc, io, keep)
        with ExitStack() as moe:
            r = Pools(nc, moe, "rt")
            rt = Names()
            rt.slot = r.sb("slot", [P, P * SLOT_SETS])
            rt.dummy = r.sb("dummy", [P, 1])
            rt.vals = r.sb("vals", [P, 2, N_TILES, 6], BF16)
            rt.parts = r.sb("parts", [P, N_TILES, N_EXP, 3], BF16)
            rt.posm = r.sb("posm", [P, N_TILES, N_EXP])
            rt.tab = r.sb("tab", [1, 6, P + 8], I32)
            rt.raw_up = r.sb("raw_up", [P, UP_SLOTS, KD, 2 * D_EXP])
            rt.raw_dn = r.sb("raw_dn", [P, 2, 2, D])
            rt.gate_in, rt.up_in, rt.down_in = r.sem("gate_in"), r.sem("up_in"), r.sem("down_in")
            routing_stage(nc, io, keep, rt)
            expert_stage(nc, io, keep, rt)
        final_stage(nc, io, keep)
    return


_INS = ['x_prompt', 'x_sample', 'state_ssm_re', 'state_ssm_im', 'cache_conv', 'ln_in_g', 'ln_in_b', 'w_in', 'lam_re',
        'lam_im', 'log_dt', 'ssm_b_re', 'ssm_b_im', 'ssm_c_re', 'ssm_c_im', 'ssm_d', 'w_glu', 'b_glu', 'conv_w',
        'beta_ssm', 'beta_conv', 'w_out', 'ln1_g', 'ln1_b', 'w_router', 'router_bias', 'w_gate', 'w_up', 'w_down',
        'ws_gate', 'ws_up', 'ws_down', 'ln2_g', 'ln2_b']
_OUTS = [("out_y_p", (1, 1024, 1024)), ("out_y_s", (1, 64, 1024)),
         ("out_ssm_re_p", (1, 1, 32, 64)), ("out_ssm_im_p", (1, 1, 32, 64)), ("out_conv_p", (1, 1, 2, 512)),
         ("out_ssm_re_s", (1, 1, 32, 64)), ("out_ssm_im_s", (1, 1, 32, 64)), ("out_conv_s", (1, 1, 2, 512))]


def kernel(**inputs):
    import numpy as _np
    import concourse.bacc as _bacc
    from concourse import mybir as _mybir
    from concourse.bass_utils import run_bass_kernel_spmd as _run

    nc = _bacc.Bacc("TRN2", target_bir_lowering=False, num_devices=1)
    arrays, args = {}, {}
    for name in _INS:
        a = _np.ascontiguousarray(inputs[name])
        arrays[f"in_{name}_dram"] = a
        args[name] = nc.dram_tensor(f"in_{name}_dram", a.shape, _mybir.dt.from_np(a.dtype), kind="ExternalInput").ap()
    for name, shape in _OUTS:
        args[name] = nc.dram_tensor(f"{name}_dram", shape, _mybir.dt.from_np(_np.dtype("float32")),
                                    kind="ExternalOutput").ap()
    build(nc, args)
    r = _run(nc, [arrays], core_ids=[0])
    return tuple(r.results[0][f"{name}_dram"] for name, _ in _OUTS)
```
